# Optimizing a Trainium2 kernel written in Bass

```python
import jax, jax.numpy as jnp
from jax import lax
import numpy as np

D_MODEL = 1024
BATCH = 1
SEQ = 512
DEPTH = 1

CTX_LEN = 256
GRID_W = 64
N_DIRS = 2
RMS_EPS = 1e-6
SSM_D_INNER = 2 * D_MODEL
SSM_HEAD_DIM = 64
SSM_HEADS = SSM_D_INNER // SSM_HEAD_DIM
SSM_GROUPS = 4
SSM_HEADS_PER_GROUP = SSM_HEADS // SSM_GROUPS
SSM_STATE = 128
SSM_CONV_K = 3
SSM_CONV_DIM = SSM_D_INNER + 2 * SSM_GROUPS * SSM_STATE
SSM_CHUNK = 128
HG_HEADS = 8
HG_KEY_DIM = 128
HG_VAL_DIM = D_MODEL // HG_HEADS
HG_KEY = HG_HEADS * HG_KEY_DIM
HG_VAL = HG_HEADS * HG_VAL_DIM
HG_CHUNK = 64
MOE_GROUPS = 4
MOE_EXPERTS_PER_GROUP = 8
MOE_EXPERTS = MOE_GROUPS * MOE_EXPERTS_PER_GROUP
MOE_TOP_K = 2
MOE_D_FF = 512
MOE_BLOCK = 128
COL_SIZES = (SSM_D_INNER, SSM_CONV_DIM, N_DIRS * SSM_HEADS, HG_KEY, N_DIRS * HG_KEY, HG_VAL, HG_VAL, D_MODEL, D_MODEL)
N_IN = sum(COL_SIZES)

kernel_name = 'hybrid_ssd_hgrn2_hmoe_block'

def rms_norm(x, g):
    xf = x.astype(jnp.float32)
    y = xf * lax.rsqrt(jnp.mean(xf * xf, axis=-1, keepdims=True) + RMS_EPS)
    return (y * g.astype(jnp.float32)).astype(x.dtype)

def dwconv_centred(u, w, b):
    out = lax.conv_general_dilated(u, w[:, None, :].astype(u.dtype), window_strides=(1,), padding='SAME',
                                   dimension_numbers=('NWC', 'WIO', 'NWC'), feature_group_count=u.shape[-1])
    return out + b.astype(u.dtype)

def make_dirs(ctx_f, lat_f, ctx_b, lat_b):
    fwd = jnp.concatenate([ctx_f, lat_f], axis=1)
    bwd = jnp.concatenate([jnp.flip(ctx_b, 1), jnp.flip(lat_b, 1)], axis=1)
    return jnp.concatenate([fwd, bwd], axis=0)

def merge_dirs(y, n_ctx):
    nb = y.shape[0] // 2
    fwd, bwd = y[:nb], y[nb:]
    bwd = jnp.concatenate([jnp.flip(bwd[:, :n_ctx], 1), jnp.flip(bwd[:, n_ctx:], 1)], axis=1)
    return fwd + bwd

def raster_to_cols(t, rows):
    b, s = t.shape[:2]
    return t.reshape(b, rows, GRID_W, *t.shape[2:]).swapaxes(1, 2).reshape(t.shape)

def cols_to_raster(t, rows):
    b, s = t.shape[:2]
    return t.reshape(b, GRID_W, rows, *t.shape[2:]).swapaxes(1, 2).reshape(t.shape)

def segsum_exp(a):
    t = a.shape[-1]
    cs = jnp.cumsum(a, axis=-1)
    mask = jnp.tril(jnp.ones((t, t), dtype=bool))
    return jnp.exp(jnp.where(mask, cs[..., :, None] - cs[..., None, :], -jnp.inf))

def ssd_scan(x, dt, a, bm, cm):
    f32 = jnp.float32
    z, l, g, j, p = x.shape
    n = bm.shape[-1]
    q = SSM_CHUNK
    nc = l // q
    dt = dt.astype(f32)
    xdt = (x.astype(f32) * dt[..., None]).reshape(z, nc, q, g, j, p)
    adt = (dt * a[:, None]).reshape(z, nc, q, g, j).transpose(0, 3, 4, 1, 2)
    bc = bm.astype(f32).reshape(z, nc, q, g, n)
    cc = cm.astype(f32).reshape(z, nc, q, g, n)
    a_cs = jnp.cumsum(adt, axis=-1)
    cb = jnp.einsum('zclgn,zcsgn->zgcls', cc, bc)
    w_diag = cb[:, :, None] * segsum_exp(adt)
    y_diag = jnp.einsum('zgjcls,zcsgjp->zclgjp', w_diag, xdt)
    decay_states = jnp.exp(a_cs[..., -1:] - a_cs)
    states = jnp.einsum('zclgn,zgjcl,zclgjp->zcgjpn', bc, decay_states, xdt)
    states = jnp.concatenate([jnp.zeros_like(states[:, :1]), states], axis=1)
    chunk_decay = segsum_exp(jnp.pad(a_cs[..., -1], ((0, 0), (0, 0), (0, 0), (1, 0))))
    states_in = jnp.einsum('zgjab,zbgjpn->zagjpn', chunk_decay, states)[:, :-1]
    y_off = jnp.einsum('zclgn,zcgjpn,zgjcl->zclgjp', cc, states_in, jnp.exp(a_cs))
    return (y_diag + y_off).reshape(z, l, g, j, p)

def gla_scan(q, k, v, log_f):
    f32 = jnp.float32
    z, l, h, dk = q.shape
    dv = v.shape[-1]
    c = HG_CHUNK
    nc = l // c

    def chunks(t):
        return t.astype(f32).reshape(z, nc, c, h, t.shape[-1]).transpose(1, 0, 3, 2, 4)

    mask = jnp.tril(jnp.ones((c, c), dtype=bool))[:, :, None]

    def step(state, inp):
        qc, kc, vc, lc = inp
        b = jnp.cumsum(lc, axis=2)
        inter = jnp.einsum('zhtk,zhkv->zhtv', qc * jnp.exp(b), state)
        decay = jnp.exp(jnp.where(mask, b[:, :, :, None, :] - b[:, :, None, :, :], -jnp.inf))
        att = jnp.einsum('zhtk,zhsk,zhtsk->zhts', qc, kc, decay)
        out = inter + jnp.einsum('zhts,zhsv->zhtv', att, vc)
        b_end = b[:, :, -1]
        state = jnp.exp(b_end)[..., None] * state + jnp.einsum(
            'zhsk,zhsv->zhkv', kc * jnp.exp(b_end[:, :, None] - b), vc)
        return state, out

    s0 = jnp.zeros((z, h, dk, dv), f32)
    _, out = lax.scan(step, s0, (chunks(q), chunks(k), chunks(v), chunks(log_f)))
    return out.transpose(1, 0, 3, 2, 4).reshape(z, l, h, dv)

def token_mixer(hl, hc, w_in, conv_w, conv_b, dt_bias, a_log, d_skip, g_ssm_norm, lb, g_hg_norm,
                w_branch_ssm, w_branch_hg, w_out, rows, with_ctx):
    f32 = jnp.float32
    nb, n_lat, _ = hl.shape
    n_ctx = hc.shape[1]
    splits = np.cumsum(COL_SIZES)[:-1].tolist()
    z_l, xbc_l, dtr_l, qr_l, fr_l, ir_l, og_l, gm_l, gh_l = jnp.split(hl @ w_in, splits, axis=-1)
    z_c, xbc_c, dtr_c, qr_c, fr_c, ir_c, og_c, gm_c, gh_c = jnp.split(hc @ w_in, splits, axis=-1)

    xbc_l = jax.nn.silu(dwconv_centred(xbc_l, conv_w, conv_b))
    xbc_c = jax.nn.silu(dwconv_centred(xbc_c, conv_w, conv_b))

    def ssm_split(u):
        b_, t_ = u.shape[:2]
        xs, bm, cm = jnp.split(u, [SSM_D_INNER, SSM_D_INNER + SSM_GROUPS * SSM_STATE], axis=-1)
        return (xs.reshape(b_, t_, SSM_GROUPS, SSM_HEADS_PER_GROUP, SSM_HEAD_DIM),
                bm.reshape(b_, t_, SSM_GROUPS, SSM_STATE), cm.reshape(b_, t_, SSM_GROUPS, SSM_STATE))

    def ssm_dt(u):
        b_, t_ = u.shape[:2]
        d = jax.nn.softplus(u.reshape(b_, t_, N_DIRS, SSM_HEADS).astype(f32) + dt_bias.astype(f32))
        return d.reshape(b_, t_, N_DIRS, SSM_GROUPS, SSM_HEADS_PER_GROUP)

    xs_l, bm_l, cm_l = ssm_split(xbc_l)
    xs_c, bm_c, cm_c = ssm_split(xbc_c)
    dt_l, dt_c = ssm_dt(dtr_l), ssm_dt(dtr_c)
    xs = make_dirs(xs_c, xs_l, xs_c, xs_l)
    bm = make_dirs(bm_c, bm_l, bm_c, bm_l)
    cm = make_dirs(cm_c, cm_l, cm_c, cm_l)
    dt = make_dirs(dt_c[:, :, 0], dt_l[:, :, 0], dt_c[:, :, 1], dt_l[:, :, 1])
    a = jnp.repeat(-jnp.exp(a_log.astype(f32)), nb, axis=0).reshape(N_DIRS * nb, SSM_GROUPS, SSM_HEADS_PER_GROUP)
    dsk = jnp.repeat(d_skip.astype(f32), nb, axis=0).reshape(N_DIRS * nb, 1, SSM_GROUPS, SSM_HEADS_PER_GROUP, 1)
    y = ssd_scan(xs, dt, a, bm, cm) + xs.astype(f32) * dsk
    y = merge_dirs(y, n_ctx).reshape(nb, n_ctx + n_lat, SSM_D_INNER).astype(hl.dtype)
    ys_c, ys_l = y[:, :n_ctx], y[:, n_ctx:]

    def hg_split(q, f, i):
        b_, t_ = q.shape[:2]
        qh = jax.nn.silu(q).reshape(b_, t_, HG_HEADS, HG_KEY_DIM)
        fz = f.reshape(b_, t_, N_DIRS, HG_KEY).astype(f32)
        log_f = jnp.log(lb + (1.0 - lb) * jax.nn.sigmoid(fz))
        k = (1.0 - lb) * jax.nn.sigmoid(-fz)
        shp = (b_, t_, N_DIRS, HG_HEADS, HG_KEY_DIM)
        return qh, k.reshape(shp), log_f.reshape(shp), i.reshape(b_, t_, HG_HEADS, HG_VAL_DIM)

    q_l, k_l, lf_l, v_l = hg_split(raster_to_cols(qr_l, rows), raster_to_cols(fr_l, rows), raster_to_cols(ir_l, rows))
    q_c, k_c, lf_c, v_c = hg_split(qr_c, fr_c, ir_c)
    o = gla_scan(make_dirs(q_c, q_l, q_c, q_l),
                 make_dirs(k_c[:, :, 0], k_l[:, :, 0], k_c[:, :, 1], k_l[:, :, 1]),
                 make_dirs(v_c, v_l, v_c, v_l),
                 make_dirs(lf_c[:, :, 0], lf_l[:, :, 0], lf_c[:, :, 1], lf_l[:, :, 1]))
    o = merge_dirs(o, n_ctx).astype(hl.dtype)
    o_c = o[:, :n_ctx]
    o_l = cols_to_raster(o[:, n_ctx:], rows)

    def merge(ys, z, oh, og, gm, gh):
        b_, t_ = ys.shape[:2]
        yz = (ys * jax.nn.silu(z)).reshape(b_, t_, SSM_GROUPS, SSM_D_INNER // SSM_GROUPS)
        ys = rms_norm(yz, g_ssm_norm.reshape(SSM_GROUPS, -1)).reshape(b_, t_, SSM_D_INNER)
        oh = rms_norm(oh, g_hg_norm) * jax.nn.silu(og.reshape(b_, t_, HG_HEADS, HG_VAL_DIM))
        mixed = (jax.nn.sigmoid(gm) * (ys @ w_branch_ssm)
                 + jax.nn.sigmoid(gh) * (oh.reshape(b_, t_, HG_VAL) @ w_branch_hg))
        return mixed @ w_out

    out_l = merge(ys_l, z_l, o_l, og_l, gm_l, gh_l)
    out_c = merge(ys_c, z_c, o_c, og_c, gm_c, gh_c) if with_ctx else None
    return out_l, out_c

def hier_moe(h, w_gr, b_gr, w_er, b_er, w_gate, w_up, w_down):
    f32 = jnp.float32
    n, d = h.shape
    g_prob = jax.nn.softmax((h @ w_gr).astype(f32) + b_gr.astype(f32), axis=-1)
    p_grp, grp = lax.top_k(g_prob, 1)
    e_logits = jnp.einsum('nd,gde->nge', h, w_er).astype(f32) + b_er.astype(f32)
    e_logits = e_logits[jnp.arange(n), grp[:, 0]]
    top_v, top_i = lax.top_k(e_logits, MOE_TOP_K)
    weight = p_grp * jax.nn.softmax(top_v, axis=-1)
    expert = grp * MOE_EXPERTS_PER_GROUP + top_i
    flat_e = expert.reshape(-1)
    flat_w = weight.reshape(-1).astype(h.dtype)
    flat_tok = jnp.repeat(jnp.arange(n, dtype=jnp.int32), MOE_TOP_K)
    m = n * MOE_TOP_K
    r = MOE_BLOCK
    counts = jnp.bincount(flat_e, length=MOE_EXPERTS)
    padded = (counts + r - 1) // r * r
    pad_end = jnp.cumsum(padded)
    pad_start = pad_end - padded
    cnt_start = jnp.cumsum(counts) - counts
    order = jnp.argsort(flat_e)
    e_sorted = flat_e[order]
    dest = pad_start[e_sorted] + jnp.arange(m) - cnt_start[e_sorted]
    cap = -(-(m + MOE_EXPERTS * r) // r) * r
    n_blk = cap // r
    tok_buf = jnp.zeros((cap,), jnp.int32).at[dest].set(flat_tok[order])
    w_buf = jnp.zeros((cap,), h.dtype).at[dest].set(flat_w[order])
    blk_e = jnp.minimum(jnp.searchsorted(pad_end, jnp.arange(n_blk) * r, side='right'), MOE_EXPERTS - 1)
    xb = h[tok_buf].reshape(n_blk, r, d)

    def expert_block(args):
        xr, e = args
        return (jax.nn.silu(xr @ w_gate[e]) * (xr @ w_up[e])) @ w_down[e]

    yb = lax.map(expert_block, (xb, blk_e)).reshape(cap, d)
    return jnp.zeros_like(h).at[tok_buf].add(yb * w_buf[:, None])

def setup_inputs(seed: int = 0) -> dict:
    key = jax.random.key(seed)
    ks = iter(jax.random.split(key, 32))
    f32 = jnp.float32
    D = D_MODEL

    def nrm(shape, scale):
        return jax.random.normal(next(ks), shape, f32) * scale

    u_dt = jax.random.uniform(next(ks), (DEPTH, N_DIRS, SSM_HEADS), f32)
    dt0 = jnp.exp(u_dt * (np.log(0.1) - np.log(0.001)) + np.log(0.001)).astype(f32)
    return {
        'x': nrm((BATCH, SEQ, D), 1.0),
        'c': nrm((BATCH, D), 1.0),
        'ctx': nrm((BATCH, CTX_LEN, D), 1.0),
        'c_ctx': nrm((D,), 1.0),
        'w_ada': nrm((DEPTH, D, 6 * D), 0.5 * D ** -0.5),
        'b_ada': nrm((DEPTH, 6 * D), 0.01),
        'g_pre_mix': 1.0 + nrm((DEPTH, D), 0.02),
        'g_post_mix': 1.0 + nrm((DEPTH, D), 0.02),
        'g_pre_ffn': 1.0 + nrm((DEPTH, D), 0.02),
        'g_post_ffn': 1.0 + nrm((DEPTH, D), 0.02),
        'w_in': nrm((DEPTH, D, N_IN), D ** -0.5),
        'conv_w': nrm((DEPTH, SSM_CONV_K, SSM_CONV_DIM), SSM_CONV_K ** -0.5),
        'conv_b': nrm((DEPTH, SSM_CONV_DIM), 0.01),
        'dt_bias': dt0 + jnp.log(-jnp.expm1(-dt0)),
        'a_log': jnp.log(jax.random.uniform(next(ks), (DEPTH, N_DIRS, SSM_HEADS), f32, 1.0, 16.0)),
        'd_skip': 1.0 + nrm((DEPTH, N_DIRS, SSM_HEADS), 0.1),
        'g_ssm_norm': 1.0 + nrm((DEPTH, SSM_D_INNER), 0.02),
        'hg_lb': nrm((DEPTH + 1, N_DIRS, HG_KEY), 0.1),
        'g_hg_norm': 1.0 + nrm((DEPTH, HG_VAL_DIM), 0.02),
        'w_branch_ssm': nrm((DEPTH, SSM_D_INNER, D), SSM_D_INNER ** -0.5),
        'w_branch_hg': nrm((DEPTH, HG_VAL, D), HG_VAL ** -0.5),
        'w_out': nrm((DEPTH, D, D), D ** -0.5),
        'w_group_router': nrm((DEPTH, D, MOE_GROUPS), D ** -0.5),
        'b_group_router': nrm((DEPTH, MOE_GROUPS), 0.01),
        'w_expert_router': nrm((DEPTH, MOE_GROUPS, D, MOE_EXPERTS_PER_GROUP), D ** -0.5),
        'b_expert_router': nrm((DEPTH, MOE_GROUPS, MOE_EXPERTS_PER_GROUP), 0.01),
        'w_gate': nrm((DEPTH, MOE_EXPERTS, D, MOE_D_FF), D ** -0.5),
        'w_up': nrm((DEPTH, MOE_EXPERTS, D, MOE_D_FF), D ** -0.5),
        'w_down': nrm((DEPTH, MOE_EXPERTS, MOE_D_FF, D), MOE_D_FF ** -0.5),
    }

def reference(x, c, ctx, c_ctx, w_ada, b_ada, g_pre_mix, g_post_mix, g_pre_ffn, g_post_ffn, w_in,
              conv_w, conv_b, dt_bias, a_log, d_skip, g_ssm_norm, hg_lb, g_hg_norm, w_branch_ssm,
              w_branch_hg, w_out, w_group_router, b_group_router, w_expert_router, b_expert_router,
              w_gate, w_up, w_down):
    nb, n_lat, d = x.shape
    rows = n_lat // GRID_W
    lb_all = jnp.cumsum(jax.nn.softmax(hg_lb.astype(jnp.float32), axis=0), axis=0)
    xl, xc = x, ctx
    for layer in range(DEPTH):
        last = layer == DEPTH - 1
        mod_l = (jax.nn.silu(c) @ w_ada[layer] + b_ada[layer])[:, None, :]
        mod_c = (jax.nn.silu(c_ctx) @ w_ada[layer] + b_ada[layer])[None, None, :]
        sh1_l, sc1_l, gt1_l, sh2_l, sc2_l, gt2_l = jnp.split(mod_l, 6, axis=-1)
        sh1_c, sc1_c, gt1_c, sh2_c, sc2_c, gt2_c = jnp.split(mod_c, 6, axis=-1)

        hl = rms_norm(xl, g_pre_mix[layer]) * (1.0 + sc1_l) + sh1_l
        hc = rms_norm(xc, g_pre_mix[layer]) * (1.0 + sc1_c) + sh1_c
        mix_l, mix_c = token_mixer(hl, hc, w_in[layer], conv_w[layer], conv_b[layer], dt_bias[layer],
                                   a_log[layer], d_skip[layer], g_ssm_norm[layer], lb_all[layer],
                                   g_hg_norm[layer], w_branch_ssm[layer], w_branch_hg[layer], w_out[layer],
                                   rows, not last)
        xl = xl + gt1_l * rms_norm(mix_l, g_post_mix[layer])

        hl = rms_norm(xl, g_pre_ffn[layer]) * (1.0 + sc2_l) + sh2_l
        moe_w = (w_group_router[layer], b_group_router[layer], w_expert_router[layer], b_expert_router[layer],
                 w_gate[layer], w_up[layer], w_down[layer])
        if last:
            ffn_l = hier_moe(hl.reshape(-1, d), *moe_w).reshape(xl.shape)
        else:
            xc = xc + gt1_c * rms_norm(mix_c, g_post_mix[layer])
            hc = rms_norm(xc, g_pre_ffn[layer]) * (1.0 + sc2_c) + sh2_c
            ffn = hier_moe(jnp.concatenate([hl.reshape(-1, d), hc.reshape(-1, d)], axis=0), *moe_w)
            ffn_l = ffn[:nb * n_lat].reshape(xl.shape)
            xc = xc + gt2_c * rms_norm(ffn[nb * n_lat:].reshape(xc.shape), g_post_ffn[layer])
        xl = xl + gt2_l * rms_norm(ffn_l, g_post_ffn[layer])
    return xl


_drawn_inputs = setup_inputs


def setup_inputs(seed=0):
    import zlib

    import numpy as np

    out = dict(_drawn_inputs(seed))
    spreads = {}
    factors = {'ctx': 3.987,
     'g_post_mix': 2.746,
     'g_post_ffn': 26.71,
     'conv_b': 8.0,
     'hg_lb': 8.0,
     'g_hg_norm': 6.587,
     'b_group_router': 4.262,
     'b_expert_router': 3.439,
     'g_ssm_norm': 3.212}
    for name, (base, spread) in spreads.items():
        noise = np.random.default_rng([zlib.crc32(name.encode()), seed]).standard_normal(out[name].shape)
        drawn = base * np.exp(spread * noise) if base else spread * noise
        out[name] = __import__('jax').numpy.asarray(drawn.astype(out[name].dtype))
    for name, factor in factors.items():
        out[name] = (out[name] * factor).astype(out[name].dtype)
    return out
```

```python
from contextlib import ExitStack

import numpy as np
import concourse.bass as bass
from concourse import mybir

F32 = mybir.dt.float32
I32 = mybir.dt.int32
U32 = mybir.dt.uint32
U8 = mybir.dt.uint8
ALU = mybir.AluOpType
ACT = mybir.ActivationFunctionType
AX = mybir.AxisListType

P = 128
D = 1024
KT = D // P
LAT = 512
CTX = 256
T = LAT + CTX
NCH = T // P
LCH = LAT // P
GRID_W = 64
ROWS = LAT // GRID_W
EPS = 1e-6

G = 4
HG = 8
HD = 64
GW = HG * HD
NS = 128
DIN = G * GW
HEADS = G * HG
HH = 8
OFF_Z = 0
OFF_X = DIN
OFF_B = OFF_X + DIN
OFF_C = OFF_B + G * NS
OFF_DT = OFF_C + G * NS
OFF_Q = OFF_DT + 2 * HEADS
OFF_F = OFF_Q + D
OFF_I = OFF_F + 2 * D
OFF_OG = OFF_I + D
OFF_GM = OFF_OG + D
OFF_GH = OFF_GM + D
N_IN = OFF_GH + D
ORDER = [[4, 5, 0, 1, 2], [5, 4, 3, 2, 1]]
R_BADA, R_GPRE, R_C, R_CCTX, R_LB, R_GSSM, R_GHG = 0, 48, 56, 64, 72, 104, 120
N_COLS1 = 121
LEVELS = [64, 32, 16, 8, 4, 2, 1]
E = 32
EG = 4
EPG = 8
FF = 512
FT = FF // P
BLOCKS = E + 2 * LAT // P
START = 1
F_MIN = 1e-19


class Own:

    def __init__(self, eng, sem):
        self.eng, self.sem, self.n, self.off = eng, sem, 0, 0

    def mark(self, ins):
        ins.then_inc(self.sem, 1)
        self.n += 1
        return ins

    def wait(self):
        self.eng.wait_ge(self.sem, self.off + self.n)

    def link(self, ins):
        self.mark(ins)
        self.wait()

    def enter(self, i, per):
        self.base, self.per = self.n, per
        self.off = i * per

    def leave(self, trips):
        assert self.n - self.base == self.per, (self.n - self.base, self.per)
        self.n = self.base + self.per * trips
        self.off = 0


def build(nc, x, c, ctx, c_ctx, w_ada, b_ada, g_pre_mix, g_post_mix, g_pre_ffn, g_post_ffn, w_in,
          conv_w, conv_b, dt_bias, a_log, d_skip, g_ssm_norm, hg_lb, g_hg_norm, w_branch_ssm,
          w_branch_hg, w_out, w_group_router, b_group_router, w_expert_router, b_expert_router,
          w_gate, w_up, w_down, out):
    modrows = nc.dram_tensor("modrows", (8, 512), F32, kind="Internal").ap()
    acs_dram = nc.dram_tensor("acs_dram", (2 * HEADS, T), F32, kind="Internal").ap()

    es = ExitStack()
    with es:
        def sb(name, shape, dt=F32):
            return es.enter_context(nc.sbuf_tensor(name, shape, dt))

        def sem(name):
            return es.enter_context(nc.semaphore(name))

        bank = [es.enter_context(nc.psum_tensor(f"bank{i}", [P, 512], F32)) for i in range(8)]

        ident = sb("ident", [P, P])
        ones = sb("ones", [P, P])
        upper = sb("upper", [P, P])
        lower = sb("lower", [P, P])
        chunk_on = sb("chunk_on", [P, T])
        cols1 = sb("cols1", [P, N_COLS1])
        cols2 = sb("cols2", [P, 4, 24])
        sc_in = sb("sc_in", [P, 2 * KT])
        modT = sb("modT", [P, 16, 2])
        amod = sb("amod", [P, KT, 2])
        hT = sb("hT", [P, KT, T])
        ysT = sb("ysT", [P, DIN // P, LAT])
        arena = sb("arena", [P, 34100])

        at = [0]

        def take(*shape):
            n = int(np.prod(shape))
            v = arena[:, at[0]:at[0] + n]
            at[0] += n
            assert at[0] <= 34100, at[0]
            if len(shape) == 1:
                return v
            names = " ".join(f"d{i}" for i in range(len(shape)))
            return v.rearrange(f"p ({names}) -> p {names}", **{f"d{i}": s for i, s in enumerate(shape)})

        hTp = take(KT, LAT)
        ohT = take(KT, LAT)
        after_long = at[0]

        xin = take(NCH, D)
        junk = take(D)
        wada = [take(KT, 512) for _ in range(4)][::-1]
        adar = ysT[0:2, 0:4, :].rearrange("v n f -> v (n f)")
        rows1 = take(P)
        rows2 = take(P)

        at[0] = 24064
        wdt = take(KT, 64)
        dtx = take(T)
        dtu = take(T)
        dtv = take(T)
        dtT = take(T)
        acsT = take(T)
        at[0] = KT * LAT
        wx = take(KT, GW)
        wB = take(KT, NS)
        wC = take(KT, NS)
        cacc = [take(T) for _ in range(2)]
        xw = [v[:, 0:GW] for v in cacc]
        xs = take(4, T)
        CBm = xs[:, 0:2, 0:LAT]
        Dh = [xs[:, 2 + i, 0:LAT] for i in range(2)]
        Wh = [take(LAT) for i in range(2)]
        Bt = take(T)
        Ct = take(LAT)
        xtok = take(NCH, GW)
        Btok = take(NCH, NS)
        xdt = take(2, LCH, GW)
        zs = take(LCH, GW)
        Sst = take(2, LCH, GW)
        stmp = take(GW)
        yt = take(LCH, GW)

        dt_tok = sb("dt_tok", [P, NCH, 2 * HEADS])
        acs_tok = sb("acs_tok", [P, NCH, 2 * HEADS])
        dexp = sb("dexp", [P, NCH, 2 * HEADS])
        eacs = sb("eacs", [P, NCH, 2 * HEADS])
        cdec = sb("cdec", [P, 2 * HEADS, NCH])
        vec64e = sb("vec64e", [2 * HEADS, NCH])
        vec64 = sb("vec64", [2 * HEADS, 4])
        dskb = sb("dskb", [P, 2, HEADS])
        dsum = sb("dsum", [P, HEADS])
        acsg = sb("acsg", [2 * HG, LAT])
        cwg = sb("cwg", [P, 4, 6])
        gsg = sb("gsg", [P, 4])
        ssq = sb("ssq", [P, 8])
        epsb = sb("epsb", [P, 1])
        rst = sb("rst", [P, 8])


        s_rows = sem("rows_loaded")
        s_x = sem("x_loaded")
        s_ctx = sem("ctx_loaded")
        s_vec = sem("vectors_loaded")
        s_ada = [sem(f"w_ada_loaded{r}") for r in range(4)]
        s_const = sem("constants_set")
        s_turned = sem("rows_transposed")
        s_cols = sem("columns_ready")
        s_silu_c = sem("silu_c_ready")
        s_ada_used = sem("w_ada_used")
        s_mod = sem("modulation_ready")
        s_modr = sem("modulation_rows_copied")
        s_modst = sem("modulation_rows_stored")
        s_rstd0 = sem("x_rstd_ready")
        s_xn = sem("x_normalised")
        s_xt = sem("x_transposed")
        s_hl = sem("latent_h_ready")
        s_hc = sem("context_h_ready")
        s_hp = sem("grid_h_ready")
        s_act = sem("scalar_steps")
        s_dve = sem("vector_steps")
        s_pool = sem("gpsimd_steps")
        s_dta = sem("step_size_scalar_stages")
        A_EXP, DT_EXP, DT_LOG, DECAYS_COPIED, DECAY_EXPS = 1, 2, 3, 4, 6
        s_dtv = sem("step_size_vector_stages")
        DT_ABS, DT_ONE_PLUS, SUMS, ENDS_SPREAD, DECAY_DIFFS, FACTORS = 1, 2, 3, 4, 5, 6
        s_dtt = sem("step_size_tensor_stages")
        DT_PROJECTED, SUMS_TURNED, ENDS_BROADCAST = 1, 3, 4
        s_rv = sem("routing_vector_stages")
        GROUP_MAX, EXPERT_DIFFS, CHOICES, SLOT_CHOICES, TABLES = 1, 2, 3, 4, 5
        s_ra = sem("routing_scalar_stages")
        GROUP_EXPS, EXPERT_EXPS = 1, 2
        s_rp = sem("routing_tensor_stages")
        LOGITS, RANKS, SLOT_TABLE = 1, 2, 3
        s_wdt = sem("w_dt_loaded")
        s_acst = sem("acs_stored")
        s_wx = sem("w_x_loaded")
        s_wbc = sem("w_bc_loaded")
        s_wz = sem("w_z_loaded")
        s_acsg = sem("group_decays_loaded")
        s_cwg = sem("group_columns_ready")
        s_xp = sem("x_tile_projected")
        s_xc = sem("x_tile_centre_ready")
        s_cv = sem("x_tile_convolved")
        s_xsil = sem("x_tile_ready")
        s_zp = sem("z_tile_projected")
        s_zc = sem("z_tile_copied")
        s_zs = sem("z_gate_ready")
        s_yi = sem("y_started")
        s_xtr = sem("x_chunk_transposed")
        s_xtk = sem("x_chunk_ready")
        s_btr = sem("b_transposed")
        s_btk = sem("b_chunks_ready")
        s_cb = sem("cb_ready")
        s_cbm = sem("cb_masked")
        s_xdt = sem("x_dt_ready")
        s_bc = sem("decay_row_broadcast")
        s_dd = sem("decay_difference_ready")
        s_le = sem("decay_exp_ready")
        s_ww = sem("weights_ready")
        s_yd = sem("weights_used")
        s_xw = sem("decayed_x_ready")
        s_kv = sem("chunk_state_ready")
        s_kvu = sem("chunk_state_used")
        s_yo = sem("state_output_ready")
        s_you = sem("state_output_used")
        s_yz = sem("gated_y_ready")
        s_ysum = sem("y_squares_summed")
        s_ysq = sem("y_rstd_ready")
        s_yn = sem("y_normalised")
        s_yt = sem("y_transposed")
        s_ys = sem("y_tile_ready")

        w_in_t = w_in[0].rearrange("(k p) n -> p k n", p=P)
        w_ada_t = w_ada[0].rearrange("(k p) n -> p k n", p=P)

        def row_tiles(v):
            return v.rearrange("(r p) -> r p", p=P)

        def modulate_sync(sp):
            sp.dma_start(rows1[R_BADA:R_BADA + 48, :], row_tiles(b_ada[0])).then_inc(s_rows, 16)
            sp.dma_start(rows1[R_GPRE:R_GPRE + 8, :], row_tiles(g_pre_mix[0])).then_inc(s_rows, 16)
            sp.dma_start(rows1[R_C:R_C + 8, :], row_tiles(c[0])).then_inc(s_rows, 16)
            sp.dma_start(rows1[R_CCTX:R_CCTX + 8, :], row_tiles(c_ctx)).then_inc(s_rows, 16)
            sp.dma_start(rows1[R_LB:R_LB + 32, :], hg_lb.rearrange("l d (r p) -> (l d r) p", p=P)).then_inc(s_rows, 16)
            sp.dma_start(rows1[R_GSSM:R_GSSM + 16, :], row_tiles(g_ssm_norm[0])).then_inc(s_rows, 16)
            sp.dma_start(rows1[R_GHG:R_GHG + 1, :], g_hg_norm).then_inc(s_rows, 16)
            sp.dma_start(rows2[0:72, :], conv_w[0].rearrange("k (r p) -> (k r) p", p=P)).then_inc(s_rows, 16)
            sp.dma_start(rows2[72:96, :], row_tiles(conv_b[0])).then_inc(s_rows, 16)
            sp.dma_start(xin[:, 0:LCH, :], x[0].rearrange("(i p) d -> p i d", p=P)).then_inc(s_x, 16)
            sp.dma_start(xin[:, LCH:NCH, :], ctx[0].rearrange("(i p) d -> p i d", p=P)).then_inc(s_ctx, 16)
            for n in range(4):
                sp.dma_start(wada[n], w_ada_t[:, :, n * 512:(n + 1) * 512]).then_inc(s_ada[n], 16)
            sp.dma_start(vec64[:, 0:1], dt_bias[0].rearrange("d (h u) -> (d h) u", u=1)).then_inc(s_vec, 16)
            sp.dma_start(vec64[:, 1:2], a_log[0].rearrange("d (h u) -> (d h) u", u=1)).then_inc(s_vec, 16)
            sp.dma_start(dskb[:, :, :], d_skip[0].rearrange("(u d) h -> u d h", u=1).broadcast_to([P, 2, HEADS])).then_inc(s_vec, 16)

        def modulate_gpsimd(pool, own):
            pool.memset(ones[:, :], 1.0).then_inc(s_const, 1)
            pool.memset(chunk_on[:, :], 1.0).then_inc(own.sem, 1)
            pool.memset(ident[:, :], 0.0).then_inc(own.sem, 1)
            own.n += 2
            own.wait()
            pool.memset(chunk_on[:, :].rearrange("p (c t) -> p c t", t=P)[:, :, 0:1], 0.0).then_inc(s_const, 1)
            pool.affine_select(out=ident[:, :], in_=ident[:, :], compare_op=ALU.not_equal, fill=1.0,
                               base=0, pattern=[[-1, P]], channel_multiplier=1).then_inc(s_const, 1)
            pool.wait_ge(s_const, 3)
            pool.affine_select(out=upper[:, :], in_=ones[:, :], compare_op=ALU.is_ge, fill=0.0,
                               base=0, pattern=[[1, P]], channel_multiplier=-1).then_inc(s_const, 1)
            pool.affine_select(out=lower[:, :], in_=ones[:, :], compare_op=ALU.is_ge, fill=0.0,
                               base=0, pattern=[[-1, P]], channel_multiplier=1).then_inc(s_const, 1)
            for k in range(KT):
                pool.wait_ge(s_hl, k + 1)
                pool.tensor_copy(hTp[:, k, :].rearrange("p (w r) -> p w r", r=ROWS),
                                 hT[:, k, 0:LAT].rearrange("p (r w) -> p w r", r=ROWS)).then_inc(s_hp, 1)

        def modulate_scalar(act, own):
            act.wait_ge(s_cols, 1)
            act.activation(sc_in[:, :], cols1[:, R_C:R_C + 16], ACT.Silu).then_inc(s_silu_c, 1)
            act.wait_ge(s_x, 16)
            for i in range(NCH):
                if i == LCH:
                    act.wait_ge(s_ctx, 16)
                own.link(act.activation(junk, xin[:, i, :], ACT.Square, accum_out=ssq[:, i:i + 1]))
            own.link(act.activation(rst[:, 0:NCH], ssq[:, 0:NCH], ACT.Ln, scale=1.0 / D, bias=epsb[:, 0:1]))
            act.activation(rst[:, 0:NCH], rst[:, 0:NCH], ACT.Exp, scale=-0.5).then_inc(s_rstd0, 1)
            act.wait_ge(s_mod, 1)
            for k in range(KT):
                act.wait_ge(s_xt, 2 * k + 2)
                act.activation(hT[:, k, LAT:T], bank[5 + k % 2][:, 0:CTX], ACT.Identity,
                               scale=amod[:, k, 1:2], bias=modT[:, k, 1:2]).then_inc(s_hc, 1)

        ADA_BANK = [1, 2, 7, 0]

        def modulate_tensor(pe):
            pe.wait_ge(s_const, 3)
            pe.wait_ge(s_rows, 16 * 9)
            pe.transpose(bank[0][:, 0:N_COLS1], rows1[0:N_COLS1, :], ident[0:N_COLS1, 0:N_COLS1])
            pe.transpose(bank[0][:, P:P + 96], rows2[0:96, :], ident[0:96, 0:96]).then_inc(s_turned, 1)
            pe.wait_ge(s_silu_c, 1)
            vecs = sc_in[:, :].rearrange("p (v k) -> p k v", v=2)

            def ada(n):
                pe.wait_ge(s_ada[n], 16)
                for k in range(KT):
                    mm = pe.matmul(bank[ADA_BANK[n]][0:2, :], vecs[:, k, :], wada[n][:, k, :],
                                   start=(k == 0), stop=(k == KT - 1))
                mm.then_inc(s_ada_used, 1)

            def turn_x(k):
                if k >= 2:
                    pe.wait_ge(s_hl, k - 1)
                for i in range(LCH):
                    mm = pe.transpose(bank[3 + k % 2][:, i * P:(i + 1) * P], xin[:, i, k * P:(k + 1) * P], ident[:, :])
                mm.then_inc(s_xt, 1)
                if k >= 2:
                    pe.wait_ge(s_hc, k - 1)
                for i in range(2):
                    mm = pe.transpose(bank[5 + k % 2][:, i * P:(i + 1) * P],
                                      xin[:, LCH + i, k * P:(k + 1) * P], ident[:, :])
                mm.then_inc(s_xt, 1)

            ada(0)
            ada(1)
            pe.wait_ge(s_xn, NCH)
            turn_x(0)
            turn_x(1)
            ada(2)
            ada(3)
            pe.wait_ge(s_modr, 4)
            for f in range(16):
                mm = pe.transpose(bank[1][:, 2 * f:2 * f + 2], adar[:, f * P:(f + 1) * P], ident[0:2, 0:2])
            mm.then_inc(s_turned, 1)
            for k in range(2, KT):
                turn_x(k)

        def modulate_vector(dve, own):
            own.link(dve.memset(epsb[:, :], EPS))
            dve.wait_ge(s_turned, 1)
            own.link(dve.tensor_copy(cols1[:, :], bank[0][:, 0:N_COLS1]))
            dve.tensor_copy(cols2[:, :, :].rearrange("p a b -> p (a b)"), bank[0][:, P:P + 96]).then_inc(s_cols, 1)
            dve.wait_ge(s_rstd0, 1)
            for i in range(NCH):
                dve.tensor_scalar(xin[:, i, :], xin[:, i, :], rst[:, i:i + 1], None, ALU.mult).then_inc(s_xn, 1)
            for n in range(4):
                dve.wait_ge(s_ada_used, n + 1)
                dve.tensor_copy(adar[:, n * 512:(n + 1) * 512], bank[ADA_BANK[n]][0:2, :]).then_inc(s_modr, 1)
            dve.wait_ge(s_turned, 2)
            own.link(dve.tensor_tensor(modT[:, 0:16, :], bank[1][:, 0:32].rearrange("p (f v) -> p f v", v=2),
                                       cols1[:, 0:16].unsqueeze(2).broadcast_to([P, 16, 2]), ALU.add))
            own.link(dve.tensor_scalar(amod[:, :, :], modT[:, 8:16, :], 1.0, None, ALU.add))
            dve.tensor_tensor(amod[:, :, :], amod[:, :, :],
                              cols1[:, R_GPRE:R_GPRE + 8].unsqueeze(2).broadcast_to([P, 8, 2]), ALU.mult).then_inc(s_mod, 1)
            dve.wait_ge(s_mod, 1)
            for k in range(KT):
                dve.wait_ge(s_xt, 2 * k + 1)
                dve.tensor_scalar(hT[:, k, 0:LAT], bank[3 + k % 2][:, :], amod[:, k, 0:1], modT[:, k, 0:1],
                                  ALU.mult, ALU.add).then_inc(s_hl, 1)

        def bc64(v):
            return v.unsqueeze(len(v.shape)).broadcast_to(list(v.shape) + [HD])

        def heads(v):
            return v.rearrange("p (h q) -> p h q", q=HD)

        def ssd_sync(sp):
            sp.wait_ge(s_ada_used, 2)
            sp.dma_start(wdt, w_in_t[:, :, OFF_DT:OFF_DT + 64]).then_inc(s_wdt, 16)
            sp.wait_ge(s_dtv, SUMS)
            sp.dma_start(acs_dram, acsT[0:64, :]).then_inc(s_acst, 16)
            sp.wait_ge(s_acst, 16)
            sp.wait_ge(s_xt, 2 * KT)
            with sp.Fori(0, G) as g:
                sp.wait_ge(s_zp, START + 4 * g)
                sp.dma_start(wx, w_in_t[:, :, bass.ds(OFF_X + g * GW, GW)]).then_inc(s_wx, 16)
                sp.wait_ge(s_xp, START + 6 * g)
                sp.dma_start(wB, w_in_t[:, :, bass.ds(OFF_B + g * NS, NS)]).then_inc(s_wbc, 16)
                sp.dma_start(wC, w_in_t[:, :, bass.ds(OFF_C + g * NS, NS)]).then_inc(s_wbc, 16)
                sp.wait_ge(s_bc, START + 16 * g)
                for d in range(2):
                    sp.dma_start(acsg[d * HG:(d + 1) * HG, :], acs_dram[bass.ds(d * HEADS + g * HG, HG), 0:LAT]).then_inc(s_acsg, 16)

        def ssd_gpsimd(pool):
            with pool.Fori(0, G) as g:
                pool.wait_ge(s_xtk, 6 * g + 6)
                pool.wait_ge(s_dtv, FACTORS)
                pool.wait_ge(s_yt, START + 4 * g)
                for cc in range(LCH):
                    ins = pool.tensor_tensor(heads(yt[:, cc, :]), heads(xtok[:, cc, :]),
                                             bc64(dsum[:, bass.ds(g * HG, HG)]), ALU.mult)
                ins.then_inc(s_yi, 1)
                pool.wait_ge(s_xsil, 6 * g + 6)
                for k in range(10):
                    ch, d = ORDER[k % 2][k // 2], k % 2
                    if k >= 2:
                        pool.wait_ge(s_kv, START + 10 * g + k - 1)
                    pool.tensor_tensor(heads(xw[k % 2]), heads(xtok[:, ch, :]),
                                       bc64(dexp[:, ch, bass.ds(d * HEADS + g * HG, HG)]), ALU.mult).then_inc(s_xw, 1)

        def ssd_scalar(act, own):
            act.wait_ge(s_vec, 48)
            act.activation(vec64[:, 2:3], vec64[:, 1:2], ACT.Exp).then_inc(s_dta, 1)
            act.wait_ge(s_dtv, DT_ABS)
            act.activation(dtu[0:64, :], dtu[0:64, :], ACT.Exp, scale=-1.0).then_inc(s_dta, 1)
            act.wait_ge(s_dtv, DT_ONE_PLUS)
            act.activation(acsT[0:64, :], dtv[0:64, :], ACT.Ln).then_inc(s_dta, 1)
            act.wait_ge(s_dtt, SUMS_TURNED)
            tb = bank[2][:, 0:384].rearrange("p (c h) -> p c h", c=NCH)
            ta = bank[3][:, 0:384].rearrange("p (c h) -> p c h", c=NCH)
            own.link(act.copy(dt_tok[:, :, :], tb))
            own.link(act.copy(acs_tok[:, :, :], ta))
            act.activation(eacs[:, :, :], ta, ACT.Exp).then_inc(s_dta, 1)
            act.wait_ge(s_dtt, ENDS_BROADCAST)
            act.activation(cdec[:, :, :], bank[4][:, 0:384].rearrange("p (h c) -> p h c", c=NCH), ACT.Exp).then_inc(s_dta, 1)
            act.wait_ge(s_dtv, DECAY_DIFFS)
            act.activation(dexp[:, :, :], dexp[:, :, :], ACT.Exp).then_inc(s_dta, 1)
            with act.Fori(0, G) as g:
                act.wait_ge(s_cwg, g + 1)
                act.wait_ge(s_kv, START + 10 * g)
                act.wait_ge(s_yz, START + 4 * g)
                act.wait_ge(s_yd, START + 16 * g)

                def silu(j):
                    act.wait_ge(s_cv, 6 * g + j + 1)
                    dst = xs[:, j, :] if j < 4 else (Bt if j == 4 else Ct)
                    n = LAT if j == 5 else T
                    act.activation(dst[:, 0:n], cacc[j % 2][:, 0:n], ACT.Silu, bias=cwg[:, 3, j:j + 1]).then_inc(s_xsil, 1)

                for j in range(6):
                    act.wait_ge(s_xp, START + 6 * g + j + 1)
                    if j >= 2:
                        act.wait_ge(s_xsil, 6 * g + j - 1)
                    ins = act.activation(cacc[j % 2][:, 0:LAT], bank[2 * (j % 2)][:, :], ACT.Identity, scale=cwg[:, 1, j:j + 1])
                    if j < 5:
                        ins = act.activation(cacc[j % 2][:, LAT:T], bank[2 * (j % 2) + 1][:, 0:CTX], ACT.Identity, scale=cwg[:, 1, j:j + 1])
                    ins.then_inc(s_xc, 1)
                    if j == 4:
                        act.dma_start(wx, w_in_t[:, :, bass.ds(OFF_Z + g * GW, GW)]).then_inc(s_wz, 16)
                    if j:
                        silu(j - 1)
                silu(5)
                for i in range(NCH):
                    act.wait_ge(s_xtr, 6 * g + i + 1)
                    act.copy(xtok[:, i, :], bank[4 + i % 4][:, :]).then_inc(s_xtk, 1)
                act.wait_ge(s_btr, g + 1)
                act.copy(Btok[:, 0:4, :].rearrange("p a b -> p (a b)"), bank[0][:, :])
                act.copy(Btok[:, 4:6, :].rearrange("p a b -> p (a b)"), bank[1][:, 0:CTX]).then_inc(s_btk, 1)
                for j in range(16):
                    act.wait_ge(s_dd, 16 * g + j + 1)
                    act.activation(Dh[j % 2], Dh[j % 2], ACT.Exp).then_inc(s_le, 1)
                    if j % 4 == 3:
                        act.wait_ge(s_zp, START + 4 * g + j // 4 + 1)
                        act.copy(zs[:, j // 4, :], bank[3][:, :]).then_inc(s_zc, 1)
                act.wait_ge(s_zc, 4 * g + 4)
                act.activation(zs.rearrange("p a b -> p (a b)"), zs.rearrange("p a b -> p (a b)"), ACT.Silu).then_inc(s_zs, 1)
                act.wait_ge(s_yd, START + 16 * g + 16)
                for cc in range(LCH):
                    act.wait_ge(s_yz, START + 4 * g + cc + 1)
                    ins = act.activation((Wh + Dh)[cc], yt[:, cc, :], ACT.Square, accum_out=ssq[:, cc:cc + 1])
                ins.then_inc(s_ysum, 1)
                act.wait_ge(s_ysum, 2 * g + 1)
                act.activation(rst[:, 0:4], ssq[:, 0:4], ACT.Ln, scale=1.0 / GW, bias=epsb[:, 0:1]).then_inc(s_ysum, 1)
                act.wait_ge(s_ysum, 2 * g + 2)
                act.activation(rst[:, 0:4], rst[:, 0:4], ACT.Exp, scale=-0.5).then_inc(s_ysq, 1)
                for f in range(4):
                    act.wait_ge(s_yt, START + 4 * g + f + 1)
                    act.activation(ysT[:, bass.ds(g * 4 + f, 1), :].rearrange("p a b -> p (a b)"), bank[f % 2][:, :],
                                   ACT.Identity, scale=gsg[:, f:f + 1]).then_inc(s_ys, 1)

        def ssd_tensor(pe):
            pe.wait_ge(s_wdt, 16)
            pe.wait_ge(s_hl, KT)
            pe.wait_ge(s_hc, KT)
            for k in range(KT):
                pe.matmul(bank[0][0:64, :], wdt[:, k, :], hT[:, k, 0:LAT], start=(k == 0), stop=(k == KT - 1))
            for k in range(KT):
                mm = pe.matmul(bank[1][0:64, 0:CTX], wdt[:, k, :], hT[:, k, LAT:T], start=(k == 0), stop=(k == KT - 1))
            mm.then_inc(s_dtt, 1)
            pe.wait_ge(s_dtv, SUMS)
            for i in range(NCH):
                mm = pe.transpose(bank[2][:, i * 64:(i + 1) * 64], dtT[0:64, i * P:(i + 1) * P], ident[0:64, 0:64])
            mm.then_inc(s_dtt, 1)
            for i in range(NCH):
                mm = pe.transpose(bank[3][:, i * 64:(i + 1) * 64], acsT[0:64, i * P:(i + 1) * P], ident[0:64, 0:64])
            mm.then_inc(s_dtt, 1)
            pe.wait_ge(s_dtv, ENDS_SPREAD)
            pe.matmul(bank[4][:, 0:384], ones[0:64, :], dtx[0:64, 0:384], start=True, stop=True).then_inc(s_dtt, 1)
            pe.wait_ge(s_dta, DECAY_EXPS - 1)
            pe.wait_ge(s_dtv, DECAY_DIFFS)
            with pe.Fori(0, G) as g:
                pe.wait_ge(s_ys, START + 4 * g)
                pe.wait_ge(s_you, START + 8 * g)
                pe.wait_ge(s_wx, 16 * g + 16)
                for j in range(6):
                    if j == 4:
                        pe.wait_ge(s_wbc, 32 * g + 32)
                    if j >= 2:
                        pe.wait_ge(s_cv, 6 * g + j - 1)
                    w = wx[:, :, j * P:(j + 1) * P] if j < 4 else (wB if j == 4 else wC)
                    b = 2 * (j % 2)
                    for k in range(KT):
                        mm = pe.matmul(bank[b][:, :], w[:, k, :], hT[:, k, 0:LAT], start=(k == 0), stop=(k == KT - 1))
                    if j < 5:
                        for k in range(KT):
                            mm = pe.matmul(bank[b + 1][:, 0:CTX], w[:, k, :], hT[:, k, LAT:T], start=(k == 0), stop=(k == KT - 1))
                    mm.then_inc(s_xp, 1)
                pe.wait_ge(s_xsil, 6 * g + 4)
                pe.wait_ge(s_yz, START + 4 * g)
                for i in range(NCH):
                    if i >= 4:
                        pe.wait_ge(s_xtk, 6 * g + i - 3)
                    for f in range(4):
                        mm = pe.transpose(bank[4 + i % 4][:, f * P:(f + 1) * P], xs[:, f, i * P:(i + 1) * P], ident[:, :])
                    mm.then_inc(s_xtr, 1)
                pe.wait_ge(s_xsil, 6 * g + 6)
                for i in range(NCH):
                    mm = pe.transpose(bank[i // 4][:, (i % 4) * P:(i % 4 + 1) * P], Bt[:, i * P:(i + 1) * P], ident[:, :])
                mm.then_inc(s_btr, 1)
                for cc in range(LCH):
                    mm = pe.matmul(bank[2][:, cc * P:(cc + 1) * P], Bt[:, cc * P:(cc + 1) * P], Ct[:, cc * P:(cc + 1) * P],
                                   start=True, stop=True)
                mm.then_inc(s_cb, 1)
                pe.wait_ge(s_acsg, 32 * g + 32)

                def broadcast(j):
                    h, d = j // 2, j % 2
                    if j >= 2:
                        pe.wait_ge(s_dd, 16 * g + j - 1)
                    elif j == 0:
                        pe.wait_ge(s_btk, g + 1)
                    r = d * HG + h
                    pe.matmul(bank[j % 2][:, :], ident[0:16, r:r + 1].broadcast_to([16, P]), acsg[:, :],
                              start=True, stop=True).then_inc(s_bc, 1)

                broadcast(0)
                pe.wait_ge(s_xtk, 6 * g + 6)
                pe.wait_ge(s_xdt, g + 1)
                for j in range(16):
                    h, d = j // 2, j % 2
                    if j < 15:
                        broadcast(j + 1)
                    if j < 10:
                        ch, kd = ORDER[j % 2][j // 2], j % 2
                        pe.wait_ge(s_xw, 10 * g + j + 1)
                        if j:
                            pe.wait_ge(s_kvu, 10 * g + j)
                        else:
                            pe.wait_ge(s_cbm, g + 1)
                        pe.matmul(bank[2][:, :], Btok[:, ch, :], xw[j % 2], start=True, stop=True).then_inc(s_kv, 1)
                    if j % 4 == 2:
                        i = j // 4
                        if i:
                            pe.wait_ge(s_zc, 4 * g + i)
                        else:
                            pe.wait_ge(s_wz, 16 * g + 16)
                        for k in range(KT):
                            mm = pe.matmul(bank[3][:, :], hT[:, k, i * P:(i + 1) * P], wx[:, k, :], start=(k == 0), stop=(k == KT - 1))
                        mm.then_inc(s_zp, 1)
                    pe.wait_ge(s_ww, 16 * g + j + 1)
                    for cc in range(LCH):
                        mm = pe.matmul(bank[4 + cc][:, h * HD:(h + 1) * HD], Wh[j % 2][:, cc * P:(cc + 1) * P],
                                       xdt[:, d, cc, h * HD:(h + 1) * HD], start=(d == 0), stop=(d == 1))
                    mm.then_inc(s_yd, 1)
                for q in range(8):
                    m, d = q // 2, q % 2
                    cc = m if d == 0 else LCH - 1 - m
                    pe.wait_ge(s_kvu, 10 * g + 10)
                    if q >= 2:
                        pe.wait_ge(s_you, START + 8 * g + q - 1)
                    elif q == 1:
                        pe.wait_ge(s_zc, 4 * g + 4)
                    pe.matmul(bank[2 + q % 2][:, :], Ct[:, cc * P:(cc + 1) * P], Sst[:, d, m, :],
                              start=True, stop=True).then_inc(s_yo, 1)
                pe.wait_ge(s_yn, 4 * g + 4)
                for f in range(4):
                    if f >= 2:
                        pe.wait_ge(s_ys, START + 4 * g + f - 1)
                    for cc in range(LCH):
                        mm = pe.transpose(bank[f % 2][:, cc * P:(cc + 1) * P], yt[:, cc, f * P:(f + 1) * P], ident[:, :])
                    mm.then_inc(s_yt, 1)

        def ssd_vector(dve, own):
            R = slice(0, 64)
            dve.wait_ge(s_dtt, DT_PROJECTED)
            dve.wait_ge(s_vec, 48)
            own.mark(dve.tensor_scalar(dtx[R, 0:LAT], bank[0][R, :], vec64[:, 0:1], None, ALU.add))
            own.link(dve.tensor_scalar(dtx[R, LAT:T], bank[1][R, 0:CTX], vec64[:, 0:1], None, ALU.add))
            dve.scalar_tensor_tensor(dtu[R, :], dtx[R, :], -1.0, dtx[R, :], ALU.mult, ALU.max).then_inc(s_dtv, 1)
            dve.wait_ge(s_dta, DT_EXP)
            dve.tensor_scalar(dtv[R, :], dtu[R, :], 1.0, None, ALU.add).then_inc(s_dtv, 1)
            dve.wait_ge(s_dta, DT_LOG)
            own.link(dve.tensor_scalar(dtT[R, :], dtv[R, :], 1.0, None, ALU.is_equal))
            own.mark(dve.scalar_tensor_tensor(dtv[R, :], dtv[R, :], -1.0, dtT[R, :], ALU.add, ALU.add))
            own.link(dve.tensor_tensor(acsT[R, :], acsT[R, :], dtT[R, :], ALU.add))
            own.link(dve.reciprocal(dtv[R, :], dtv[R, :]))
            own.link(dve.tensor_tensor(acsT[R, :], acsT[R, :], dtv[R, :], ALU.mult))
            own.link(dve.tensor_tensor(acsT[R, :], acsT[R, :], dtu[R, :], ALU.mult))
            own.link(dve.scalar_tensor_tensor(dtT[R, :], dtx[R, :], 0.0, acsT[R, :], ALU.max, ALU.add))
            dve.wait_ge(s_dta, A_EXP)
            own.link(dve.tensor_scalar(dtu[R, :], dtT[R, :], vec64[:, 2:3], -1.0, ALU.mult, ALU.mult))
            own.link(dve.tensor_tensor_scan(acsT[R, :], chunk_on[R, :], dtu[R, :], 0.0, ALU.mult, ALU.add))
            ends = acsT[R, :].rearrange("p (c t) -> p c t", t=P)[:, :, P - 1:P]
            own.link(dve.tensor_copy(vec64e[:, :], ends.rearrange("p c t -> p (c t)")))
            Bk = slice(32, 64)
            own.link(dve.tensor_tensor(dtu[Bk, :], dtu[Bk, :], acsT[Bk, :], ALU.subtract))
            dve.tensor_tensor(acsT[Bk, :].rearrange("p (c t) -> p c t", t=P), dtu[Bk, :].rearrange("p (c t) -> p c t", t=P),
                              vec64e[Bk, :].unsqueeze(2).broadcast_to([32, NCH, P]), ALU.add).then_inc(s_dtv, 1)
            dve.wait_ge(s_const, 5)
            dve.tensor_tensor(dtx[R, 0:384].rearrange("p (h c) -> p h c", c=NCH),
                              ident[R, 0:64].unsqueeze(2).broadcast_to([64, 64, NCH]),
                              vec64e[:, :].unsqueeze(1).broadcast_to([64, 64, NCH]), ALU.mult).then_inc(s_dtv, 1)
            dve.wait_ge(s_dta, DECAY_EXPS - 1)
            dve.tensor_tensor(dexp[:, :, :], bank[4][:, 0:384].rearrange("p (h c) -> p c h", c=NCH), acs_tok[:, :, :],
                              ALU.subtract).then_inc(s_dtv, 1)
            dve.wait_ge(s_dta, DECAY_EXPS)
            own.mark(dve.tensor_tensor(dexp[:, :, :], dexp[:, :, :], dt_tok[:, :, :], ALU.mult))
            dve.tensor_tensor(dsum[:, :], dskb[:, 0, :], dskb[:, 1, :], ALU.add).then_inc(s_dtv, 1)
            with dve.Fori(0, G) as g:
                own.enter(g, 50)
                dve.wait_ge(s_ys, START + 4 * g)
                own.mark(dve.tensor_copy(gsg[:, :], cols1[:, bass.ds(R_GSSM + g * 4, 4)]))
                own.mark(dve.tensor_copy(cwg[:, :, 0:4], cols2[:, :, bass.ds(g * 4, 4)]))
                own.mark(dve.tensor_copy(cwg[:, :, 4:5], cols2[:, :, bass.ds(g + 16, 1)]))
                dve.tensor_copy(cwg[:, :, 5:6], cols2[:, :, bass.ds(g + 20, 1)]).then_inc(s_cwg, 1)
                own.wait()
                dve.wait_ge(s_cwg, g + 1)
                for j in range(6):
                    dve.wait_ge(s_xc, 6 * g + j + 1)
                    ca, b = cacc[j % 2], 2 * (j % 2)
                    segs = [(0, LAT, bank[b])] + ([(LAT, CTX, bank[b + 1])] if j < 5 else [])
                    for o, n, ps in segs:
                        own.mark(dve.scalar_tensor_tensor(ca[:, o + 1:o + n], ps[:, 0:n - 1], cwg[:, 0, j:j + 1],
                                                          ca[:, o + 1:o + n], ALU.mult, ALU.add))
                    own.wait()
                    for o, n, ps in segs:
                        ins = dve.scalar_tensor_tensor(ca[:, o:o + n - 1], ps[:, 1:n], cwg[:, 2, j:j + 1],
                                                       ca[:, o:o + n - 1], ALU.mult, ALU.add)
                    ins.then_inc(s_cv, 1)
                dve.wait_ge(s_xtk, 6 * g + 4)
                for d in range(2):
                    for cc in range(LCH):
                        ins = dve.tensor_tensor(heads(xdt[:, d, cc, :]), heads(xtok[:, cc, :]),
                                                bc64(dt_tok[:, cc, bass.ds(d * HEADS + g * HG, HG)]), ALU.mult)
                ins.then_inc(s_xdt, 1)
                dve.wait_ge(s_cb, g + 1)
                for d, mask in ((0, upper), (1, lower)):
                    ins = dve.tensor_tensor(CBm[:, d, :].rearrange("p (c t) -> p c t", t=P),
                                            bank[2][:, :].rearrange("p (c t) -> p c t", t=P),
                                            mask[:, :].unsqueeze(1).broadcast_to([P, LCH, P]), ALU.mult)
                ins.then_inc(s_cbm, 1)
                dve.wait_ge(s_cbm, g + 1)

                def difference(j):
                    h, d = j // 2, j % 2
                    dve.wait_ge(s_bc, START + 16 * g + j + 1)
                    own.link(dve.tensor_tensor(Dh[j % 2].rearrange("p (c t) -> p c t", t=P),
                                               bank[j % 2][:, :].rearrange("p (c t) -> p c t", t=P),
                                               acs_tok[:, 0:LCH, bass.ds(g * HG + (d * HEADS + h), 1)].broadcast_to([P, LCH, P]),
                                               ALU.subtract))
                    dve.tensor_scalar(Dh[j % 2], Dh[j % 2], 0.0, None, ALU.min).then_inc(s_dd, 1)

                def weight(j):
                    dve.wait_ge(s_le, 16 * g + j + 1)
                    if j >= 2:
                        dve.wait_ge(s_yd, START + 16 * g + j - 1)
                    dve.tensor_tensor(Wh[j % 2], Dh[j % 2], CBm[:, j % 2, :], ALU.mult).then_inc(s_ww, 1)

                difference(0)
                for j in range(16):
                    if j < 15:
                        difference(j + 1)
                    weight(j)
                    if j < 10:
                        step, d = j // 2, j % 2
                        dve.wait_ge(s_kv, START + 10 * g + j + 1)
                        new = 1 if step == 0 else step - 1
                        if step == 0:
                            dve.wait_ge(s_yo, START + 8 * g)
                            dve.tensor_copy(Sst[:, d, new, :], bank[2][:, :]).then_inc(s_kvu, 1)
                        else:
                            old = 1 if step == 1 else step - 2
                            dve.wait_ge(s_kvu, 10 * g + j - 1)
                            own.link(dve.tensor_tensor(heads(stmp), heads(Sst[:, d, old, :]),
                                                       cdec[:, bass.ds(d * HEADS + g * HG, HG), ORDER[d][step]:ORDER[d][step] + 1].broadcast_to([P, HG, HD]),
                                                       ALU.mult))
                            dve.tensor_tensor(Sst[:, d, new, :], stmp, bank[2][:, :], ALU.add).then_inc(s_kvu, 1)
                dve.wait_ge(s_yi, g + 1)
                for q in range(8):
                    m, d = q // 2, q % 2
                    cc = m if d == 0 else LCH - 1 - m
                    dve.wait_ge(s_yo, START + 8 * g + q + 1)
                    dve.tensor_tensor(heads(Dh[q % 2]), heads(bank[2 + q % 2][:, :]),
                                      bc64(eacs[:, cc, bass.ds(d * HEADS + g * HG, HG)]), ALU.mult).then_inc(s_you, 1)
                    dve.wait_ge(s_you, START + 8 * g + q + 1)
                    own.link(dve.tensor_tensor(yt[:, cc, :], yt[:, cc, :], Dh[q % 2], ALU.add))
                dve.wait_ge(s_yd, START + 16 * g + 16)
                dve.wait_ge(s_zs, g + 1)
                for cc in range(LCH):
                    own.link(dve.tensor_tensor(yt[:, cc, :], yt[:, cc, :], bank[4 + cc][:, :], ALU.add))
                    dve.tensor_tensor(yt[:, cc, :], yt[:, cc, :], zs[:, cc, :], ALU.mult).then_inc(s_yz, 1)
                dve.wait_ge(s_ysq, g + 1)
                for cc in range(LCH):
                    dve.tensor_scalar(yt[:, cc, :], yt[:, cc, :], rst[:, cc:cc + 1], None, ALU.mult).then_inc(s_yn, 1)
                own.leave(G)

        at[0] = after_long
        wh = [take(KT, P) for _ in range(5)]
        pf = [take(T) for _ in range(2)]
        pq, pog, pV = take(LAT), take(LAT), take(T)
        lf = [take(T) for _ in range(2)]
        kh = [take(T) for _ in range(2)]
        bh = [take(T) for _ in range(2)]
        qh, ogh, Vh = take(LAT), take(LAT), take(NCH, P)
        KD = [take(T) for _ in range(2)]
        KDt = take(2, 5, P)
        QE = [v[:, 0:LAT] for v in lf]
        Eb = [take(2, LAT) for _ in range(2)]
        Wl = [take(2, LAT) for _ in range(2)]
        att = take(LAT)
        Sg = take(2, LCH, P)
        sqb, rsd = take(LAT), take(LAT)
        sog = take(LAT)
        tot = take(2, NCH)
        etot = take(2, NCH)
        lev = take(len(LEVELS), P)
        lb, oml, lbt = take(16), take(16), take(32)
        lbh, omlh, ghg = take(2), take(2), take(1)
        NL = len(LEVELS)
        OFFS = [OFF_F, OFF_F + D, OFF_Q, OFF_OG, OFF_I]
        UW = [0, 0, 1, 1, 2, 3, 4, 4]
        s_wh = [sem(f"head_weights_loaded{i}") for i in range(5)]
        s_lev = sem("level_masks_set")
        s_lbe = sem("bound_exps_ready")
        s_lbd = sem("bound_differences_ready")
        s_lbh = sem("head_bounds_ready")
        s_pu = sem("unit_projected")
        s_pev = sem("unit_copied")
        s_sg = sem("sigmoids_ready")
        s_vc = sem("v_ready")
        s_ln = sem("log_gate_ready")
        s_q = sem("q_og_ready")
        s_b = sem("gate_sums_ready")
        s_kdd = sem("end_differences_ready")
        s_kde = sem("end_exps_ready")
        s_kd = sem("decayed_keys_ready")
        s_kdT = sem("decayed_keys_transposed")
        s_kdc = sem("decayed_keys_copied")
        s_kvH = sem("head_chunk_states_ready")
        s_chain = sem("head_states_ready")
        s_qee = sem("q_exps_ready")
        s_qe = sem("decayed_q_ready")
        s_et = sem("end_decays_ready")
        s_ld = sem("level_differences_ready")
        s_lex = sem("level_exps_ready")
        s_lw = sem("level_operand_ready")
        s_la = sem("level_product_ready")
        s_lp = sem("level_merged")
        s_out = sem("head_output_ready")
        s_sqh = sem("head_squares_ready")
        s_sum = sem("head_squares_summed")
        s_rsl = sem("head_log_ready")
        s_rsH = sem("head_rstd_ready")
        s_ohn = sem("head_normalised")
        s_ohd = sem("head_done")

        def hg_sync(sp):
            sp.wait_ge(s_yt, START + 16)
            sp.wait_ge(s_ysq, G)
            sp.wait_ge(s_yn, 16)

            def load(h, i):
                sp.dma_start(wh[i], w_in_t[:, :, bass.ds(OFFS[i] + h * P, P)]).then_inc(s_wh[i], 16)

            for i in range(5):
                load(0, i)
            with sp.Fori(0, HH - 1) as h:
                for i, u in enumerate([2, 4, 5, 6, 8]):
                    sp.wait_ge(s_pu, 8 * h + u)
                    load(h + 1, i)

        def level_view(v, half):
            return v[:, 0:LAT].rearrange("p (n u) -> p n u", u=2 * half)

        def hg_gpsimd(pool, own):
            pool.wait_ge(s_yt, START + 16)
            pool.wait_ge(s_yn, 16)
            own.link(pool.memset(lev.rearrange("p a b -> p (a b)"), 0.0))
            for i in range(2 * NL):
                half, d = LEVELS[i // 2], i % 2
                v = level_view_p(lev[:, i // 2, :], half)[:, :, (1 - d) * half:(2 - d) * half]
                n = P // (2 * half)
                o = level_view_p(ones[:, :], half)[:, :, 0:half]
                own.link(pool.affine_select(out=v, in_=o, compare_op=ALU.is_ge, fill=0.0, base=-d * half,
                                            pattern=[[-2 * half, n], [0, half]], channel_multiplier=1))
                pool.affine_select(out=v, in_=v, compare_op=ALU.is_ge, fill=0.0, base=(1 + d) * half - 1,
                                   pattern=[[2 * half, n], [0, half]], channel_multiplier=-1).then_inc(s_lev, 1)

            def body(h):
                def end_differences(d):
                    pool.wait_ge(s_b, START + 2 * h + d + 1)
                    pool.wait_ge(s_kdT, START + h)
                    pool.tensor_tensor(KD[d].rearrange("p (c t) -> p c t", t=P),
                                       tot[:, d, :].unsqueeze(2).broadcast_to([P, NCH, P]),
                                       bh[d].rearrange("p (c t) -> p c t", t=P), ALU.subtract).then_inc(s_kdd, 1)

                end_differences(0)
                pool.wait_ge(s_b, START + 2 * h + 2)
                for i in range(NL):
                    if i == 1:
                        end_differences(1)
                    if i == 2:
                        pool.wait_ge(s_pev, START + 8 * h + 8)
                        pool.wait_ge(s_out, START + h)
                    if i == 3:
                        pool.tensor_copy(Vh.rearrange("p a b -> p (a b)"), pV).then_inc(s_vc, 1)
                    half = LEVELS[i]
                    if i >= 2:
                        pool.wait_ge(s_lw, START + NL * h + i - 1)
                    else:
                        pool.wait_ge(s_lw, START + NL * h)
                    ek, eq = [level_view(Eb[i % 2][:, side, :], half) for side in range(2)]
                    n = LAT // (2 * half)
                    for d in range(2):
                        bv = level_view(bh[d], half)
                        mid = bv[:, :, half - 1 + d:half + d].broadcast_to([P, n, half])
                        first, second = (eq, ek) if d else (ek, eq)
                        one, two = (bv[:, :, 0:half], mid) if d else (mid, bv[:, :, 0:half])
                        pool.tensor_tensor(first[:, :, 0:half], one, two, ALU.subtract)
                        one, two = (mid, bv[:, :, half:]) if d else (bv[:, :, half:], mid)
                        ins = pool.tensor_tensor(second[:, :, half:], one, two, ALU.subtract)
                    ins.then_inc(s_ld, 1)

            with pool.Fori(0, HH - 1) as h:
                body(h)
            body(HH - 1)

        def level_view_p(v, half):
            return v.rearrange("p (n u) -> p n u", u=2 * half)

        def hg_scalar(act):
            act.wait_ge(s_lbd, 1)
            act.activation(lbt, lbt, ACT.Exp).then_inc(s_lbe, 1)

            def unit_copy(h, u):
                act.wait_ge(s_pu, 8 * h + u + 1)
                dst, n = [(pf[0][:, 0:LAT], LAT), (pf[0][:, LAT:T], CTX), (pf[1][:, 0:LAT], LAT), (pf[1][:, LAT:T], CTX),
                          (pq, LAT), (pog, LAT), (pV[:, 0:LAT], LAT), (pV[:, LAT:T], CTX)][u]
                act.copy(dst, bank[u % 2][:, 0:n]).then_inc(s_pev, 1)

            def start(h):
                act.wait_ge(s_pev, START + 8 * h + 8)
                act.wait_ge(s_out, START + h)
                act.wait_ge(s_lw, START + NL * h)
                act.wait_ge(s_b, START + 2 * h)
                act.wait_ge(s_la, START + (NL + 1) * h)
                for d in range(2):
                    act.activation(lf[d], pf[d], ACT.Sigmoid)
                    act.activation(kh[d], pf[d], ACT.Sigmoid, scale=-1.0).then_inc(s_sg, 1)
                act.activation(qh, pq, ACT.Sigmoid).then_inc(s_sg, 1)
                act.activation(sog, pog, ACT.Sigmoid).then_inc(s_sg, 1)
                act.wait_ge(s_lbh, h + 1)
                act.wait_ge(s_sg, 4 * h + 4)
                for d in range(2):
                    act.activation(lf[d], lf[d], ACT.Ln, scale=omlh[:, d:d + 1], bias=lbh[:, d:d + 1]).then_inc(s_ln, 1)

            def end_exps(h, d):
                act.wait_ge(s_kdd, 2 * h + d + 1)
                act.activation(KD[d], KD[d], ACT.Exp).then_inc(s_kde, 1)

            def body(h, last):
                if not last:
                    unit_copy(h + 1, 0)
                    unit_copy(h + 1, 1)
                end_exps(h, 0)
                for i in range(NL):
                    if i == 1:
                        if not last:
                            unit_copy(h + 1, 2)
                        end_exps(h, 1)
                        for d in range(2):
                            act.activation(QE[d], bh[d][:, 0:LAT], ACT.Exp).then_inc(s_qee, 1)
                        act.wait_ge(s_chain, START + h)
                        act.activation(etot.rearrange("p a b -> p (a b)"), tot.rearrange("p a b -> p (a b)"), ACT.Exp).then_inc(s_et, 1)
                    act.wait_ge(s_ld, START + NL * h + i + 1)
                    ev = Eb[i % 2].rearrange("p a b -> p (a b)")
                    act.activation(ev, ev, ACT.Exp).then_inc(s_lex, 1)
                    if i == 1:
                        act.wait_ge(s_kdT, START + h + 1)
                        act.wait_ge(s_kvH, START + h)
                        act.copy(KDt[:, 0, 0:4, :].rearrange("p a b -> p (a b)"), bank[7][:, :])
                        act.copy(KDt[:, 1, 0:4, :].rearrange("p a b -> p (a b)"), bank[6][:, :])
                        act.copy(KDt[:, :, 4, :], bank[5][:, 256:512].rearrange("p (a b) -> p a b", a=2)).then_inc(s_kdc, 1)
                    if not last and i in (1, 3, 5):
                        act.wait_ge(s_q, h + 1)
                        unit_copy(h + 1, 3 + i // 2)
                if not last:
                    act.wait_ge(s_vc, h + 1)
                    unit_copy(h + 1, 6)
                act.wait_ge(s_out, START + h + 1)
                act.wait_ge(s_ohd, START + h)
                act.activation(sqb, bank[6][:, :], ACT.Square).then_inc(s_sqh, 1)
                if not last:
                    unit_copy(h + 1, 7)
                    start(h + 1)
                act.wait_ge(s_sum, h + 1)
                act.wait_ge(s_ohn, START + h)
                act.activation(rsd, bank[7][:, :], ACT.Ln, scale=1.0 / P, bias=epsb[:, 0:1]).then_inc(s_rsl, 1)
                act.wait_ge(s_rsl, h + 1)
                act.activation(rsd, rsd, ACT.Exp, scale=-0.5).then_inc(s_rsH, 1)

            for u in range(8):
                unit_copy(0, u)
            start(0)
            with act.Fori(0, HH - 1) as h:
                body(h, False)
            body(HH - 1, True)

        def hg_tensor(pe):
            pe.wait_ge(s_ys, START + 16)
            pe.wait_ge(s_hp, KT)

            def unit(h, u):
                w, b = wh[UW[u]], bank[u % 2]
                pe.wait_ge(s_wh[UW[u]], 16 * h + 16)
                if u >= 2:
                    pe.wait_ge(s_pev, START + 8 * h + u - 1)
                else:
                    pe.wait_ge(s_pev, START + 8 * h)
                if u in (1, 3):
                    for k in range(KT):
                        mm = pe.matmul(b[:, 0:CTX], w[:, k, :], hT[:, k, LAT:T], start=(k == 0), stop=(k == KT - 1))
                elif u < 6:
                    src = hT if u == 5 else hTp
                    for k in range(KT):
                        mm = pe.matmul(b[:, :], w[:, k, :], src[:, k, 0:LAT], start=(k == 0), stop=(k == KT - 1))
                else:
                    for i in range(LCH if u == 6 else 2):
                        for k in range(KT):
                            lhs = hTp[:, k, i * P:(i + 1) * P] if u == 6 else hT[:, k, LAT + i * P:LAT + (i + 1) * P]
                            mm = pe.matmul(b[:, i * P:(i + 1) * P], lhs, w[:, k, :], start=(k == 0), stop=(k == KT - 1))
                mm.then_inc(s_pu, 1)

            for u in range(8):
                unit(0, u)

            def body(h, last):
                if not last:
                    for u in range(4):
                        unit(h + 1, u)
                pe.wait_ge(s_q, h + 1)
                pe.wait_ge(s_lp, START + (NL + 1) * h)
                for cc in range(LCH):
                    cs = slice(cc * P, (cc + 1) * P)
                    for d in range(2):
                        mm = pe.matmul(bank[2][:, cs], kh[d][:, cs], qh[:, cs], start=(d == 0), stop=(d == 1))
                mm.then_inc(s_la, 1)
                for i in range(NL):
                    if i == 1:
                        pe.wait_ge(s_kd, 2 * h + 2)
                        pe.wait_ge(s_ohd, START + h)
                        pe.wait_ge(s_chain, START + h)
                        for d in range(2):
                            for k in range(5):
                                ch = ORDER[d][k]
                                dst = bank[7 - d][:, k * P:(k + 1) * P] if k < 4 else bank[5][:, 256 + d * P:384 + d * P]
                                mm = pe.transpose(dst, KD[d][:, ch * P:(ch + 1) * P], ident[:, :])
                        mm.then_inc(s_kdT, 1)
                    pe.wait_ge(s_lw, START + NL * h + i + 1)
                    pe.wait_ge(s_lp, START + (NL + 1) * h + i)
                    w = Wl[i % 2]
                    for cc in range(LCH):
                        mm = pe.matmul(bank[3 - i % 2][:, cc * P:(cc + 1) * P], w[:, 0, cc * P:(cc + 1) * P], w[:, 1, cc * P:(cc + 1) * P],
                                       start=True, stop=True)
                    mm.then_inc(s_la, 1)
                    if i == 3:
                        pe.wait_ge(s_kdc, h + 1)
                        pe.wait_ge(s_vc, h + 1)
                        for d in range(2):
                            for k in range(5):
                                dst = bank[(4, 7)[d]][:, k * P:(k + 1) * P] if k < 4 else bank[5][:, d * P:(d + 1) * P]
                                mm = pe.matmul(dst, KDt[:, d, k, :], Vh[:, ORDER[d][k], :], start=True, stop=True)
                        mm.then_inc(s_kvH, 1)
                    if not last and i in (2, 4):
                        unit(h + 1, 3 + i // 2)
                if not last:
                    unit(h + 1, 6)
                pe.wait_ge(s_lp, START + (NL + 1) * (h + 1))
                pe.wait_ge(s_chain, START + h + 1)
                pe.wait_ge(s_qe, 2 * h + 2)
                for cc in range(LCH):
                    o, cs = bank[6][:, cc * P:(cc + 1) * P], slice(cc * P, (cc + 1) * P)
                    pe.matmul(o, Vh[:, cc, :], att[:, cs], start=True, stop=False)
                    pe.matmul(o, Sg[:, 0, cc, :], QE[0][:, cs], start=False, stop=False)
                    mm = pe.matmul(o, Sg[:, 1, LCH - 1 - cc, :], QE[1][:, cs], start=False, stop=True)
                mm.then_inc(s_out, 1)
                if not last:
                    unit(h + 1, 7)
                pe.wait_ge(s_sqh, h + 1)
                pe.matmul(bank[7][:, :], ones[:, :], sqb, start=True, stop=True).then_inc(s_sum, 1)

            with pe.Fori(0, HH - 1) as h:
                body(h, False)
            body(HH - 1, True)

        def hg_vector(dve, own):
            a0, a1 = cols1[:, R_LB:R_LB + 16], cols1[:, R_LB + 16:R_LB + 32]
            dve.wait_ge(s_yt, START + 16)
            dve.wait_ge(s_ysq, G)
            own.link(dve.tensor_tensor(lb, a0, a1, ALU.max))
            own.mark(dve.tensor_tensor(lbt[:, 0:16], a0, lb, ALU.subtract))
            dve.tensor_tensor(lbt[:, 16:32], a1, lb, ALU.subtract).then_inc(s_lbd, 1)
            dve.wait_ge(s_lbe, 1)
            own.wait()
            own.link(dve.tensor_tensor(oml, lbt[:, 0:16], lbt[:, 16:32], ALU.add))
            own.link(dve.reciprocal(oml, oml))
            own.link(dve.tensor_tensor(lb, lbt[:, 0:16], oml, ALU.mult))
            own.mark(dve.tensor_scalar(lb, lb, F_MIN, None, ALU.max))
            own.mark(dve.tensor_tensor(oml, lbt[:, 16:32], oml, ALU.mult))
            own.link(dve.tensor_copy(ghg, cols1[:, R_GHG:R_GHG + 1]))
            dve.wait_ge(s_lev, 2 * NL)

            def start(h):
                dve.wait_ge(s_ln, START + 2 * h)
                own.mark(dve.tensor_copy(lbh, lb.rearrange("p (d h) -> p h d", d=2)[:, bass.ds(h, 1), :].rearrange("p a b -> p (a b)")))
                dve.tensor_copy(omlh, oml.rearrange("p (d h) -> p h d", d=2)[:, bass.ds(h, 1), :].rearrange("p a b -> p (a b)")).then_inc(s_lbh, 1)
                dve.wait_ge(s_lbh, h + 1)
                for d in range(2):
                    dve.wait_ge(s_sg, 4 * h + d + 1)
                    own.mark(dve.tensor_scalar(kh[d], kh[d], omlh[:, d:d + 1], None, ALU.mult))
                dve.wait_ge(s_sg, 4 * h + 3)
                dve.tensor_tensor(qh, pq, qh, ALU.mult).then_inc(s_q, 1)

            def output_gate(h):
                dve.wait_ge(s_sg, 4 * h + 4)
                dve.wait_ge(s_ohd, START + h)
                own.mark(dve.tensor_tensor(ogh, pog, sog, ALU.mult))

            def finish(h):
                dve.wait_ge(s_rsH, h + 1)
                dve.scalar_tensor_tensor(sqb, bank[6][:, :], ghg, rsd, ALU.mult, ALU.mult).then_inc(s_ohn, 1)
                dve.wait_ge(s_ohn, START + h + 1)
                own.wait()
                dve.tensor_tensor(ohT[:, bass.ds(h, 1), :].rearrange("p a (r w) -> p (a r) w", w=GRID_W),
                                  sqb.rearrange("p (w r) -> p r w", r=ROWS),
                                  ogh.rearrange("p (r w) -> p r w", w=GRID_W), ALU.mult).then_inc(s_ohd, 1)

            def sums(h):
                dve.wait_ge(s_ld, START + NL * h)
                dve.wait_ge(s_qee, START + 2 * h)
                dve.wait_ge(s_et, START + h)
                for d in range(2):
                    dve.wait_ge(s_ln, START + 2 * h + d + 1)
                    own.link(dve.tensor_tensor_scan(bh[d], chunk_on[:, :], lf[d], 0.0, ALU.mult, ALU.add))
                    c3 = bh[d].rearrange("p (c t) -> p c t", t=P)
                    if d == 0:
                        dve.tensor_copy(tot[:, d, :], c3[:, :, P - 1]).then_inc(s_b, 1)
                    else:
                        own.mark(dve.tensor_copy(tot[:, d, :], c3[:, :, P - 1]))
                        own.link(dve.tensor_tensor(lf[d], lf[d], bh[d], ALU.subtract))
                        dve.tensor_tensor(c3, lf[d].rearrange("p (c t) -> p c t", t=P),
                                          tot[:, d, :].unsqueeze(2).broadcast_to([P, NCH, P]), ALU.add).then_inc(s_b, 1)
            def body(h, last):
                def end_keys(d):
                    dve.wait_ge(s_kde, 2 * h + d + 1)
                    dve.tensor_tensor(KD[d], KD[d], kh[d], ALU.mult).then_inc(s_kd, 1)

                dve.wait_ge(s_q, h + 1)
                end_keys(0)
                dve.wait_ge(s_out, START + h)
                a3 = att.rearrange("p (c t) -> p c t", t=P)

                def merge(i):
                    m = ident[:, :] if i == 0 else lev[:, i - 1, :]
                    dve.copy_predicated(a3, m.bitcast(U32).unsqueeze(1).broadcast_to([P, LCH, P]),
                                        bank[2 + i % 2][:, :].rearrange("p (c t) -> p c t", t=P)).then_inc(s_lp, 1)

                for i in range(NL):
                    if i == 1:
                        end_keys(1)
                        for d in range(2):
                            dve.wait_ge(s_qee, START + 2 * h + d + 1)
                            dve.tensor_tensor(QE[d], QE[d], qh, ALU.mult).then_inc(s_qe, 1)
                    half = LEVELS[i]
                    dve.wait_ge(s_lex, NL * h + i + 1)
                    if i:
                        dve.wait_ge(s_la, START + (NL + 1) * h + i)
                    if i >= 2:
                        dve.wait_ge(s_lp, START + (NL + 1) * h + i - 1)
                    ev, wv = level_view(Eb[i % 2][:, 0, :], half), level_view(Wl[i % 2][:, 0, :], half)
                    for d in range(2):
                        s = slice(d * half, (d + 1) * half)
                        own.mark(dve.tensor_tensor(wv[:, :, s], ev[:, :, s], level_view(kh[d], half)[:, :, s], ALU.mult))
                    dve.tensor_tensor(Wl[i % 2][:, 1, :], Eb[i % 2][:, 1, :], qh, ALU.mult).then_inc(s_lw, 1)
                    if i:
                        merge(i - 1)
                dve.wait_ge(s_kvH, START + h + 1)
                dve.wait_ge(s_et, START + h + 1)
                for k in range(5):
                    if k < 2:
                        dve.wait_ge(s_la, START + (NL + 1) * h + NL + k)
                        dve.wait_ge(s_lp, START + (NL + 1) * h + NL + k - 1)
                    for d in range(2):
                        kv = bank[(4, 7)[d]][:, k * P:(k + 1) * P] if k < 4 else bank[5][:, d * P:(d + 1) * P]
                        if k == 0:
                            ins = dve.tensor_copy(Sg[:, d, 1, :], kv)
                        else:
                            ch, old = ORDER[d][k], 1 if k == 1 else k - 2
                            ins = dve.scalar_tensor_tensor(Sg[:, d, k - 1, :], Sg[:, d, old, :], etot[:, d, ch:ch + 1], kv,
                                                           ALU.mult, ALU.add)
                        if (k, d) == (4, 1):
                            ins.then_inc(s_chain, 1)
                        else:
                            own.mark(ins)
                    if k < 2:
                        merge(NL - 1 + k)
                    own.wait()
                if not last:
                    start(h + 1)
                    sums(h + 1)
                finish(h)
                if not last:
                    output_gate(h + 1)

            start(0)
            sums(0)
            output_gate(0)
            with dve.Fori(0, HH - 1) as h:
                own.enter(h, 31)
                body(h, False)
                own.leave(HH - 1)
            body(HH - 1, True)

        at[0] = after_long
        wm = [take(40, P) for _ in range(2)]
        mixT = take(KT, LAT)
        wout = take(KT, D)
        sgm = [take(LAT) for _ in range(2)]
        sgh = [take(LAT) for _ in range(2)]
        adac = take(512)
        adaw = take(512)
        wada2 = hTp
        at[0] = after_long
        rowv = take(4, D)
        rowg = take(3, D)
        tmpd = [take(D) for _ in range(2)]
        hflat = hT[:, :, :].rearrange("p a b -> p (a b)")
        yflat = ysT[:, :, :].rearrange("p a b -> p (a b)")
        xres = hflat[:, 0:LCH * D].rearrange("p (c d) -> p c d", d=D)
        xl = yflat[:, 0:LCH * D].rearrange("p (c d) -> p c d", d=D)
        h2 = yflat[:, LCH * D:2 * LCH * D].rearrange("p (c d) -> p c d", d=D)
        h2T = mixT
        wr = hflat[:, 4096:4096 + KT * 36].rearrange("p (k e) -> p k e", e=36)
        brow = hflat[:, 4400:4436]
        s_wm = [sem(f"merge_weights_loaded{r}") for r in range(2)]
        s_wout = sem("w_out_loaded")
        s_gmp = sem("gates_projected")
        s_brp = sem("branches_projected")
        s_gms = sem("gates_ready")
        s_mx = sem("mixed_tile_ready")
        s_rowv = sem("rows_broadcast")
        s_xres = sem("x_reloaded")
        s_wr = sem("router_loaded")
        s_mo = sem("mix_chunk_projected")
        s_mr = sem("mix_rstd_ready")
        s_xl = sem("residual_ready")
        s_xl2 = sem("residual_rstd_ready")
        s_h2 = sem("h2_ready")
        s_h2t = sem("h2_transposed")
        s_h2T = sem("h2_columns_ready")
        s_h2st = sem("h2_stored")
        s_aw = sem("modulation_weights_loaded")
        s_ab = sem("modulation_bias_loaded")
        s_ac = sem("modulation_terms_ready")
        s_as = sem("modulation_terms_summed")
        s_ar = sem("modulation_chunk_ready")
        wbs_t = w_branch_ssm[0].rearrange("(k p) n -> p k n", p=P)
        wbh_t = w_branch_hg[0].rearrange("(k p) n -> p k n", p=P)

        h2_dram = nc.dram_tensor("h2_dram", (LAT, D), F32, kind="Internal").ap()
        y_dram = nc.dram_tensor("y_dram", (2 * LAT, D), F32, kind="Internal").ap()

        def merge_sync(sp):
            sp.wait_ge(s_ohd, START + HH)

            def load(j, r, warm):
                if warm:
                    sp.wait_ge(s_brp, j - 1)
                for o, n, src in ((0, 8, w_in_t[:, :, bass.ds(OFF_GM + j * P, P)]),
                                  (8, 8, w_in_t[:, :, bass.ds(OFF_GH + j * P, P)]),
                                  (16, 16, wbs_t[:, :, bass.ds(j * P, P)]),
                                  (32, 8, wbh_t[:, :, bass.ds(j * P, P)])):
                    sp.dma_start(wm[r][:, o:o + n, :], src).then_inc(s_wm[r], 16)
                if warm or r:
                    sp.wait_ge(s_ac, j)
                sp.dma_start(wada2, w_ada_t[:, :, bass.ds(2 * D + j * 512, 512)]).then_inc(s_aw, 16)
                if warm or r:
                    sp.wait_ge(s_modst, 16 * j)
                sp.dma_start(adaw[0:1, :], b_ada[:, bass.ds(2 * D + j * 512, 512)]).then_inc(s_ab, 16)

            load(0, 0, False)
            sp.dma_start(wout, w_out[0].rearrange("(k p) n -> p k n", p=P)).then_inc(s_wout, 16)
            load(1, 1, False)
            with sp.Fori(1, KT // 2) as t:
                for r in range(2):
                    load(t * 2 + r, r, True)
            sp.wait_ge(s_brp, KT)
            sp.wait_ge(s_modst, 16 * 8)
            for i in range(4):
                src = modrows[2 * i:2 * i + 2, :].rearrange("(u r) p -> u (r p)", u=1)
                sp.dma_start(rowv[:, i, :], src.broadcast_to([P, D])).then_inc(s_rowv, 16)
            for i, v in enumerate((g_post_mix, g_pre_ffn, g_post_ffn)):
                sp.dma_start(rowg[:, i, :], v.broadcast_to([P, D])).then_inc(s_rowv, 16)
            sp.dma_start(xres, x[0].rearrange("(i p) d -> p i d", p=P)).then_inc(s_xres, 16)
            sp.dma_start(wr[:, :, 0:4], w_group_router[0].rearrange("(k p) g -> p k g", p=P)).then_inc(s_wr, 16)
            for g in range(EG):
                sp.dma_start(wr[:, :, 4 + 8 * g:12 + 8 * g], w_expert_router[0, g].rearrange("(k p) e -> p k e", p=P)).then_inc(s_wr, 16)
            sp.dma_start(brow[:, 0:4], b_group_router.broadcast_to([P, EG])).then_inc(s_wr, 16)
            sp.dma_start(brow[:, 4:36], b_expert_router.rearrange("u g e -> u (g e)").broadcast_to([P, E])).then_inc(s_wr, 16)
            for cc in range(LCH):
                sp.wait_ge(s_h2, cc + 1)
                sp.dma_start(h2_dram[cc * P:(cc + 1) * P, :], h2[:, cc, :]).then_inc(s_h2st, 16)

        def merge_tensor(pe):
            pe.wait_ge(s_ohd, START + HH)

            def pair(t, warm):
                for r in range(2):
                    j = t * 2 + r
                    pe.wait_ge(s_wm[r], t * 64 + 64)
                    if warm:
                        pe.wait_ge(s_mx, j - 1)
                        pe.wait_ge(s_ar, j - 1)
                    for b, o in ((4 * r, 0), (4 * r + 1, 8)):
                        for k in range(KT):
                            mm = pe.matmul(bank[b][:, :], wm[r][:, o + k, :], hT[:, k, 0:LAT], start=(k == 0), stop=(k == KT - 1))
                    mm.then_inc(s_gmp, 1)
                    for k in range(16):
                        pe.matmul(bank[4 * r + 2][:, :], wm[r][:, 16 + k, :], ysT[:, k, :], start=(k == 0), stop=(k == 15))
                    for k in range(KT):
                        mm = pe.matmul(bank[4 * r + 3][:, :], wm[r][:, 32 + k, :], ohT[:, k, :], start=(k == 0), stop=(k == KT - 1))
                    mm.then_inc(s_brp, 1)
                    pe.wait_ge(s_gms, j + 1)
                    pe.wait_ge(s_ac, j + 1)
                    pe.matmul(bank[4 * r][0:1, :], ones[:, 0:1], adac, start=True, stop=True).then_inc(s_as, 1)

            pair(0, False)
            with pe.Fori(1, KT // 2) as t:
                pair(t, True)
            pe.wait_ge(s_wout, 16)
            pe.wait_ge(s_mx, KT)
            pe.wait_ge(s_ar, KT)
            for cc in range(LCH):
                for hf in range(2):
                    for k in range(KT):
                        mm = pe.matmul(bank[2 * cc + hf][:, :], mixT[:, k, cc * P:(cc + 1) * P], wout[:, k, hf * 512:(hf + 1) * 512],
                                       start=(k == 0), stop=(k == KT - 1))
                mm.then_inc(s_mo, 1)
            pe.wait_ge(s_h2, LCH)
            for k in range(KT):
                if k >= 2:
                    pe.wait_ge(s_h2T, k - 1)
                for cc in range(LCH):
                    mm = pe.transpose(bank[k % 2][:, cc * P:(cc + 1) * P], h2[:, cc, k * P:(k + 1) * P], ident[:, :])
                mm.then_inc(s_h2t, 1)
            pe.wait_ge(s_h2T, KT)
            pe.wait_ge(s_wr, 16 * 7)
            for cc in range(LCH):
                for k in range(KT):
                    mm = pe.matmul(bank[2][:, cc * 36:(cc + 1) * 36], h2T[:, k, cc * P:(cc + 1) * P], wr[:, k, :],
                                   start=(k == 0), stop=(k == KT - 1))
            mm.then_inc(s_rp, 1)

        def merge_scalar(act, own):
            def pair(t, warm):
                for r in range(2):
                    j = t * 2 + r
                    act.wait_ge(s_gmp, j + 1)
                    if warm:
                        act.wait_ge(s_mx, j - 1)
                    act.activation(sgm[r], bank[4 * r][:, :], ACT.Sigmoid)
                    act.activation(sgh[r], bank[4 * r + 1][:, :], ACT.Sigmoid).then_inc(s_gms, 1)
                    act.wait_ge(s_ar, j + 1)
                    act.dma_start(modrows[bass.ds(j, 1), :], adaw[0:1, :]).then_inc(s_modst, 16)

            pair(0, False)
            with act.Fori(1, KT // 2) as t:
                pair(t, True)
            act.wait_ge(s_mx, KT)
            act.wait_ge(s_brp, KT)
            for cc in range(LCH):
                act.wait_ge(s_mo, cc + 1)
                own.mark(act.activation(hflat[:, 5120:5632], bank[2 * cc][:, :], ACT.Square, accum_out=ssq[:, 0:1]))
                own.link(act.activation(hflat[:, 5632:6144], bank[2 * cc + 1][:, :], ACT.Square, accum_out=ssq[:, 1:2]))
                own.link(act.activation(ssq[:, 2:3], ssq[:, 0:1], ACT.Identity, bias=ssq[:, 1:2]))
                if cc:
                    act.wait_ge(s_xl, cc)
                own.link(act.activation(rst[:, 0:1], ssq[:, 2:3], ACT.Ln, scale=1.0 / D, bias=epsb[:, 0:1]))
                act.activation(rst[:, 0:1], rst[:, 0:1], ACT.Exp, scale=-0.5).then_inc(s_mr, 1)
                act.wait_ge(s_xl, cc + 1)
                if cc:
                    act.wait_ge(s_h2, cc)
                own.link(act.activation(hflat[:, 5120:6144], xl[:, cc, :], ACT.Square, accum_out=ssq[:, 3:4]))
                own.link(act.activation(rst[:, 1:2], ssq[:, 3:4], ACT.Ln, scale=1.0 / D, bias=epsb[:, 0:1]))
                act.activation(rst[:, 1:2], rst[:, 1:2], ACT.Exp, scale=-0.5).then_inc(s_xl2, 1)
            for k in range(KT):
                act.wait_ge(s_h2t, k + 1)
                act.copy(h2T[:, k, :], bank[k % 2][:, :]).then_inc(s_h2T, 1)

        def merge_vector(dve, own):
            def pair(t, warm):
                for r in range(2):
                    j = t * 2 + r
                    dve.wait_ge(s_aw, 16 * j + 16)
                    if warm or r:
                        dve.wait_ge(s_as, j)
                    own.link(dve.tensor_scalar(adac, wada2[:, 0, :], sc_in[:, 0:1], None, ALU.mult))
                    for k in range(1, KT):
                        ins = dve.scalar_tensor_tensor(adac, wada2[:, k, :], sc_in[:, k:k + 1], adac, ALU.mult, ALU.add)
                        if k < KT - 1:
                            own.link(ins)
                    ins.then_inc(s_ac, 1)
                    dve.wait_ge(s_gms, j + 1)
                    dve.wait_ge(s_brp, j + 1)
                    own.mark(dve.tensor_tensor(sgm[r], sgm[r], bank[4 * r + 2][:, :], ALU.mult))
                    own.link(dve.tensor_tensor(sgh[r], sgh[r], bank[4 * r + 3][:, :], ALU.mult))
                    dve.tensor_tensor(mixT[:, bass.ds(j, 1), :].rearrange("p a b -> p (a b)"), sgm[r], sgh[r], ALU.add).then_inc(s_mx, 1)
                    dve.wait_ge(s_as, j + 1)
                    dve.wait_ge(s_ab, 16 * j + 16)
                    dve.tensor_tensor(adaw[0:1, :], adaw[0:1, :], bank[4 * r][0:1, :], ALU.add).then_inc(s_ar, 1)

            pair(0, False)
            with dve.Fori(1, KT // 2) as t:
                own.enter(t - 1, 18)
                pair(t, True)
                own.leave(KT // 2 - 1)
            dve.wait_ge(s_rowv, 16 * 7)
            dve.wait_ge(s_xres, 16)
            own.mark(dve.tensor_tensor(rowv[:, 0, :], rowv[:, 0, :], rowg[:, 0, :], ALU.mult))
            own.mark(dve.scalar_tensor_tensor(rowv[:, 2, :], rowv[:, 2, :], 1.0, rowg[:, 1, :], ALU.add, ALU.mult))
            own.link(dve.tensor_tensor(rowv[:, 3, :], rowv[:, 3, :], rowg[:, 2, :], ALU.mult))
            for cc in range(LCH):
                tm = tmpd[cc % 2]
                dve.wait_ge(s_mr, cc + 1)
                for hf in range(2):
                    s = slice(hf * 512, (hf + 1) * 512)
                    own.mark(dve.scalar_tensor_tensor(tm[:, s], bank[2 * cc + hf][:, :], rst[:, 0:1], rowv[:, 0, s], ALU.mult, ALU.mult))
                own.wait()
                dve.tensor_tensor(xl[:, cc, :], tm, xres[:, cc, :], ALU.add).then_inc(s_xl, 1)
                dve.wait_ge(s_xl2, cc + 1)
                own.link(dve.scalar_tensor_tensor(tm, xl[:, cc, :], rst[:, 1:2], rowv[:, 2, :], ALU.mult, ALU.mult))
                dve.tensor_tensor(h2[:, cc, :], tm, rowv[:, 1, :], ALU.add).then_inc(s_h2, 1)

        NT = 2 * LCH
        NB = BLOCKS + 2
        at[0] = 2 * 3 * 4096
        xg = [take(D) for _ in range(2)]
        xgT = take(KT, P)
        gu = [take(FF) for _ in range(2)]
        guT = take(FT, P)
        yb = [take(D) for _ in range(2)]
        gidx = take(NB).bitcast(U32)
        sidx = take(NB).bitcast(U32)
        bexp = take(NB).bitcast(I32)
        npair = take(1).bitcast(I32)
        idg = [take(1).bitcast(U32) for _ in range(2)]
        ids = [take(1).bitcast(U32) for _ in range(2)]
        wsel = take(2, LCH)
        pad = take(1)
        row_keep = take(D)
        assert at[0] <= 34100
        at[0] = 0
        it_i = take(P).bitcast(I32)
        pid_i = take(NT).bitcast(I32)
        iof = take(P)
        pidf = take(NT)
        revg = take(EG)
        lg = take(LCH, 36)
        gmx, gsm, pg = take(LCH), take(LCH), take(LCH)
        gex, goh = take(LCH, EG), take(LCH, EG)
        top = take(LCH, 8)
        topi = take(LCH, 8).bitcast(U32)
        ef = take(2, LCH)
        oh = take(NT, E)
        strict = take(P)
        rank = take(NT, E)
        tsum = take(NT, E)
        cnt, nblk, binc, bst = take(E), take(E), take(E), take(E)
        tE = take(NT, E)
        rk, fl, blk, c1 = take(NT), take(NT), take(NT), take(NT)
        soh = take(NT, P)
        boh = take(NT, NB)
        cmpb = take(NB, E)
        bef = take(NB)
        tbl, inv, hi_ = take(NB), take(NB), take(NB)
        assert at[0] <= after_long
        s_iota = sem("index_rows_ready")
        s_wg = [sem(f"gate_up_loaded{r}") for r in range(2)]
        s_wd = [sem(f"down_loaded{r}") for r in range(2)]
        s_xg = [sem(f"rows_gathered{r}") for r in range(2)]
        s_xgt = sem("rows_transposed_for_experts")
        s_xgc = sem("row_columns_ready")
        s_g = sem("gate_projected")
        s_u = sem("up_projected")
        s_sig = sem("gate_activated")
        s_gu = sem("gated_ready")
        s_gut = sem("gated_transposed")
        s_guc = sem("gated_columns_ready")
        s_d = sem("down_projected")
        s_yb = sem("expert_rows_ready")
        s_sc = [sem(f"rows_scattered{r}") for r in range(2)]
        s_idx = sem("index_columns_copied")
        s_z = sem("gather_rows_cleared")
        s_yl = sem("expert_outputs_loaded")
        s_fa = sem("choices_added")
        s_fs = sem("ffn_squares_ready")
        s_fo = sem("output_chunk_ready")
        s_done = sem("output_stored")

        def route_gpsimd(pool, own):
            pool.wait_ge(s_ac, KT)
            own.mark(pool.iota(it_i, [[1, P]], base=0, channel_multiplier=0))
            own.link(pool.iota(pid_i, [[P, NT]], base=1, channel_multiplier=1))
            own.link(pool.tensor_copy(iof, it_i))
            own.link(pool.tensor_copy(pidf, pid_i))
            pool.tensor_scalar(revg, iof[:, 0:EG], -1.0, float(EG), ALU.mult, ALU.add).then_inc(s_iota, 1)

        def route_scalar(act):
            act.wait_ge(s_rv, GROUP_MAX)
            act.activation(gex.rearrange("p a b -> p (a b)"), gex.rearrange("p a b -> p (a b)"), ACT.Exp).then_inc(s_ra, 1)
            act.wait_ge(s_rv, EXPERT_DIFFS)
            act.activation(ef[:, 1, :], ef[:, 1, :], ACT.Exp).then_inc(s_ra, 1)

        def route_tensor(pe):
            pe.wait_ge(s_rv, CHOICES)
            ohf = oh.rearrange("p a b -> p (a b)")
            pe.matmul(bank[3][:, 0:NT * E], strict, ohf, start=True, stop=True)
            pe.matmul(bank[4][:, 0:NT * E], ones[:, :], ohf, start=True, stop=True).then_inc(s_rp, 1)
            pe.wait_ge(s_rv, SLOT_CHOICES)
            for j in range(NT):
                mm = pe.matmul(bank[5][:, 0:NB], soh[:, j, :], boh[:, j, :], start=(j == 0), stop=(j == NT - 1))
            mm.then_inc(s_rp, 1)

        def route_vector(dve, own):
            L = own.link

            def over(v, n):
                return v.unsqueeze(len(v.shape)).broadcast_to(list(v.shape) + [n])

            dve.wait_ge(s_rp, LOGITS)
            dve.wait_ge(s_iota, 1)
            L(dve.tensor_copy(row_keep, rowv[:, 3, :]))
            L(dve.tensor_tensor(lg, bank[2][:, 0:144].rearrange("p (c e) -> p c e", e=36),
                                brow.unsqueeze(1).broadcast_to([P, LCH, 36]), ALU.add))
            L(dve.tensor_reduce(gmx, lg[:, :, 0:EG], AX.X, ALU.max))
            L(dve.tensor_tensor(goh, lg[:, :, 0:EG], over(gmx, EG), ALU.is_equal))
            L(dve.tensor_tensor(goh, goh, revg.unsqueeze(1).broadcast_to([P, LCH, EG]), ALU.mult))
            L(dve.tensor_reduce(gsm, goh, AX.X, ALU.max))
            L(dve.tensor_tensor(goh, goh, over(gsm, EG), ALU.is_equal))
            dve.tensor_tensor(gex, lg[:, :, 0:EG], over(gmx, EG), ALU.subtract).then_inc(s_rv, 1)
            dve.wait_ge(s_ra, GROUP_EXPS)
            L(dve.tensor_reduce(gsm, gex, AX.X, ALU.add))
            L(dve.reciprocal(pg, gsm))
            L(dve.tensor_scalar(goh, goh, -1.0, 1e30, ALU.add, ALU.mult))
            for g in range(EG):
                own.mark(dve.tensor_tensor(lg[:, :, 4 + 8 * g:12 + 8 * g], lg[:, :, 4 + 8 * g:12 + 8 * g],
                                           goh[:, :, g:g + 1].broadcast_to([P, LCH, EPG]), ALU.add))
            own.wait()
            for cc in range(LCH):
                own.mark(dve.max(top[:, cc, :], lg[:, cc, 4:36]))
            own.wait()
            for cc in range(LCH):
                own.mark(dve.max_index(topi[:, cc, :], top[:, cc, :], lg[:, cc, 4:36]))
            own.wait()
            dve.tensor_tensor(ef[:, 1, :], top[:, :, 1], top[:, :, 0], ALU.subtract).then_inc(s_rv, 1)
            dve.wait_ge(s_ra, EXPERT_EXPS)
            L(dve.tensor_scalar(wsel[:, 0, :], ef[:, 1, :], 1.0, None, ALU.add))
            L(dve.reciprocal(wsel[:, 0, :], wsel[:, 0, :]))
            L(dve.tensor_tensor(wsel[:, 0, :], wsel[:, 0, :], pg, ALU.mult))
            L(dve.tensor_tensor(wsel[:, 1, :], wsel[:, 0, :], ef[:, 1, :], ALU.mult))
            for k in range(2):
                own.mark(dve.tensor_copy(ef[:, k, :], topi[:, :, k]))
            own.wait()
            own.mark(dve.tensor_tensor(strict, upper[:, :], ident[:, :], ALU.subtract))
            dve.tensor_tensor(oh, iof[:, 0:E].unsqueeze(1).broadcast_to([P, NT, E]),
                              over(ef.rearrange("p a b -> p (a b)"), E), ALU.is_equal).then_inc(s_rv, 1)
            own.wait()
            dve.wait_ge(s_rp, RANKS)
            own.mark(dve.tensor_copy(rank.rearrange("p a b -> p (a b)"), bank[3][:, 0:NT * E]))
            own.mark(dve.tensor_copy(tsum.rearrange("p a b -> p (a b)"), bank[4][:, 0:NT * E]))
            own.wait()
            L(dve.tensor_copy(cnt, tsum[:, 0, :]))
            for j in range(1, NT):
                L(dve.tensor_tensor(rank[:, j, :], rank[:, j, :], cnt, ALU.add))
                L(dve.tensor_tensor(cnt, cnt, tsum[:, j, :], ALU.add))
            L(dve.tensor_scalar(nblk, cnt, 0.0, None, ALU.is_gt))
            for m in range(1, LAT // P):
                L(dve.scalar_tensor_tensor(nblk, cnt, float(m * P), nblk, ALU.is_gt, ALU.add))
            L(dve.tensor_tensor_scan(binc, ones[:, 0:E], nblk, 0.0, ALU.mult, ALU.add))
            L(dve.tensor_tensor(bst, binc, nblk, ALU.subtract))
            L(dve.tensor_tensor(tE, oh, rank, ALU.mult))
            L(dve.tensor_reduce(rk, tE, AX.X, ALU.add))
            L(dve.tensor_tensor(tE, oh, bst.unsqueeze(1).broadcast_to([P, NT, E]), ALU.mult))
            L(dve.tensor_reduce(blk, tE, AX.X, ALU.add))
            L(dve.tensor_scalar(fl, rk, float(P), None, ALU.is_ge))
            for m in range(2, LAT // P):
                L(dve.scalar_tensor_tensor(fl, rk, float(m * P), fl, ALU.is_ge, ALU.add))
            L(dve.tensor_tensor(blk, blk, fl, ALU.add))
            L(dve.scalar_tensor_tensor(rk, fl, -float(P), rk, ALU.mult, ALU.add))
            L(dve.tensor_tensor(soh, iof.unsqueeze(1).broadcast_to([P, NT, P]), over(rk, P), ALU.is_equal))
            L(dve.tensor_tensor(boh, iof[:, 0:NB].unsqueeze(1).broadcast_to([P, NT, NB]), over(blk, NB), ALU.is_equal))
            dve.tensor_tensor(boh, boh, over(pidf, NB), ALU.mult).then_inc(s_rv, 1)
            L(dve.tensor_tensor(cmpb, over(iof[:, 0:NB], E), binc.unsqueeze(1).broadcast_to([P, NB, E]), ALU.is_ge))
            L(dve.tensor_reduce(bef, cmpb, AX.X, ALU.add))
            L(dve.tensor_scalar(bef, bef, float(E - 1), None, ALU.min))
            L(dve.tensor_copy(bexp, bef))
            L(dve.tensor_scalar(bef, iof[:, 0:NB], binc[:, E - 1:E], None, ALU.is_lt))
            L(dve.tensor_reduce(c1[:, 0:1], bef.rearrange("p (a b) -> p a b", b=2)[:, :, 0], AX.X, ALU.add))
            L(dve.tensor_copy(npair, c1[:, 0:1]))
            dve.wait_ge(s_rp, SLOT_TABLE)
            L(dve.tensor_copy(tbl, bank[5][:, 0:NB]))
            L(dve.tensor_scalar(inv, tbl, 0.0, None, ALU.is_equal))
            L(dve.tensor_scalar(hi_, tbl, float(LAT), -float(LAT), ALU.is_gt, ALU.mult))
            L(dve.tensor_scalar(inv, inv, 4096.0, -1.0, ALU.mult, ALU.add))
            L(dve.tensor_tensor(tbl, tbl, inv, ALU.add))
            L(dve.tensor_copy(sidx, tbl))
            L(dve.tensor_tensor(tbl, tbl, hi_, ALU.add))
            dve.tensor_copy(gidx, tbl).then_inc(s_rv, 1)

        we = [arena[:, 12288 * r:12288 * (r + 1)] for r in range(2)]
        wgt = [w[:, 0:4096].rearrange("p (k f) -> p k f", f=FF) for w in we]
        wut = [w[:, 4096:8192].rearrange("p (k f) -> p k f", f=FF) for w in we]
        wdt_ = [w[:, 8192:12288].rearrange("p (k n) -> p k n", n=D) for w in we]

        def experts_sync(sp):
            sp.wait_ge(s_rv, TABLES)
            sp.wait_ge(s_h2st, 16 * LCH)
            n = sp.value_load(npair[0:1, 0:1], min_val=NT // 2, max_val=BLOCKS // 2)

            def load(t, warm):
                for r in range(2):
                    i = t * 2 + r
                    e = sp.value_load(bexp[0:1, bass.ds(i, 1)], min_val=0, max_val=E - 1)
                    if warm:
                        sp.wait_ge(s_u, START + i - 1)
                    sp.dma_start(wgt[r], w_gate[0, bass.ds(e, 1)].rearrange("u (k p) f -> p (u k) f", p=P)).then_inc(s_wg[r], 16)
                    sp.dma_start(wut[r], w_up[0, bass.ds(e, 1)].rearrange("u (k p) f -> p (u k) f", p=P)).then_inc(s_wg[r], 16)
                    if warm:
                        sp.wait_ge(s_d, START + i - 1)
                    sp.dma_start(wdt_[r], w_down[0, bass.ds(e, 1)].rearrange("u (k p) n -> p (u k) n", p=P)).then_inc(s_wd[r], 16)

            load(0, False)
            with sp.Fori(1, n) as t:
                load(t, True)
            sp.wait_ge(s_sc[0], n * 16)
            sp.wait_ge(s_sc[1], n * 16)
            yl = arena[:, 0:8192].rearrange("p (j d) -> p j d", d=D)
            sp.dma_start(yl, y_dram.rearrange("(j p) d -> p j d", p=P)).then_inc(s_yl, 16)
            for cc in range(LCH):
                sp.wait_ge(s_fo, cc + 1)
                sp.dma_start(out[0, cc * P:(cc + 1) * P, :], yl[:, cc, :]).then_inc(s_done, 16)
            sp.wait_ge(s_done, 16 * LCH)

        def experts_gpsimd(pool, own):
            pool.wait_ge(s_rv, TABLES)
            pool.wait_ge(s_h2st, 16 * LCH)
            pool.memset(xg[0], 0.0).then_inc(s_z, 1)
            own.link(pool.memset(pad, 0.0))
            pool.memset(xg[1], 0.0).then_inc(s_z, 1)
            pool.wait_ge(s_z, 2)
            n = pool.value_load(npair[0:1, 0:1], min_val=NT // 2, max_val=BLOCKS // 2)

            def gather(i, r, copied):
                pool.tensor_copy(idg[r], gidx[:, bass.ds(i, 1)]).then_inc(s_idx, 1)
                pool.wait_ge(s_idx, copied)
                pool.tensor_tensor(pad, pad, pad, ALU.mult)
                pool.indirect_dma_start(out=xg[r], out_offset=None, in_=h2_dram,
                                        in_offset=bass.IndirectOffsetOnAxis(ap=idg[r], axis=0),
                                        bounds_check=LAT - 1, oob_is_err=False).then_inc(s_xg[r], 16)

            gather(0, 0, 1)
            with pool.Fori(0, n) as t:
                for r in range(2):
                    i = t * 2 + r
                    pool.wait_ge(s_xgt, START + i)
                    gather(i + 1, 1 - r, i * 2 + 2)
                    pool.tensor_copy(ids[r], sidx[:, bass.ds(i, 1)]).then_inc(s_idx, 1)
                    pool.wait_ge(s_yb, START + i + 1)
                    pool.wait_ge(s_idx, i * 2 + 3)
                    pool.tensor_tensor(pad, pad, pad, ALU.mult)
                    pool.indirect_dma_start(out=y_dram, out_offset=bass.IndirectOffsetOnAxis(ap=ids[r], axis=0),
                                            in_=yb[r], in_offset=None,
                                            bounds_check=2 * LAT - 1, oob_is_err=False).then_inc(s_sc[r], 16)
            pool.wait_ge(s_xg[0], n * 16 + 16)

        def experts_scalar(act, own):
            act.wait_ge(s_rv, TABLES)
            n = act.value_load(npair[0:1, 0:1], min_val=NT // 2, max_val=BLOCKS // 2)

            def columns(i):
                act.wait_ge(s_xgt, START + i + 1)
                act.wait_ge(s_u, START + i)
                act.copy(xgT[:, 0:4, :].rearrange("p a b -> p (a b)"), bank[0][:, :])
                act.copy(xgT[:, 4:8, :].rearrange("p a b -> p (a b)"), bank[1][:, :]).then_inc(s_xgc, 1)

            columns(0)
            with act.Fori(0, n) as t:
                for r in range(2):
                    i = t * 2 + r
                    act.wait_ge(s_g, i + 1)
                    if r == 0:
                        act.wait_ge(s_gut, START + t * 2)
                    act.activation(gu[r], bank[2][:, :], ACT.Silu).then_inc(s_sig, 1)
                    columns(i + 1)
                    act.wait_ge(s_gut, START + i + 1)
                    act.wait_ge(s_d, START + i)
                    act.copy(guT.rearrange("p a b -> p (a b)"), bank[4][:, :]).then_inc(s_guc, 1)
            for cc in range(LCH):
                act.wait_ge(s_fa, cc + 1)
                own.link(act.activation(tmpf[cc % 2], ylc[:, cc, :], ACT.Square, accum_out=ssq[:, 4 + cc:5 + cc]))
                own.link(act.activation(rst[:, 4 + cc:5 + cc], ssq[:, 4 + cc:5 + cc], ACT.Ln, scale=1.0 / D, bias=epsb[:, 0:1]))
                act.activation(rst[:, 4 + cc:5 + cc], rst[:, 4 + cc:5 + cc], ACT.Exp, scale=-0.5).then_inc(s_fs, 1)

        def experts_tensor(pe):
            pe.wait_ge(s_rv, TABLES)
            n = pe.value_load(npair[0:1, 0:1], min_val=NT // 2, max_val=BLOCKS // 2)

            def rows(i, r, cnt):
                pe.wait_ge(s_xg[r], cnt)
                pe.wait_ge(s_xgc, START + i)
                for k in range(KT):
                    mm = pe.transpose(bank[k // 4][:, (k % 4) * P:(k % 4 + 1) * P], xg[r][:, k * P:(k + 1) * P], ident[:, :])
                mm.then_inc(s_xgt, 1)

            rows(0, 0, 16)
            with pe.Fori(0, n) as t:
                for r in range(2):
                    i = t * 2 + r
                    pe.wait_ge(s_xgc, START + i + 1)
                    pe.wait_ge(s_wg[r], t * 32 + 32)
                    pe.wait_ge(s_sig, START + i)
                    for k in range(KT):
                        mm = pe.matmul(bank[2][:, :], xgT[:, k, :], wgt[r][:, k, :], start=(k == 0), stop=(k == KT - 1))
                    mm.then_inc(s_g, 1)
                    pe.wait_ge(s_gu, START + i)
                    for k in range(KT):
                        mm = pe.matmul(bank[3][:, :], xgT[:, k, :], wut[r][:, k, :], start=(k == 0), stop=(k == KT - 1))
                    mm.then_inc(s_u, 1)
                    rows(i + 1, 1 - r, t * 16 + 16 + 16 * r)
                    pe.wait_ge(s_gu, START + i + 1)
                    for f in range(FT):
                        mm = pe.transpose(bank[4][:, f * P:(f + 1) * P], gu[r][:, f * P:(f + 1) * P], ident[:, :])
                    mm.then_inc(s_gut, 1)
                    pe.wait_ge(s_guc, i + 1)
                    pe.wait_ge(s_wd[r], t * 16 + 16)
                    pe.wait_ge(s_yb, START + i)
                    for hf in range(2):
                        for f in range(FT):
                            mm = pe.matmul(bank[5 + hf][:, :], guT[:, f, :], wdt_[r][:, f, hf * 512:(hf + 1) * 512],
                                           start=(f == 0), stop=(f == FT - 1))
                    mm.then_inc(s_d, 1)

        ylc = arena[:, 0:4096].rearrange("p (j d) -> p j d", d=D)
        yl1 = arena[:, 4096:8192].rearrange("p (j d) -> p j d", d=D)
        tmpf = [arena[:, 8192 + D * i:8192 + D * (i + 1)] for i in range(2)]

        def experts_vector(dve, own):
            dve.wait_ge(s_rv, TABLES)
            n = dve.value_load(npair[0:1, 0:1], min_val=NT // 2, max_val=BLOCKS // 2)

            def pair(t, warm):
                for r in range(2):
                    i = t * 2 + r
                    dve.wait_ge(s_sig, START + i + 1)
                    dve.wait_ge(s_u, START + i + 1)
                    dve.tensor_tensor(gu[r], gu[r], bank[3][:, :], ALU.mult).then_inc(s_gu, 1)
                    dve.wait_ge(s_d, START + i + 1)
                    if warm:
                        dve.wait_ge(s_sc[r], t * 16)
                    dve.tensor_copy(yb[r][:, 0:512], bank[5][:, :])
                    dve.tensor_copy(yb[r][:, 512:1024], bank[6][:, :]).then_inc(s_yb, 1)

            pair(0, False)
            with dve.Fori(1, n) as t:
                pair(t, True)
            dve.wait_ge(s_yl, 16)
            for cc in range(LCH):
                own.link(dve.tensor_scalar(ylc[:, cc, :], ylc[:, cc, :], wsel[:, 0, cc:cc + 1], None, ALU.mult))
                dve.scalar_tensor_tensor(ylc[:, cc, :], yl1[:, cc, :], wsel[:, 1, cc:cc + 1], ylc[:, cc, :],
                                         ALU.mult, ALU.add).then_inc(s_fa, 1)
            for cc in range(LCH):
                dve.wait_ge(s_fs, cc + 1)
                own.wait()
                dve.scalar_tensor_tensor(ylc[:, cc, :], ylc[:, cc, :], rst[:, 4 + cc:5 + cc], row_keep,
                                         ALU.mult, ALU.mult).then_inc(own.sem, 1)
                own.n += 1
                own.wait()
                dve.tensor_tensor(ylc[:, cc, :], ylc[:, cc, :], xl[:, cc, :], ALU.add).then_inc(s_fo, 1)

        block = es.enter_context(nc.Block())

        @block.sync
        def _(sp):
            modulate_sync(sp)
            ssd_sync(sp)
            hg_sync(sp)
            merge_sync(sp)
            experts_sync(sp)

        @block.gpsimd
        def _(pool):
            for s in (s_ld,):
                pool.sem_inc(s, START)
            own = Own(pool, s_pool)
            modulate_gpsimd(pool, own)
            ssd_gpsimd(pool)
            hg_gpsimd(pool, own)
            route_gpsimd(pool, own)
            experts_gpsimd(pool, own)

        @block.scalar
        def _(act):
            for s in (s_ys, s_pev, s_ln, s_qee, s_et, s_sig, s_xgc):
                act.sem_inc(s, START)
            own = Own(act, s_act)
            modulate_scalar(act, own)
            ssd_scalar(act, own)
            hg_scalar(act)
            merge_scalar(act, own)
            route_scalar(act)
            experts_scalar(act, own)

        @block.tensor
        def _(pe):
            for s in (s_xp, s_zp, s_bc, s_kv, s_yd, s_yo, s_yt, s_kdT, s_la, s_kvH, s_out, s_xgt, s_u, s_d,
                      s_gut):
                pe.sem_inc(s, START)
            modulate_tensor(pe)
            ssd_tensor(pe)
            hg_tensor(pe)
            merge_tensor(pe)
            route_tensor(pe)
            experts_tensor(pe)

        @block.vector
        def _(dve):
            for s in (s_yz, s_you, s_b, s_chain, s_lp, s_lw, s_ohd, s_ohn, s_gu, s_yb):
                dve.sem_inc(s, START)
            own = Own(dve, s_dve)
            modulate_vector(dve, own)
            ssd_vector(dve, own)
            hg_vector(dve, own)
            merge_vector(dve, own)
            route_vector(dve, own)
            experts_vector(dve, own)


_INS = ['x', 'c', 'ctx', 'c_ctx', 'w_ada', 'b_ada', 'g_pre_mix', 'g_post_mix', 'g_pre_ffn', 'g_post_ffn', 'w_in',
        'conv_w', 'conv_b', 'dt_bias', 'a_log', 'd_skip', 'g_ssm_norm', 'hg_lb', 'g_hg_norm', 'w_branch_ssm',
        'w_branch_hg', 'w_out', 'w_group_router', 'b_group_router', 'w_expert_router', 'b_expert_router',
        'w_gate', 'w_up', 'w_down']
_OUTS = [((1, LAT, D), 'float32')]


def kernel(**inputs):
    import numpy as _np
    import concourse.bacc as _bacc
    from concourse import mybir as _mybir
    from concourse.bass_utils import run_bass_kernel_spmd as _run

    nc = _bacc.Bacc("TRN2", target_bir_lowering=False, num_devices=1)
    arrays, args = {}, []
    for name in _INS:
        a = _np.ascontiguousarray(inputs[name])
        arrays[f"in_{name}_dram"] = a
        args.append(nc.dram_tensor(f"in_{name}_dram", a.shape, _mybir.dt.from_np(a.dtype), kind="ExternalInput").ap())
    for i, (shape, dtype) in enumerate(_OUTS):
        dt = _mybir.dt.from_np(_np.dtype(dtype))
        args.append(nc.dram_tensor(f"out_{i}_dram", shape, dt, kind="ExternalOutput").ap())
    build(nc, *args)
    r = _run(nc, [arrays], core_ids=[0])
    got = tuple(r.results[0][f"out_{i}_dram"] for i in range(len(_OUTS)))
    return got[0]
```

```python
from contextlib import ExitStack

import numpy as np
import concourse.bass as bass
from concourse import mybir

F32 = mybir.dt.float32
I32 = mybir.dt.int32
U32 = mybir.dt.uint32
U8 = mybir.dt.uint8
ALU = mybir.AluOpType
ACT = mybir.ActivationFunctionType
AX = mybir.AxisListType

P = 128
D = 1024
KT = D // P
LAT = 512
CTX = 256
T = LAT + CTX
NCH = T // P
LCH = LAT // P
GRID_W = 64
ROWS = LAT // GRID_W
EPS = 1e-6

G = 4
HG = 8
HD = 64
GW = HG * HD
NS = 128
DIN = G * GW
HEADS = G * HG
HH = 8
OFF_Z = 0
OFF_X = DIN
OFF_B = OFF_X + DIN
OFF_C = OFF_B + G * NS
OFF_DT = OFF_C + G * NS
OFF_Q = OFF_DT + 2 * HEADS
OFF_F = OFF_Q + D
OFF_I = OFF_F + 2 * D
OFF_OG = OFF_I + D
OFF_GM = OFF_OG + D
OFF_GH = OFF_GM + D
N_IN = OFF_GH + D
ORDER = [[4, 5, 0, 1, 2], [5, 4, 3, 2, 1]]
R_BADA, R_GPRE, R_C, R_CCTX, R_LB, R_GSSM, R_GHG = 0, 48, 56, 64, 72, 104, 120
N_COLS1 = 121
LEVELS = [64, 32, 16, 8, 4, 2, 1]
E = 32
EG = 4
EPG = 8
FF = 512
FT = FF // P
BLOCKS = E + 2 * LAT // P
START = 1
F_MIN = 1e-19


class Own:

    def __init__(self, eng, sem):
        self.eng, self.sem, self.n, self.off = eng, sem, 0, 0

    def mark(self, ins):
        ins.then_inc(self.sem, 1)
        self.n += 1
        return ins

    def wait(self):
        self.eng.wait_ge(self.sem, self.off + self.n)

    def link(self, ins):
        self.mark(ins)
        self.wait()

    def enter(self, i, per):
        self.base, self.per = self.n, per
        self.off = i * per

    def leave(self, trips):
        assert self.n - self.base == self.per, (self.n - self.base, self.per)
        self.n = self.base + self.per * trips
        self.off = 0


def build(nc, x, c, ctx, c_ctx, w_ada, b_ada, g_pre_mix, g_post_mix, g_pre_ffn, g_post_ffn, w_in,
          conv_w, conv_b, dt_bias, a_log, d_skip, g_ssm_norm, hg_lb, g_hg_norm, w_branch_ssm,
          w_branch_hg, w_out, w_group_router, b_group_router, w_expert_router, b_expert_router,
          w_gate, w_up, w_down, out):
    modrows = nc.dram_tensor("modrows", (8, 512), F32, kind="Internal").ap()
    acs_dram = nc.dram_tensor("acs_dram", (2 * HEADS, T), F32, kind="Internal").ap()

    es = ExitStack()
    with es:
        def sb(name, shape, dt=F32):
            return es.enter_context(nc.sbuf_tensor(name, shape, dt))

        def sem(name):
            return es.enter_context(nc.semaphore(name))

        bank = [es.enter_context(nc.psum_tensor(f"bank{i}", [P, 512], F32)) for i in range(8)]

        ident = sb("ident", [P, P])
        ones = sb("ones", [P, P])
        upper = sb("upper", [P, P])
        lower = sb("lower", [P, P])
        chunk_on = sb("chunk_on", [P, T])
        cols1 = sb("cols1", [P, N_COLS1])
        cols2 = sb("cols2", [P, 4, 24])
        sc_in = sb("sc_in", [P, 2 * KT])
        modT = sb("modT", [P, 16, 2])
        amod = sb("amod", [P, KT, 2])
        hT = sb("hT", [P, KT, T])
        ysT = sb("ysT", [P, DIN // P, LAT])
        arena = sb("arena", [P, 34100])

        at = [0]

        def take(*shape):
            n = int(np.prod(shape))
            v = arena[:, at[0]:at[0] + n]
            at[0] += n
            assert at[0] <= 34100, at[0]
            if len(shape) == 1:
                return v
            names = " ".join(f"d{i}" for i in range(len(shape)))
            return v.rearrange(f"p ({names}) -> p {names}", **{f"d{i}": s for i, s in enumerate(shape)})

        hTp = take(KT, LAT)
        ohT = take(KT, LAT)
        after_long = at[0]

        xin = take(NCH, D)
        junk = take(D)
        wada = [take(KT, 512) for _ in range(4)][::-1]
        adar = ysT[0:2, 0:4, :].rearrange("v n f -> v (n f)")
        rows1 = take(P)
        rows2 = take(P)

        at[0] = 24064
        wdt = take(KT, 64)
        dtx = take(T)
        dtu = take(T)
        dtv = take(T)
        dtT = take(T)
        acsT = take(T)
        at[0] = KT * LAT
        wx = take(KT, GW)
        wB = take(KT, NS)
        wC = take(KT, NS)
        xw = [take(GW) for _ in range(2)]
        xs = take(4, T)
        CBm = ysT[:, 12:14, :]
        Wh = [take(2, LAT), ysT[:, 14:16, :]]
        Bt = take(T)
        Ct = take(LAT)
        xtok = take(NCH, GW)
        Btok = take(NCH, NS)
        xdt = take(2, LCH, GW)
        zs = take(LCH, GW)
        Sst = take(2, LCH, GW)
        stmp = take(GW)
        yt = take(LCH, GW)

        dt_tok = sb("dt_tok", [P, NCH, 2 * HEADS])
        acs_tok = sb("acs_tok", [P, NCH, 2 * HEADS])
        dexp = sb("dexp", [P, NCH, 2 * HEADS])
        eacs = sb("eacs", [P, NCH, 2 * HEADS])
        cdec = sb("cdec", [P, 2 * HEADS, NCH])
        vec64e = sb("vec64e", [2 * HEADS, NCH])
        vec64 = sb("vec64", [2 * HEADS, 4])
        dskb = sb("dskb", [P, 2, HEADS])
        dsum = sb("dsum", [P, HEADS])
        acol = sb("acol", [P, LCH, 2, HG])
        cwg = sb("cwg", [P, 4, 6])
        gsg = sb("gsg", [P, 4])
        ssq = sb("ssq", [P, 8])
        epsb = sb("epsb", [P, 1])
        rst = sb("rst", [P, 8])


        s_rows = sem("rows_loaded")
        s_x = sem("x_loaded")
        s_ctx = sem("ctx_loaded")
        s_vec = sem("vectors_loaded")
        s_ada = [sem(f"w_ada_loaded{r}") for r in range(4)]
        s_const = sem("constants_set")
        s_turned = sem("rows_transposed")
        s_cols = sem("columns_ready")
        s_silu_c = sem("silu_c_ready")
        s_ada_used = sem("w_ada_used")
        s_mod = sem("modulation_ready")
        s_modr = sem("modulation_rows_copied")
        s_modst = sem("modulation_rows_stored")
        s_rstd0 = sem("x_rstd_ready")
        s_xn = sem("x_normalised")
        s_xt = sem("x_transposed")
        s_hl = sem("latent_h_ready")
        s_hc = sem("context_h_ready")
        s_hp = sem("grid_h_ready")
        s_act = sem("scalar_steps")
        s_dve = sem("vector_steps")
        s_pool = sem("gpsimd_steps")
        s_dta = sem("step_size_scalar_stages")
        A_EXP, DT_EXP, DT_LOG, DECAYS_COPIED, DECAY_EXPS = 1, 2, 3, 4, 6
        s_dtv = sem("step_size_vector_stages")
        DT_ABS, DT_ONE_PLUS, SUMS, ENDS_SPREAD, DECAY_DIFFS, FACTORS = 1, 2, 3, 4, 5, 6
        s_dtt = sem("step_size_tensor_stages")
        DT_PROJECTED, SUMS_TURNED, ENDS_BROADCAST = 1, 3, 4
        s_rv = sem("routing_vector_stages")
        GROUP_MAX, EXPERT_DIFFS, CHOICES, EXPERTS, SLOT_CHOICES, TABLES = 1, 2, 3, 4, 5, 6
        s_ra = sem("routing_scalar_stages")
        GROUP_EXPS, EXPERT_EXPS = 1, 2
        s_rp = sem("routing_tensor_stages")
        LOGITS, RANKS, SLOT_TABLE = 1, 2, 3
        s_wdt = sem("w_dt_loaded")
        s_acst = sem("acs_stored")
        s_wx = sem("w_x_loaded")
        s_wbc = sem("w_bc_loaded")
        s_wz = sem("w_z_loaded")
        s_row = [sem(f"head_decays_loaded{r}") for r in range(2)]
        s_cwg = sem("group_columns_ready")
        s_xp = sem("x_tile_projected")
        s_xc = sem("x_tile_centre_ready")
        s_cv = sem("x_tile_convolved")
        s_xsil = sem("x_tile_ready")
        s_zp = sem("z_tile_projected")
        s_zc = sem("z_tile_copied")
        s_zs = sem("z_gate_ready")
        s_yi = sem("y_started")
        s_xtr = sem("x_chunk_transposed")
        s_xtk = sem("x_chunk_ready")
        s_btr = sem("b_transposed")
        s_btk = sem("b_chunks_ready")
        s_cb = sem("cb_ready")
        s_cbm = sem("cb_masked")
        s_xdt = sem("x_dt_ready")
        s_dd = sem("decay_difference_ready")
        s_le = sem("decay_exp_ready")
        s_ww = sem("weights_ready")
        s_yd = sem("weights_used")
        s_xw = sem("decayed_x_ready")
        s_kv = sem("chunk_state_ready")
        s_kvu = sem("chunk_state_used")
        s_yo = sem("state_output_ready")
        s_you = sem("state_output_used")
        s_yz = sem("gated_y_ready")
        s_ysum = sem("y_squares_summed")
        s_ysq = sem("y_rstd_ready")
        s_yn = sem("y_normalised")
        s_yt = sem("y_transposed")
        s_ys = sem("y_tile_ready")

        w_in_t = w_in[0].rearrange("(k p) n -> p k n", p=P)
        w_ada_t = w_ada[0].rearrange("(k p) n -> p k n", p=P)

        def row_tiles(v):
            return v.rearrange("(r p) -> r p", p=P)

        def modulate_sync(sp):
            sp.dma_start(rows1[R_BADA:R_BADA + 48, :], row_tiles(b_ada[0])).then_inc(s_rows, 16)
            sp.dma_start(rows1[R_GPRE:R_GPRE + 8, :], row_tiles(g_pre_mix[0])).then_inc(s_rows, 16)
            sp.dma_start(rows1[R_C:R_C + 8, :], row_tiles(c[0])).then_inc(s_rows, 16)
            sp.dma_start(rows1[R_CCTX:R_CCTX + 8, :], row_tiles(c_ctx)).then_inc(s_rows, 16)
            sp.dma_start(rows1[R_LB:R_LB + 32, :], hg_lb.rearrange("l d (r p) -> (l d r) p", p=P)).then_inc(s_rows, 16)
            sp.dma_start(rows1[R_GSSM:R_GSSM + 16, :], row_tiles(g_ssm_norm[0])).then_inc(s_rows, 16)
            sp.dma_start(rows1[R_GHG:R_GHG + 1, :], g_hg_norm).then_inc(s_rows, 16)
            sp.dma_start(rows2[0:72, :], conv_w[0].rearrange("k (r p) -> (k r) p", p=P)).then_inc(s_rows, 16)
            sp.dma_start(rows2[72:96, :], row_tiles(conv_b[0])).then_inc(s_rows, 16)
            sp.dma_start(xin[:, 0:LCH, :], x[0].rearrange("(i p) d -> p i d", p=P)).then_inc(s_x, 16)
            sp.dma_start(xin[:, LCH:NCH, :], ctx[0].rearrange("(i p) d -> p i d", p=P)).then_inc(s_ctx, 16)
            for n in range(4):
                sp.dma_start(wada[n], w_ada_t[:, :, n * 512:(n + 1) * 512]).then_inc(s_ada[n], 16)
            sp.dma_start(vec64[:, 0:1], dt_bias[0].rearrange("d (h u) -> (d h) u", u=1)).then_inc(s_vec, 16)
            sp.dma_start(vec64[:, 1:2], a_log[0].rearrange("d (h u) -> (d h) u", u=1)).then_inc(s_vec, 16)
            sp.dma_start(dskb[:, :, :], d_skip[0].rearrange("(u d) h -> u d h", u=1).broadcast_to([P, 2, HEADS])).then_inc(s_vec, 16)

        def modulate_gpsimd(pool, own):
            pool.memset(ones[:, :], 1.0).then_inc(s_const, 1)
            pool.memset(chunk_on[:, :], 1.0).then_inc(own.sem, 1)
            pool.memset(ident[:, :], 0.0).then_inc(own.sem, 1)
            own.n += 2
            own.wait()
            pool.memset(chunk_on[:, :].rearrange("p (c t) -> p c t", t=P)[:, :, 0:1], 0.0).then_inc(s_const, 1)
            pool.affine_select(out=ident[:, :], in_=ident[:, :], compare_op=ALU.not_equal, fill=1.0,
                               base=0, pattern=[[-1, P]], channel_multiplier=1).then_inc(s_const, 1)
            pool.wait_ge(s_const, 3)
            pool.affine_select(out=upper[:, :], in_=ones[:, :], compare_op=ALU.is_ge, fill=0.0,
                               base=0, pattern=[[1, P]], channel_multiplier=-1).then_inc(s_const, 1)
            pool.affine_select(out=lower[:, :], in_=ones[:, :], compare_op=ALU.is_ge, fill=0.0,
                               base=0, pattern=[[-1, P]], channel_multiplier=1).then_inc(s_const, 1)
            for k in range(KT):
                pool.wait_ge(s_hl, k + 1)
                pool.tensor_copy(hTp[:, k, :].rearrange("p (w r) -> p w r", r=ROWS),
                                 hT[:, k, 0:LAT].rearrange("p (r w) -> p w r", r=ROWS)).then_inc(s_hp, 1)

        def modulate_scalar(act, own):
            act.wait_ge(s_cols, 1)
            act.activation(sc_in[:, :], cols1[:, R_C:R_C + 16], ACT.Silu).then_inc(s_silu_c, 1)
            act.wait_ge(s_x, 16)
            for i in range(NCH):
                if i == LCH:
                    act.wait_ge(s_ctx, 16)
                own.link(act.activation(junk, xin[:, i, :], ACT.Square, accum_out=ssq[:, i:i + 1]))
            own.link(act.activation(rst[:, 0:NCH], ssq[:, 0:NCH], ACT.Ln, scale=1.0 / D, bias=epsb[:, 0:1]))
            act.activation(rst[:, 0:NCH], rst[:, 0:NCH], ACT.Exp, scale=-0.5).then_inc(s_rstd0, 1)
            act.wait_ge(s_mod, 1)
            for k in range(KT):
                act.wait_ge(s_xt, 2 * k + 2)
                act.activation(hT[:, k, LAT:T], bank[5 + k % 2][:, 0:CTX], ACT.Identity,
                               scale=amod[:, k, 1:2], bias=modT[:, k, 1:2]).then_inc(s_hc, 1)

        ADA_BANK = [1, 2, 7, 0]

        def modulate_tensor(pe):
            pe.wait_ge(s_const, 3)
            pe.wait_ge(s_rows, 16 * 9)
            pe.transpose(bank[0][:, 0:N_COLS1], rows1[0:N_COLS1, :], ident[0:N_COLS1, 0:N_COLS1])
            pe.transpose(bank[0][:, P:P + 96], rows2[0:96, :], ident[0:96, 0:96]).then_inc(s_turned, 1)
            pe.wait_ge(s_silu_c, 1)
            vecs = sc_in[:, :].rearrange("p (v k) -> p k v", v=2)

            def ada(n):
                pe.wait_ge(s_ada[n], 16)
                for k in range(KT):
                    mm = pe.matmul(bank[ADA_BANK[n]][0:2, :], vecs[:, k, :], wada[n][:, k, :],
                                   start=(k == 0), stop=(k == KT - 1))
                mm.then_inc(s_ada_used, 1)

            def turn_x(k):
                if k >= 2:
                    pe.wait_ge(s_hl, k - 1)
                for i in range(LCH):
                    mm = pe.transpose(bank[3 + k % 2][:, i * P:(i + 1) * P], xin[:, i, k * P:(k + 1) * P], ident[:, :])
                mm.then_inc(s_xt, 1)
                if k >= 2:
                    pe.wait_ge(s_hc, k - 1)
                for i in range(2):
                    mm = pe.transpose(bank[5 + k % 2][:, i * P:(i + 1) * P],
                                      xin[:, LCH + i, k * P:(k + 1) * P], ident[:, :])
                mm.then_inc(s_xt, 1)

            ada(0)
            ada(1)
            pe.wait_ge(s_xn, NCH)
            turn_x(0)
            turn_x(1)
            ada(2)
            ada(3)
            pe.wait_ge(s_modr, 4)
            for f in range(16):
                mm = pe.transpose(bank[1][:, 2 * f:2 * f + 2], adar[:, f * P:(f + 1) * P], ident[0:2, 0:2])
            mm.then_inc(s_turned, 1)
            for k in range(2, KT):
                turn_x(k)

        def modulate_vector(dve, own):
            own.link(dve.memset(epsb[:, :], EPS))
            dve.wait_ge(s_turned, 1)
            own.link(dve.tensor_copy(cols1[:, :], bank[0][:, 0:N_COLS1]))
            dve.tensor_copy(cols2[:, :, :].rearrange("p a b -> p (a b)"), bank[0][:, P:P + 96]).then_inc(s_cols, 1)
            dve.wait_ge(s_rstd0, 1)
            for i in range(NCH):
                dve.tensor_scalar(xin[:, i, :], xin[:, i, :], rst[:, i:i + 1], None, ALU.mult).then_inc(s_xn, 1)
            for n in range(4):
                dve.wait_ge(s_ada_used, n + 1)
                dve.tensor_copy(adar[:, n * 512:(n + 1) * 512], bank[ADA_BANK[n]][0:2, :]).then_inc(s_modr, 1)
            dve.wait_ge(s_turned, 2)
            own.link(dve.tensor_tensor(modT[:, 0:16, :], bank[1][:, 0:32].rearrange("p (f v) -> p f v", v=2),
                                       cols1[:, 0:16].unsqueeze(2).broadcast_to([P, 16, 2]), ALU.add))
            own.link(dve.tensor_scalar(amod[:, :, :], modT[:, 8:16, :], 1.0, None, ALU.add))
            dve.tensor_tensor(amod[:, :, :], amod[:, :, :],
                              cols1[:, R_GPRE:R_GPRE + 8].unsqueeze(2).broadcast_to([P, 8, 2]), ALU.mult).then_inc(s_mod, 1)
            dve.wait_ge(s_mod, 1)
            for k in range(KT):
                dve.wait_ge(s_xt, 2 * k + 1)
                dve.tensor_scalar(hT[:, k, 0:LAT], bank[3 + k % 2][:, :], amod[:, k, 0:1], modT[:, k, 0:1],
                                  ALU.mult, ALU.add).then_inc(s_hl, 1)

        def bc64(v):
            return v.unsqueeze(len(v.shape)).broadcast_to(list(v.shape) + [HD])

        def heads(v):
            return v.rearrange("p (h q) -> p h q", q=HD)

        def x_weights(eng, g):
            eng.dma_start(wx, w_in_t[:, :, bass.ds(OFF_X + g * GW, GW)]).then_inc(s_wx, 16)

        def bc_weights(sp, g):
            sp.dma_start(wB, w_in_t[:, :, bass.ds(OFF_B + g * NS, NS)]).then_inc(s_wbc, 16)
            sp.dma_start(wC, w_in_t[:, :, bass.ds(OFF_C + g * NS, NS)]).then_inc(s_wbc, 16)

        def tile_of(j):
            return xs[:, j, :] if j < 4 else (Bt if j == 4 else Ct)

        def segments(j, first):
            lat = 3 if j == 5 else (4 if first and j % 2 else 0)
            return [(0, LAT, bank[lat])] + ([(LAT, CTX, bank[lat + 1])] if j < 5 else [])

        def ssd_sync(sp):
            x_weights(sp, 0)
            sp.wait_ge(s_ada_used, 2)
            sp.dma_start(wdt, w_in_t[:, :, OFF_DT:OFF_DT + 64]).then_inc(s_wdt, 16)
            sp.wait_ge(s_dtv, SUMS)
            sp.dma_start(acs_dram, acsT[0:64, :]).then_inc(s_acst, 16)
            sp.wait_ge(s_acst, 16)
            sp.wait_ge(s_xt, 2 * KT)
            bc_weights(sp, 0)
            acs_rows = acs_dram.rearrange("(d r) t -> r d t", d=2)

            def body(g, last):
                sp.wait_ge(s_ys, START + 4 * g)
                for h in range(HG):
                    sp.wait_ge(s_yd, START + 16 * g + max(2 * h - 2, 0))
                    sp.dma_start(Wh[h % 2], acs_rows[bass.ds(g * HG + h, 1), :, 0:LAT].broadcast_to([P, 2, LAT])).then_inc(s_row[h % 2], 16)
                    if h == 3 and not last:
                        sp.wait_ge(s_zp, START + 4 * g + 4)
                        x_weights(sp, g + 1)
                    if h == 5 and not last:
                        sp.wait_ge(s_xp, START + 6 * g + 6)
                        bc_weights(sp, g + 1)

            with sp.Fori(0, G - 1) as g:
                body(g, False)
            body(G - 1, True)

        def ssd_gpsimd(pool):
            with pool.Fori(0, G) as g:
                pool.wait_ge(s_xtk, 6 * g + 6)
                pool.wait_ge(s_dtv, FACTORS)
                pool.wait_ge(s_yt, START + 4 * g)
                for cc in range(LCH):
                    ins = pool.tensor_tensor(heads(yt[:, cc, :]), heads(xtok[:, cc, :]),
                                             bc64(dsum[:, bass.ds(g * HG, HG)]), ALU.mult)
                ins.then_inc(s_yi, 1)
                for k in range(10):
                    ch, d = ORDER[k % 2][k // 2], k % 2
                    pool.wait_ge(s_kv, START + 10 * g + max(k - 1, 0))
                    pool.tensor_tensor(heads(xw[k % 2]), heads(xtok[:, ch, :]),
                                       bc64(dexp[:, ch, bass.ds(d * HEADS + g * HG, HG)]), ALU.mult).then_inc(s_xw, 1)

        def ssd_scalar(act, own):
            act.wait_ge(s_vec, 48)
            act.activation(vec64[:, 2:3], vec64[:, 1:2], ACT.Exp).then_inc(s_dta, 1)
            act.wait_ge(s_dtv, DT_ABS)
            act.activation(dtu[0:64, :], dtu[0:64, :], ACT.Exp, scale=-1.0).then_inc(s_dta, 1)
            act.wait_ge(s_dtv, DT_ONE_PLUS)
            act.activation(acsT[0:64, :], dtv[0:64, :], ACT.Ln).then_inc(s_dta, 1)
            act.wait_ge(s_dtt, SUMS_TURNED)
            tb = bank[2][:, 0:384].rearrange("p (c h) -> p c h", c=NCH)
            ta = bank[3][:, 0:384].rearrange("p (c h) -> p c h", c=NCH)
            own.link(act.copy(dt_tok[:, :, :], tb))
            own.link(act.copy(acs_tok[:, :, :], ta))
            act.activation(eacs[:, :, :], ta, ACT.Exp).then_inc(s_dta, 1)
            act.wait_ge(s_dtt, ENDS_BROADCAST)
            act.activation(cdec[:, :, :], bank[6][:, 0:384].rearrange("p (h c) -> p h c", c=NCH), ACT.Exp).then_inc(s_dta, 1)
            act.wait_ge(s_dtv, DECAY_DIFFS)
            act.activation(dexp[:, :, :], dexp[:, :, :], ACT.Exp).then_inc(s_dta, 1)

            def centre(g, j, first):
                act.wait_ge(s_xp, START + 6 * g + j + 1)
                for o, n, ps in segments(j, first):
                    ins = act.activation(tile_of(j)[:, o:o + n], ps[:, 0:n], ACT.Identity, scale=cwg[:, 1, j:j + 1])
                ins.then_inc(s_xc, 1)
                if j == 3:
                    act.dma_start(wx, w_in_t[:, :, bass.ds(OFF_Z + g * GW, GW)]).then_inc(s_wz, 16)

            def silu(g, j):
                act.wait_ge(s_cv, 6 * g + j + 1)
                v = tile_of(j)
                act.activation(v, v, ACT.Silu, bias=cwg[:, 3, j:j + 1]).then_inc(s_xsil, 1)

            def body(g, last):
                act.wait_ge(s_kv, START + 10 * g)
                act.wait_ge(s_yz, START + 4 * g)
                act.wait_ge(s_yd, START + 16 * g)
                for i in range(NCH):
                    act.wait_ge(s_xtr, 6 * g + i + 1)
                    act.copy(xtok[:, i, :], bank[4 + i % 4][:, :]).then_inc(s_xtk, 1)
                act.wait_ge(s_btr, g + 1)
                act.copy(Btok[:, 0:4, :].rearrange("p a b -> p (a b)"), bank[0][:, :])
                act.copy(Btok[:, 4:6, :].rearrange("p a b -> p (a b)"), bank[1][:, 0:CTX]).then_inc(s_btk, 1)
                for j in range(16):
                    act.wait_ge(s_dd, 16 * g + j + 1)
                    w = Wh[j // 2 % 2][:, j % 2, :]
                    act.activation(w, w, ACT.Exp).then_inc(s_le, 1)
                    if j < 4:
                        act.wait_ge(s_zp, START + 4 * g + j + 1)
                        act.copy(zs[:, j, :], bank[3][:, :]).then_inc(s_zc, 1)
                    if not last and j in (9, 11, 13):
                        if j == 9:
                            act.wait_ge(s_cwg, g + 2)
                        centre(g + 1, (j - 9) // 2, False)
                act.wait_ge(s_zc, 4 * g + 4)
                act.activation(zs.rearrange("p a b -> p (a b)"), zs.rearrange("p a b -> p (a b)"), ACT.Silu).then_inc(s_zs, 1)
                if not last:
                    for j in range(3):
                        silu(g + 1, j)
                    centre(g + 1, 3, False)
                    silu(g + 1, 3)
                act.wait_ge(s_yd, START + 16 * g + 16)
                for cc in range(LCH):
                    act.wait_ge(s_yz, START + 4 * g + cc + 1)
                    ins = act.activation(Wh[cc // 2][:, cc % 2, :], yt[:, cc, :], ACT.Square, accum_out=ssq[:, cc:cc + 1])
                ins.then_inc(s_ysum, 1)
                act.wait_ge(s_ysum, 2 * g + 1)
                act.activation(rst[:, 0:4], ssq[:, 0:4], ACT.Ln, scale=1.0 / GW, bias=epsb[:, 0:1]).then_inc(s_ysum, 1)
                act.wait_ge(s_ysum, 2 * g + 2)
                act.activation(rst[:, 0:4], rst[:, 0:4], ACT.Exp, scale=-0.5).then_inc(s_ysq, 1)
                if not last:
                    centre(g + 1, 4, False)
                    centre(g + 1, 5, False)
                for f in range(4):
                    act.wait_ge(s_yt, START + 4 * g + f + 1)
                    act.activation(ysT[:, bass.ds(g * 4 + f, 1), :].rearrange("p a b -> p (a b)"), bank[4 + f][:, :],
                                   ACT.Identity, scale=gsg[:, f:f + 1]).then_inc(s_ys, 1)
                if not last:
                    silu(g + 1, 4)
                    silu(g + 1, 5)

            act.wait_ge(s_cwg, 1)
            for j in range(6):
                centre(0, j, True)
                if j:
                    silu(0, j - 1)
            silu(0, 5)
            with act.Fori(0, G - 1) as g:
                body(g, False)
            body(G - 1, True)

        def ssd_tensor(pe):
            def project(g, j, first, parts=(0, 1)):
                w = wx[:, :, j * P:(j + 1) * P] if j < 4 else (wB if j == 4 else wC)
                segs = segments(j, first)
                if 0 in parts:
                    if j in (0, 4):
                        pe.wait_ge(s_wx if j == 0 else s_wbc, (16 if j == 0 else 32) * (g + 1))
                    if j == 5:
                        pe.wait_ge(s_you, START + 8 * g)
                    elif not first and j == 0:
                        pe.wait_ge(s_btk, g)
                    elif not first or j >= 2:
                        pe.wait_ge(s_cv, 6 * g + j - (1 if first else 0))
                for s, (o, n, ps) in enumerate(segs):
                    if s in parts:
                        for k in range(KT):
                            mm = pe.matmul(ps[:, 0:n], w[:, k, :], hT[:, k, o:o + n], start=(k == 0), stop=(k == KT - 1))
                if len(segs) - 1 in parts:
                    mm.then_inc(s_xp, 1)

            pe.wait_ge(s_wdt, 16)
            pe.wait_ge(s_hl, KT)
            pe.wait_ge(s_hc, KT)
            for k in range(KT):
                pe.matmul(bank[0][0:64, :], wdt[:, k, :], hT[:, k, 0:LAT], start=(k == 0), stop=(k == KT - 1))
            for k in range(KT):
                mm = pe.matmul(bank[1][0:64, 0:CTX], wdt[:, k, :], hT[:, k, LAT:T], start=(k == 0), stop=(k == KT - 1))
            mm.then_inc(s_dtt, 1)
            pe.wait_ge(s_dtv, DT_ABS)
            project(0, 0, True)
            project(0, 1, True)
            pe.wait_ge(s_dtv, SUMS)
            for i in range(NCH):
                mm = pe.transpose(bank[2][:, i * 64:(i + 1) * 64], dtT[0:64, i * P:(i + 1) * P], ident[0:64, 0:64])
            mm.then_inc(s_dtt, 1)
            for i in range(NCH):
                mm = pe.transpose(bank[3][:, i * 64:(i + 1) * 64], acsT[0:64, i * P:(i + 1) * P], ident[0:64, 0:64])
            mm.then_inc(s_dtt, 1)
            pe.wait_ge(s_dtv, ENDS_SPREAD)
            pe.matmul(bank[6][:, 0:384], ones[0:64, :], dtx[0:64, 0:384], start=True, stop=True).then_inc(s_dtt, 1)
            pe.wait_ge(s_dta, DECAY_EXPS - 1)
            pe.wait_ge(s_dtv, DECAY_DIFFS)

            def body(g, last):
                pe.wait_ge(s_xsil, 6 * g + 4)
                pe.wait_ge(s_ys, START + 4 * g)
                for i in range(NCH):
                    if i >= 4:
                        pe.wait_ge(s_xtk, 6 * g + i - 3)
                    for f in range(4):
                        mm = pe.transpose(bank[4 + i % 4][:, f * P:(f + 1) * P], xs[:, f, i * P:(i + 1) * P], ident[:, :])
                    mm.then_inc(s_xtr, 1)
                pe.wait_ge(s_xsil, 6 * g + 6)
                for i in range(NCH):
                    mm = pe.transpose(bank[i // 4][:, (i % 4) * P:(i % 4 + 1) * P], Bt[:, i * P:(i + 1) * P], ident[:, :])
                mm.then_inc(s_btr, 1)
                pe.wait_ge(s_you, START + 8 * g)
                for cc in range(LCH):
                    mm = pe.matmul(bank[2][:, cc * P:(cc + 1) * P], Bt[:, cc * P:(cc + 1) * P], Ct[:, cc * P:(cc + 1) * P],
                                   start=True, stop=True)
                mm.then_inc(s_cb, 1)
                for j in range(16):
                    h, d = j // 2, j % 2
                    if j < 4:
                        if j:
                            pe.wait_ge(s_zc, 4 * g + j)
                        else:
                            pe.wait_ge(s_wz, 16 * g + 16)
                        for k in range(KT):
                            mm = pe.matmul(bank[3][:, :], hT[:, k, j * P:(j + 1) * P], wx[:, k, :], start=(k == 0), stop=(k == KT - 1))
                        mm.then_inc(s_zp, 1)
                    if j < 10:
                        ch = ORDER[j % 2][j // 2]
                        pe.wait_ge(s_xw, 10 * g + j + 1)
                        if j:
                            pe.wait_ge(s_kvu, 10 * g + j)
                        else:
                            pe.wait_ge(s_cbm, g + 1)
                            pe.wait_ge(s_btk, g + 1)
                        pe.matmul(bank[2][:, :], Btok[:, ch, :], xw[j % 2], start=True, stop=True).then_inc(s_kv, 1)
                    if not last and j in (8, 10, 12):
                        project(g + 1, (j - 8) // 2, False)
                    if j == 0:
                        pe.wait_ge(s_xtk, 6 * g + 6)
                        pe.wait_ge(s_xdt, g + 1)
                    pe.wait_ge(s_ww, 16 * g + j + 1)
                    for cc in range(LCH):
                        mm = pe.matmul(bank[4 + cc][:, h * HD:(h + 1) * HD], Wh[h % 2][:, d, cc * P:(cc + 1) * P],
                                       xdt[:, d, cc, h * HD:(h + 1) * HD], start=(d == 0), stop=(d == 1))
                    mm.then_inc(s_yd, 1)
                for q in range(8):
                    m, d = q // 2, q % 2
                    cc = m if d == 0 else LCH - 1 - m
                    pe.wait_ge(s_kvu, 10 * g + 10)
                    if q >= 2:
                        pe.wait_ge(s_you, START + 8 * g + q - 1)
                    elif q == 1:
                        pe.wait_ge(s_zc, 4 * g + 4)
                    pe.matmul(bank[2 + q % 2][:, :], Ct[:, cc * P:(cc + 1) * P], Sst[:, d, m, :],
                              start=True, stop=True).then_inc(s_yo, 1)
                    if not last and q in (1, 3):
                        project(g + 1, 3, False, (q // 2,))
                if not last:
                    project(g + 1, 4, False)
                    project(g + 1, 5, False)
                pe.wait_ge(s_yn, 4 * g + 4)
                for f in range(4):
                    for cc in range(LCH):
                        mm = pe.transpose(bank[4 + f][:, cc * P:(cc + 1) * P], yt[:, cc, f * P:(f + 1) * P], ident[:, :])
                    mm.then_inc(s_yt, 1)

            for j in range(2, 6):
                project(0, j, True)
            with pe.Fori(0, G - 1) as g:
                body(g, False)
            body(G - 1, True)

        def ssd_vector(dve, own):
            R = slice(0, 64)
            dve.wait_ge(s_dtt, DT_PROJECTED)
            dve.wait_ge(s_vec, 48)
            own.mark(dve.tensor_scalar(dtx[R, 0:LAT], bank[0][R, :], vec64[:, 0:1], None, ALU.add))
            own.link(dve.tensor_scalar(dtx[R, LAT:T], bank[1][R, 0:CTX], vec64[:, 0:1], None, ALU.add))
            dve.scalar_tensor_tensor(dtu[R, :], dtx[R, :], -1.0, dtx[R, :], ALU.mult, ALU.max).then_inc(s_dtv, 1)
            dve.wait_ge(s_dta, DT_EXP)
            dve.tensor_scalar(dtv[R, :], dtu[R, :], 1.0, None, ALU.add).then_inc(s_dtv, 1)
            dve.wait_ge(s_dta, DT_LOG)
            own.link(dve.tensor_scalar(dtT[R, :], dtv[R, :], 1.0, None, ALU.is_equal))
            own.mark(dve.scalar_tensor_tensor(dtv[R, :], dtv[R, :], -1.0, dtT[R, :], ALU.add, ALU.add))
            own.link(dve.tensor_tensor(acsT[R, :], acsT[R, :], dtT[R, :], ALU.add))
            own.link(dve.reciprocal(dtv[R, :], dtv[R, :]))
            own.link(dve.tensor_tensor(acsT[R, :], acsT[R, :], dtv[R, :], ALU.mult))
            own.link(dve.tensor_tensor(acsT[R, :], acsT[R, :], dtu[R, :], ALU.mult))
            own.link(dve.scalar_tensor_tensor(dtT[R, :], dtx[R, :], 0.0, acsT[R, :], ALU.max, ALU.add))
            dve.wait_ge(s_dta, A_EXP)
            own.link(dve.tensor_scalar(dtu[R, :], dtT[R, :], vec64[:, 2:3], -1.0, ALU.mult, ALU.mult))
            own.link(dve.tensor_tensor_scan(acsT[R, :], chunk_on[R, :], dtu[R, :], 0.0, ALU.mult, ALU.add))
            ends = acsT[R, :].rearrange("p (c t) -> p c t", t=P)[:, :, P - 1:P]
            own.link(dve.tensor_copy(vec64e[:, :], ends.rearrange("p c t -> p (c t)")))
            Bk = slice(32, 64)
            own.link(dve.tensor_tensor(dtu[Bk, :], dtu[Bk, :], acsT[Bk, :], ALU.subtract))
            dve.tensor_tensor(acsT[Bk, :].rearrange("p (c t) -> p c t", t=P), dtu[Bk, :].rearrange("p (c t) -> p c t", t=P),
                              vec64e[Bk, :].unsqueeze(2).broadcast_to([32, NCH, P]), ALU.add).then_inc(s_dtv, 1)
            dve.wait_ge(s_const, 5)
            dve.tensor_tensor(dtx[R, 0:384].rearrange("p (h c) -> p h c", c=NCH),
                              ident[R, 0:64].unsqueeze(2).broadcast_to([64, 64, NCH]),
                              vec64e[:, :].unsqueeze(1).broadcast_to([64, 64, NCH]), ALU.mult).then_inc(s_dtv, 1)
            dve.wait_ge(s_dta, DECAY_EXPS - 1)
            dve.tensor_tensor(dexp[:, :, :], bank[6][:, 0:384].rearrange("p (h c) -> p c h", c=NCH), acs_tok[:, :, :],
                              ALU.subtract).then_inc(s_dtv, 1)
            dve.wait_ge(s_dta, DECAY_EXPS)
            own.mark(dve.tensor_tensor(dexp[:, :, :], dexp[:, :, :], dt_tok[:, :, :], ALU.mult))
            dve.tensor_tensor(dsum[:, :], dskb[:, 0, :], dskb[:, 1, :], ALU.add).then_inc(s_dtv, 1)

            def columns(g):
                own.mark(dve.tensor_copy(cwg[:, :, 0:4], cols2[:, :, bass.ds(g * 4, 4)]))
                own.mark(dve.tensor_copy(cwg[:, :, 4:5], cols2[:, :, bass.ds(g + 16, 1)]))
                dve.tensor_copy(cwg[:, :, 5:6], cols2[:, :, bass.ds(g + 20, 1)]).then_inc(s_cwg, 1)
                own.wait()
                dve.wait_ge(s_cwg, g + 1)

            def convolve(g, j, first):
                dve.wait_ge(s_xc, 6 * g + j + 1)
                v, segs = tile_of(j), segments(j, first)
                for o, n, ps in segs:
                    own.mark(dve.scalar_tensor_tensor(v[:, o + 1:o + n], ps[:, 0:n - 1], cwg[:, 0, j:j + 1],
                                                      v[:, o + 1:o + n], ALU.mult, ALU.add))
                own.wait()
                for o, n, ps in segs:
                    ins = dve.scalar_tensor_tensor(v[:, o:o + n - 1], ps[:, 1:n], cwg[:, 2, j:j + 1],
                                                   v[:, o:o + n - 1], ALU.mult, ALU.add)
                ins.then_inc(s_cv, 1)

            def body(g, last):
                dve.wait_ge(s_ys, START + 4 * g)
                own.mark(dve.tensor_copy(gsg[:, :], cols1[:, bass.ds(R_GSSM + g * 4, 4)]))
                for d in range(2):
                    own.mark(dve.tensor_copy(acol[:, :, d, :], acs_tok[:, 0:LCH, bass.ds(g * HG + d * HEADS, HG)]))
                own.wait()
                dve.wait_ge(s_xtk, 6 * g + 4)
                for d in range(2):
                    for cc in range(LCH):
                        ins = dve.tensor_tensor(heads(xdt[:, d, cc, :]), heads(xtok[:, cc, :]),
                                                bc64(dt_tok[:, cc, bass.ds(d * HEADS + g * HG, HG)]), ALU.mult)
                ins.then_inc(s_xdt, 1)
                dve.wait_ge(s_cb, g + 1)
                for d, mask in ((0, upper), (1, lower)):
                    ins = dve.tensor_tensor(CBm[:, d, :].rearrange("p (c t) -> p c t", t=P),
                                            bank[2][:, :].rearrange("p (c t) -> p c t", t=P),
                                            mask[:, :].unsqueeze(1).broadcast_to([P, LCH, P]), ALU.mult)
                ins.then_inc(s_cbm, 1)
                dve.wait_ge(s_cbm, g + 1)

                def difference(j):
                    h, d = j // 2, j % 2
                    dve.wait_ge(s_row[h % 2], 64 * g + 16 * (h // 2 + 1))
                    for cc in range(LCH):
                        v = Wh[h % 2][:, d, cc * P:(cc + 1) * P]
                        ins = dve.tensor_scalar(v, v, acol[:, cc, d, h:h + 1], 0.0, ALU.subtract, ALU.min)
                    ins.then_inc(s_dd, 1)

                def weight(j):
                    dve.wait_ge(s_le, 16 * g + j + 1)
                    w = Wh[j // 2 % 2][:, j % 2, :]
                    dve.tensor_tensor(w, w, CBm[:, j % 2, :], ALU.mult).then_inc(s_ww, 1)

                difference(0)
                for j in range(16):
                    if j < 15:
                        difference(j + 1)
                    weight(j)
                    if j < 10:
                        step, d = j // 2, j % 2
                        dve.wait_ge(s_kv, START + 10 * g + j + 1)
                        new = 1 if step == 0 else step - 1
                        if step == 0:
                            dve.wait_ge(s_yo, START + 8 * g)
                            dve.tensor_copy(Sst[:, d, new, :], bank[2][:, :]).then_inc(s_kvu, 1)
                        else:
                            old = 1 if step == 1 else step - 2
                            dve.wait_ge(s_kvu, 10 * g + j - 1)
                            own.link(dve.tensor_tensor(heads(stmp), heads(Sst[:, d, old, :]),
                                                       cdec[:, bass.ds(d * HEADS + g * HG, HG), ORDER[d][step]:ORDER[d][step] + 1].broadcast_to([P, HG, HD]),
                                                       ALU.mult))
                            dve.tensor_tensor(Sst[:, d, new, :], stmp, bank[2][:, :], ALU.add).then_inc(s_kvu, 1)
                    if not last and j == 8:
                        dve.wait_ge(s_xsil, 6 * g + 6)
                        columns(g + 1)
                    if not last and j in (9, 11, 13):
                        convolve(g + 1, (j - 9) // 2, False)
                dve.wait_ge(s_yi, g + 1)
                for q in range(8):
                    m, d = q // 2, q % 2
                    cc = m if d == 0 else LCH - 1 - m
                    dve.wait_ge(s_yo, START + 8 * g + q + 1)
                    if q < 2:
                        dve.wait_ge(s_yd, START + 16 * g + 14)
                    dve.tensor_tensor(heads(Wh[0][:, q % 2, :]), heads(bank[2 + q % 2][:, :]),
                                      bc64(eacs[:, cc, bass.ds(d * HEADS + g * HG, HG)]), ALU.mult).then_inc(s_you, 1)
                    dve.wait_ge(s_you, START + 8 * g + q + 1)
                    own.link(dve.tensor_tensor(yt[:, cc, :], yt[:, cc, :], Wh[0][:, q % 2, :], ALU.add))
                    if not last and q == 4:
                        convolve(g + 1, 3, False)
                dve.wait_ge(s_yd, START + 16 * g + 16)
                dve.wait_ge(s_zs, g + 1)
                for cc in range(LCH):
                    own.link(dve.tensor_tensor(yt[:, cc, :], yt[:, cc, :], bank[4 + cc][:, :], ALU.add))
                    dve.tensor_tensor(yt[:, cc, :], yt[:, cc, :], zs[:, cc, :], ALU.mult).then_inc(s_yz, 1)
                dve.wait_ge(s_ysq, g + 1)
                for cc in range(LCH):
                    dve.tensor_scalar(yt[:, cc, :], yt[:, cc, :], rst[:, cc:cc + 1], None, ALU.mult).then_inc(s_yn, 1)
                if not last:
                    convolve(g + 1, 4, False)
                    convolve(g + 1, 5, False)

            columns(0)
            for j in range(6):
                convolve(0, j, True)
            with dve.Fori(0, G - 1) as g:
                own.enter(g, 36)
                body(g, False)
                own.leave(G - 1)
            body(G - 1, True)

        at[0] = after_long
        wh = [take(KT, P) for _ in range(5)]
        pf = [take(T) for _ in range(2)]
        pq, pog, pV = take(LAT), take(LAT), take(T)
        lf = [take(T) for _ in range(2)]
        kh = [take(T) for _ in range(2)]
        bh = [take(T) for _ in range(2)]
        qh, ogh, Vh = take(LAT), take(LAT), take(NCH, P)
        KD = [take(T) for _ in range(2)]
        KDt = take(2, 5, P)
        QE = [v[:, 0:LAT] for v in lf]
        Eb = [take(2, LAT) for _ in range(2)]
        Wl = [take(2, LAT) for _ in range(2)]
        att = take(LAT)
        Sg = take(2, LCH, P)
        sqb, rsd = take(LAT), take(LAT)
        sog = take(LAT)
        tot = take(2, NCH)
        etot = take(2, NCH)
        lev = take(len(LEVELS), P)
        lb, oml, lbt = take(16), take(16), take(32)
        lbh, omlh, ghg = take(2), take(2), take(1)
        NL = len(LEVELS)
        OFFS = [OFF_F, OFF_F + D, OFF_Q, OFF_OG, OFF_I]
        UW = [0, 0, 1, 1, 2, 3, 4, 4]
        s_wh = [sem(f"head_weights_loaded{i}") for i in range(5)]
        s_lev = sem("level_masks_set")
        s_lbe = sem("bound_exps_ready")
        s_lbd = sem("bound_differences_ready")
        s_lbh = sem("head_bounds_ready")
        s_pu = sem("unit_projected")
        s_pev = sem("unit_copied")
        s_sg = sem("sigmoids_ready")
        s_vc = sem("v_ready")
        s_ln = sem("log_gate_ready")
        s_q = sem("q_og_ready")
        s_b = sem("gate_sums_ready")
        s_kdd = sem("end_differences_ready")
        s_kde = sem("end_exps_ready")
        s_kd = sem("decayed_keys_ready")
        s_kdT = sem("decayed_keys_transposed")
        s_kdc = sem("decayed_keys_copied")
        s_kvH = sem("head_chunk_states_ready")
        s_chain = sem("head_states_ready")
        s_qee = sem("q_exps_ready")
        s_qe = sem("decayed_q_ready")
        s_et = sem("end_decays_ready")
        s_ld = sem("level_differences_ready")
        s_lex = sem("level_exps_ready")
        s_lw = sem("level_operand_ready")
        s_la = sem("level_product_ready")
        s_lp = sem("level_merged")
        s_out = sem("head_output_ready")
        s_sqh = sem("head_squares_ready")
        s_sum = sem("head_squares_summed")
        s_rsl = sem("head_log_ready")
        s_rsH = sem("head_rstd_ready")
        s_ohn = sem("head_normalised")
        s_ohd = sem("head_done")

        def hg_sync(sp):
            sp.wait_ge(s_yt, START + 16)
            sp.wait_ge(s_ysq, G)
            sp.wait_ge(s_yn, 16)

            def load(h, i):
                sp.dma_start(wh[i], w_in_t[:, :, bass.ds(OFFS[i] + h * P, P)]).then_inc(s_wh[i], 16)

            for i in range(5):
                load(0, i)
            with sp.Fori(0, HH - 1) as h:
                for i, u in enumerate([2, 4, 5, 6, 8]):
                    sp.wait_ge(s_pu, 8 * h + u)
                    load(h + 1, i)

        def level_view(v, half):
            return v[:, 0:LAT].rearrange("p (n u) -> p n u", u=2 * half)

        def hg_gpsimd(pool, own):
            pool.wait_ge(s_yt, START + 16)
            pool.wait_ge(s_yn, 16)
            own.link(pool.memset(lev.rearrange("p a b -> p (a b)"), 0.0))
            for i in range(2 * NL):
                half, d = LEVELS[i // 2], i % 2
                v = level_view_p(lev[:, i // 2, :], half)[:, :, (1 - d) * half:(2 - d) * half]
                n = P // (2 * half)
                o = level_view_p(ones[:, :], half)[:, :, 0:half]
                own.link(pool.affine_select(out=v, in_=o, compare_op=ALU.is_ge, fill=0.0, base=-d * half,
                                            pattern=[[-2 * half, n], [0, half]], channel_multiplier=1))
                pool.affine_select(out=v, in_=v, compare_op=ALU.is_ge, fill=0.0, base=(1 + d) * half - 1,
                                   pattern=[[2 * half, n], [0, half]], channel_multiplier=-1).then_inc(s_lev, 1)

            def body(h):
                def end_differences(d):
                    pool.wait_ge(s_b, START + 2 * h + d + 1)
                    pool.wait_ge(s_kdT, START + h)
                    pool.tensor_tensor(KD[d].rearrange("p (c t) -> p c t", t=P),
                                       tot[:, d, :].unsqueeze(2).broadcast_to([P, NCH, P]),
                                       bh[d].rearrange("p (c t) -> p c t", t=P), ALU.subtract).then_inc(s_kdd, 1)

                end_differences(0)
                pool.wait_ge(s_b, START + 2 * h + 2)
                for i in range(NL):
                    if i == 1:
                        end_differences(1)
                    if i == 2:
                        pool.wait_ge(s_pev, START + 8 * h + 8)
                        pool.wait_ge(s_out, START + h)
                    if i == 3:
                        pool.tensor_copy(Vh.rearrange("p a b -> p (a b)"), pV).then_inc(s_vc, 1)
                    half = LEVELS[i]
                    if i >= 2:
                        pool.wait_ge(s_lw, START + NL * h + i - 1)
                    else:
                        pool.wait_ge(s_lw, START + NL * h)
                    ek, eq = [level_view(Eb[i % 2][:, side, :], half) for side in range(2)]
                    n = LAT // (2 * half)
                    for d in range(2):
                        bv = level_view(bh[d], half)
                        mid = bv[:, :, half - 1 + d:half + d].broadcast_to([P, n, half])
                        first, second = (eq, ek) if d else (ek, eq)
                        one, two = (bv[:, :, 0:half], mid) if d else (mid, bv[:, :, 0:half])
                        pool.tensor_tensor(first[:, :, 0:half], one, two, ALU.subtract)
                        one, two = (mid, bv[:, :, half:]) if d else (bv[:, :, half:], mid)
                        ins = pool.tensor_tensor(second[:, :, half:], one, two, ALU.subtract)
                    ins.then_inc(s_ld, 1)

            with pool.Fori(0, HH - 1) as h:
                body(h)
            body(HH - 1)

        def level_view_p(v, half):
            return v.rearrange("p (n u) -> p n u", u=2 * half)

        def hg_scalar(act):
            act.wait_ge(s_lbd, 1)
            act.activation(lbt, lbt, ACT.Exp).then_inc(s_lbe, 1)

            def unit_copy(h, u):
                act.wait_ge(s_pu, 8 * h + u + 1)
                dst, n = [(pf[0][:, 0:LAT], LAT), (pf[0][:, LAT:T], CTX), (pf[1][:, 0:LAT], LAT), (pf[1][:, LAT:T], CTX),
                          (pq, LAT), (pog, LAT), (pV[:, 0:LAT], LAT), (pV[:, LAT:T], CTX)][u]
                act.copy(dst, bank[u % 2][:, 0:n]).then_inc(s_pev, 1)

            def start(h):
                act.wait_ge(s_pev, START + 8 * h + 8)
                act.wait_ge(s_out, START + h)
                act.wait_ge(s_lw, START + NL * h)
                act.wait_ge(s_b, START + 2 * h)
                act.wait_ge(s_la, START + (NL + 1) * h)
                for d in range(2):
                    act.activation(lf[d], pf[d], ACT.Sigmoid)
                    act.activation(kh[d], pf[d], ACT.Sigmoid, scale=-1.0).then_inc(s_sg, 1)
                act.activation(qh, pq, ACT.Sigmoid).then_inc(s_sg, 1)
                act.activation(sog, pog, ACT.Sigmoid).then_inc(s_sg, 1)
                act.wait_ge(s_lbh, h + 1)
                act.wait_ge(s_sg, 4 * h + 4)
                for d in range(2):
                    act.activation(lf[d], lf[d], ACT.Ln, scale=omlh[:, d:d + 1], bias=lbh[:, d:d + 1]).then_inc(s_ln, 1)

            def end_exps(h, d):
                act.wait_ge(s_kdd, 2 * h + d + 1)
                act.activation(KD[d], KD[d], ACT.Exp).then_inc(s_kde, 1)

            def body(h, last):
                if not last:
                    unit_copy(h + 1, 0)
                    unit_copy(h + 1, 1)
                end_exps(h, 0)
                for i in range(NL):
                    if i == 1:
                        if not last:
                            unit_copy(h + 1, 2)
                        end_exps(h, 1)
                        for d in range(2):
                            act.activation(QE[d], bh[d][:, 0:LAT], ACT.Exp).then_inc(s_qee, 1)
                        act.wait_ge(s_chain, START + h)
                        act.activation(etot.rearrange("p a b -> p (a b)"), tot.rearrange("p a b -> p (a b)"), ACT.Exp).then_inc(s_et, 1)
                    act.wait_ge(s_ld, START + NL * h + i + 1)
                    ev = Eb[i % 2].rearrange("p a b -> p (a b)")
                    act.activation(ev, ev, ACT.Exp).then_inc(s_lex, 1)
                    if i == 1:
                        act.wait_ge(s_kdT, START + h + 1)
                        act.wait_ge(s_kvH, START + h)
                        act.copy(KDt[:, 0, 0:4, :].rearrange("p a b -> p (a b)"), bank[7][:, :])
                        act.copy(KDt[:, 1, 0:4, :].rearrange("p a b -> p (a b)"), bank[6][:, :])
                        act.copy(KDt[:, :, 4, :], bank[5][:, 256:512].rearrange("p (a b) -> p a b", a=2)).then_inc(s_kdc, 1)
                    if not last and i in (2, 4, 6):
                        act.wait_ge(s_q, h + 1)
                        unit_copy(h + 1, 2 + i // 2)
                if not last:
                    act.wait_ge(s_vc, h + 1)
                    unit_copy(h + 1, 6)
                act.wait_ge(s_out, START + h + 1)
                act.wait_ge(s_ohd, START + h)
                act.activation(sqb, bank[6][:, :], ACT.Square).then_inc(s_sqh, 1)
                if not last:
                    unit_copy(h + 1, 7)
                    start(h + 1)
                act.wait_ge(s_sum, h + 1)
                act.wait_ge(s_ohn, START + h)
                act.activation(rsd, bank[7][:, :], ACT.Ln, scale=1.0 / P, bias=epsb[:, 0:1]).then_inc(s_rsl, 1)
                act.wait_ge(s_rsl, h + 1)
                act.activation(rsd, rsd, ACT.Exp, scale=-0.5).then_inc(s_rsH, 1)

            for u in range(8):
                unit_copy(0, u)
            start(0)
            with act.Fori(0, HH - 1) as h:
                body(h, False)
            body(HH - 1, True)

        def merge_gate(pe, b, r):
            for k in range(KT):
                mm = pe.matmul(bank[4 * r + b][:, :], wm[r][:, 8 * b + k, :], hT[:, k, 0:LAT], start=(k == 0), stop=(k == KT - 1))
            if b:
                mm.then_inc(s_gmp, 1)

        def hg_tensor(pe):
            pe.wait_ge(s_ys, START + 16)
            pe.wait_ge(s_hp, KT)

            def unit(h, u):
                w, b = wh[UW[u]], bank[u % 2]
                pe.wait_ge(s_wh[UW[u]], 16 * h + 16)
                if u >= 2:
                    pe.wait_ge(s_pev, START + 8 * h + u - 1)
                else:
                    pe.wait_ge(s_pev, START + 8 * h)
                if u in (1, 3):
                    for k in range(KT):
                        mm = pe.matmul(b[:, 0:CTX], w[:, k, :], hT[:, k, LAT:T], start=(k == 0), stop=(k == KT - 1))
                elif u < 6:
                    src = hT if u == 5 else hTp
                    for k in range(KT):
                        mm = pe.matmul(b[:, :], w[:, k, :], src[:, k, 0:LAT], start=(k == 0), stop=(k == KT - 1))
                else:
                    for i in range(LCH if u == 6 else 2):
                        for k in range(KT):
                            lhs = hTp[:, k, i * P:(i + 1) * P] if u == 6 else hT[:, k, LAT + i * P:LAT + (i + 1) * P]
                            mm = pe.matmul(b[:, i * P:(i + 1) * P], lhs, w[:, k, :], start=(k == 0), stop=(k == KT - 1))
                mm.then_inc(s_pu, 1)

            for u in range(8):
                unit(0, u)

            def body(h, last):
                if not last:
                    for u in range(4):
                        unit(h + 1, u)
                pe.wait_ge(s_q, h + 1)
                pe.wait_ge(s_lp, START + (NL + 1) * h)
                for cc in range(LCH):
                    cs = slice(cc * P, (cc + 1) * P)
                    for d in range(2):
                        mm = pe.matmul(bank[2][:, cs], kh[d][:, cs], qh[:, cs], start=(d == 0), stop=(d == 1))
                mm.then_inc(s_la, 1)
                for i in range(NL):
                    if i == 1:
                        pe.wait_ge(s_kd, 2 * h + 2)
                        pe.wait_ge(s_ohd, START + h)
                        pe.wait_ge(s_chain, START + h)
                        for d in range(2):
                            for k in range(5):
                                ch = ORDER[d][k]
                                dst = bank[7 - d][:, k * P:(k + 1) * P] if k < 4 else bank[5][:, 256 + d * P:384 + d * P]
                                mm = pe.transpose(dst, KD[d][:, ch * P:(ch + 1) * P], ident[:, :])
                        mm.then_inc(s_kdT, 1)
                    pe.wait_ge(s_lw, START + NL * h + i + 1)
                    pe.wait_ge(s_lp, START + (NL + 1) * h + i)
                    w = Wl[i % 2]
                    for cc in range(LCH):
                        mm = pe.matmul(bank[3 - i % 2][:, cc * P:(cc + 1) * P], w[:, 0, cc * P:(cc + 1) * P], w[:, 1, cc * P:(cc + 1) * P],
                                       start=True, stop=True)
                    mm.then_inc(s_la, 1)
                    if i == 3:
                        pe.wait_ge(s_kdc, h + 1)
                        pe.wait_ge(s_vc, h + 1)
                        for d in range(2):
                            for k in range(5):
                                dst = bank[(4, 7)[d]][:, k * P:(k + 1) * P] if k < 4 else bank[5][:, d * P:(d + 1) * P]
                                mm = pe.matmul(dst, KDt[:, d, k, :], Vh[:, ORDER[d][k], :], start=True, stop=True)
                        mm.then_inc(s_kvH, 1)
                    if not last and i in (2, 4):
                        unit(h + 1, 3 + i // 2)
                    if last and i in (0, 2):
                        if i == 0:
                            pe.wait_ge(s_pev, START + 8 * HH)
                        pe.wait_ge(s_wm[0], 64)
                        merge_gate(pe, i // 2, 0)
                if not last:
                    unit(h + 1, 6)
                pe.wait_ge(s_lp, START + (NL + 1) * (h + 1))
                pe.wait_ge(s_chain, START + h + 1)
                pe.wait_ge(s_qe, 2 * h + 2)
                for cc in range(LCH):
                    o, cs = bank[6][:, cc * P:(cc + 1) * P], slice(cc * P, (cc + 1) * P)
                    pe.matmul(o, Vh[:, cc, :], att[:, cs], start=True, stop=False)
                    pe.matmul(o, Sg[:, 0, cc, :], QE[0][:, cs], start=False, stop=False)
                    mm = pe.matmul(o, Sg[:, 1, LCH - 1 - cc, :], QE[1][:, cs], start=False, stop=True)
                mm.then_inc(s_out, 1)
                if not last:
                    unit(h + 1, 7)
                pe.wait_ge(s_sqh, h + 1)
                pe.matmul(bank[7][:, :], ones[:, :], sqb, start=True, stop=True).then_inc(s_sum, 1)

            with pe.Fori(0, HH - 1) as h:
                body(h, False)
            body(HH - 1, True)

        def hg_vector(dve, own):
            a0, a1 = cols1[:, R_LB:R_LB + 16], cols1[:, R_LB + 16:R_LB + 32]
            dve.wait_ge(s_yt, START + 16)
            dve.wait_ge(s_ysq, G)
            own.link(dve.tensor_tensor(lb, a0, a1, ALU.max))
            own.mark(dve.tensor_tensor(lbt[:, 0:16], a0, lb, ALU.subtract))
            dve.tensor_tensor(lbt[:, 16:32], a1, lb, ALU.subtract).then_inc(s_lbd, 1)
            dve.wait_ge(s_lbe, 1)
            own.wait()
            own.link(dve.tensor_tensor(oml, lbt[:, 0:16], lbt[:, 16:32], ALU.add))
            own.link(dve.reciprocal(oml, oml))
            own.link(dve.tensor_tensor(lb, lbt[:, 0:16], oml, ALU.mult))
            own.mark(dve.tensor_scalar(lb, lb, F_MIN, None, ALU.max))
            own.mark(dve.tensor_tensor(oml, lbt[:, 16:32], oml, ALU.mult))
            own.link(dve.tensor_copy(ghg, cols1[:, R_GHG:R_GHG + 1]))
            dve.wait_ge(s_lev, 2 * NL)

            def start(h):
                dve.wait_ge(s_ln, START + 2 * h)
                own.mark(dve.tensor_copy(lbh, lb.rearrange("p (d h) -> p h d", d=2)[:, bass.ds(h, 1), :].rearrange("p a b -> p (a b)")))
                dve.tensor_copy(omlh, oml.rearrange("p (d h) -> p h d", d=2)[:, bass.ds(h, 1), :].rearrange("p a b -> p (a b)")).then_inc(s_lbh, 1)
                dve.wait_ge(s_lbh, h + 1)
                for d in range(2):
                    dve.wait_ge(s_sg, 4 * h + d + 1)
                    own.mark(dve.tensor_scalar(kh[d], kh[d], omlh[:, d:d + 1], None, ALU.mult))
                dve.wait_ge(s_sg, 4 * h + 3)
                dve.tensor_tensor(qh, pq, qh, ALU.mult).then_inc(s_q, 1)

            def output_gate(h):
                dve.wait_ge(s_sg, 4 * h + 4)
                dve.wait_ge(s_ohd, START + h)
                own.mark(dve.tensor_tensor(ogh, pog, sog, ALU.mult))

            def finish(h):
                dve.wait_ge(s_rsH, h + 1)
                dve.scalar_tensor_tensor(sqb, bank[6][:, :], ghg, rsd, ALU.mult, ALU.mult).then_inc(s_ohn, 1)
                dve.wait_ge(s_ohn, START + h + 1)
                own.wait()
                dve.tensor_tensor(ohT[:, bass.ds(h, 1), :].rearrange("p a (r w) -> p (a r) w", w=GRID_W),
                                  sqb.rearrange("p (w r) -> p r w", r=ROWS),
                                  ogh.rearrange("p (r w) -> p r w", w=GRID_W), ALU.mult).then_inc(s_ohd, 1)

            def sums(h):
                dve.wait_ge(s_ld, START + NL * h)
                dve.wait_ge(s_qee, START + 2 * h)
                dve.wait_ge(s_et, START + h)
                for d in range(2):
                    dve.wait_ge(s_ln, START + 2 * h + d + 1)
                    own.link(dve.tensor_tensor_scan(bh[d], chunk_on[:, :], lf[d], 0.0, ALU.mult, ALU.add))
                    c3 = bh[d].rearrange("p (c t) -> p c t", t=P)
                    if d == 0:
                        dve.tensor_copy(tot[:, d, :], c3[:, :, P - 1]).then_inc(s_b, 1)
                    else:
                        own.mark(dve.tensor_copy(tot[:, d, :], c3[:, :, P - 1]))
                        own.link(dve.tensor_tensor(lf[d], lf[d], bh[d], ALU.subtract))
                        dve.tensor_tensor(c3, lf[d].rearrange("p (c t) -> p c t", t=P),
                                          tot[:, d, :].unsqueeze(2).broadcast_to([P, NCH, P]), ALU.add).then_inc(s_b, 1)
            def body(h, last):
                def end_keys(d):
                    dve.wait_ge(s_kde, 2 * h + d + 1)
                    dve.tensor_tensor(KD[d], KD[d], kh[d], ALU.mult).then_inc(s_kd, 1)

                dve.wait_ge(s_q, h + 1)
                end_keys(0)
                dve.wait_ge(s_out, START + h)
                a3 = att.rearrange("p (c t) -> p c t", t=P)

                def merge(i):
                    m = ident[:, :] if i == 0 else lev[:, i - 1, :]
                    dve.copy_predicated(a3, m.bitcast(U32).unsqueeze(1).broadcast_to([P, LCH, P]),
                                        bank[2 + i % 2][:, :].rearrange("p (c t) -> p c t", t=P)).then_inc(s_lp, 1)

                for i in range(NL):
                    if i == 1:
                        end_keys(1)
                        for d in range(2):
                            dve.wait_ge(s_qee, START + 2 * h + d + 1)
                            dve.tensor_tensor(QE[d], QE[d], qh, ALU.mult).then_inc(s_qe, 1)
                    half = LEVELS[i]
                    dve.wait_ge(s_lex, NL * h + i + 1)
                    if i:
                        dve.wait_ge(s_la, START + (NL + 1) * h + i)
                    if i >= 2:
                        dve.wait_ge(s_lp, START + (NL + 1) * h + i - 1)
                    ev, wv = level_view(Eb[i % 2][:, 0, :], half), level_view(Wl[i % 2][:, 0, :], half)
                    for d in range(2):
                        s = slice(d * half, (d + 1) * half)
                        own.mark(dve.tensor_tensor(wv[:, :, s], ev[:, :, s], level_view(kh[d], half)[:, :, s], ALU.mult))
                    dve.tensor_tensor(Wl[i % 2][:, 1, :], Eb[i % 2][:, 1, :], qh, ALU.mult).then_inc(s_lw, 1)
                    if i:
                        merge(i - 1)
                dve.wait_ge(s_kvH, START + h + 1)
                dve.wait_ge(s_et, START + h + 1)
                for k in range(5):
                    if k < 2:
                        dve.wait_ge(s_la, START + (NL + 1) * h + NL + k)
                        dve.wait_ge(s_lp, START + (NL + 1) * h + NL + k - 1)
                    for d in range(2):
                        kv = bank[(4, 7)[d]][:, k * P:(k + 1) * P] if k < 4 else bank[5][:, d * P:(d + 1) * P]
                        if k == 0:
                            ins = dve.tensor_copy(Sg[:, d, 1, :], kv)
                        else:
                            ch, old = ORDER[d][k], 1 if k == 1 else k - 2
                            ins = dve.scalar_tensor_tensor(Sg[:, d, k - 1, :], Sg[:, d, old, :], etot[:, d, ch:ch + 1], kv,
                                                           ALU.mult, ALU.add)
                        if (k, d) == (4, 1):
                            ins.then_inc(s_chain, 1)
                        else:
                            own.mark(ins)
                    if k < 2:
                        merge(NL - 1 + k)
                    own.wait()
                if not last:
                    start(h + 1)
                    sums(h + 1)
                finish(h)
                if not last:
                    output_gate(h + 1)

            start(0)
            sums(0)
            output_gate(0)
            with dve.Fori(0, HH - 1) as h:
                own.enter(h, 31)
                body(h, False)
                own.leave(HH - 1)
            body(HH - 1, True)

        at[0] = after_long
        wm = [take(40, P) for _ in range(2)]
        mixT = take(KT, LAT)
        wout = take(KT, D)
        sgm = [take(LAT) for _ in range(2)]
        sgh = [take(LAT) for _ in range(2)]
        adac = take(512)
        adaw = take(512)
        wada2 = hTp
        at[0] = after_long
        rowv = take(4, D)
        rowg = take(3, D)
        tmpd = [take(D) for _ in range(2)]
        hflat = hT[:, :, :].rearrange("p a b -> p (a b)")
        yflat = ysT[:, :, :].rearrange("p a b -> p (a b)")
        xres = hflat[:, 0:LCH * D].rearrange("p (c d) -> p c d", d=D)
        xl = yflat[:, 0:LCH * D].rearrange("p (c d) -> p c d", d=D)
        h2 = yflat[:, LCH * D:2 * LCH * D].rearrange("p (c d) -> p c d", d=D)
        h2T = mixT
        wr = hflat[:, 4096:4096 + KT * 36].rearrange("p (k e) -> p k e", e=36)
        brow = hflat[:, 4400:4436]
        s_wm = [sem(f"merge_weights_loaded{r}") for r in range(2)]
        s_wout = sem("w_out_loaded")
        s_gmp = sem("gates_projected")
        s_brp = sem("branches_projected")
        s_gms = sem("gates_ready")
        s_mx = sem("mixed_tile_ready")
        s_rowv = sem("rows_broadcast")
        s_xres = sem("x_reloaded")
        s_wr = sem("router_loaded")
        s_mo = sem("mix_chunk_projected")
        s_mr = sem("mix_rstd_ready")
        s_xl = sem("residual_ready")
        s_xl2 = sem("residual_rstd_ready")
        s_h2 = sem("h2_ready")
        s_h2t = sem("h2_transposed")
        s_h2T = sem("h2_columns_ready")
        s_h2st = sem("h2_stored")
        s_aw = sem("modulation_weights_loaded")
        s_ab = sem("modulation_bias_loaded")
        s_ac = sem("modulation_terms_ready")
        s_as = sem("modulation_terms_summed")
        s_ar = sem("modulation_chunk_ready")
        wbs_t = w_branch_ssm[0].rearrange("(k p) n -> p k n", p=P)
        wbh_t = w_branch_hg[0].rearrange("(k p) n -> p k n", p=P)

        h2_dram = nc.dram_tensor("h2_dram", (LAT, D), F32, kind="Internal").ap()
        y_dram = nc.dram_tensor("y_dram", (2 * LAT, D), F32, kind="Internal").ap()

        def merge_sync(sp):

            def weights(j, r):
                for o, n, src in ((0, 8, w_in_t[:, :, bass.ds(OFF_GM + j * P, P)]),
                                  (8, 8, w_in_t[:, :, bass.ds(OFF_GH + j * P, P)]),
                                  (16, 16, wbs_t[:, :, bass.ds(j * P, P)]),
                                  (32, 8, wbh_t[:, :, bass.ds(j * P, P)])):
                    sp.dma_start(wm[r][:, o:o + n, :], src).then_inc(s_wm[r], 16)

            def load(j, r, warm):
                if warm:
                    sp.wait_ge(s_brp, j - 1)
                    weights(j, r)
                if warm or r:
                    sp.wait_ge(s_ac, j)
                sp.dma_start(wada2, w_ada_t[:, :, bass.ds(2 * D + j * 512, 512)]).then_inc(s_aw, 16)
                if warm or r:
                    sp.wait_ge(s_modst, 16 * j)
                sp.dma_start(adaw[0:1, :], b_ada[:, bass.ds(2 * D + j * 512, 512)]).then_inc(s_ab, 16)

            sp.wait_ge(s_pu, 8 * HH)
            weights(0, 0)
            sp.wait_ge(s_ohd, START + HH)
            weights(1, 1)
            load(0, 0, False)
            sp.dma_start(wout, w_out[0].rearrange("(k p) n -> p k n", p=P)).then_inc(s_wout, 16)
            load(1, 1, False)
            with sp.Fori(1, KT // 2) as t:
                for r in range(2):
                    load(t * 2 + r, r, True)
            sp.wait_ge(s_brp, KT)
            sp.wait_ge(s_modst, 16 * 8)
            for i in range(4):
                src = modrows[2 * i:2 * i + 2, :].rearrange("(u r) p -> u (r p)", u=1)
                sp.dma_start(rowv[:, i, :], src.broadcast_to([P, D])).then_inc(s_rowv, 16)
            for i, v in enumerate((g_post_mix, g_pre_ffn, g_post_ffn)):
                sp.dma_start(rowg[:, i, :], v.broadcast_to([P, D])).then_inc(s_rowv, 16)
            sp.dma_start(xres, x[0].rearrange("(i p) d -> p i d", p=P)).then_inc(s_xres, 16)
            sp.dma_start(wr[:, :, 0:4], w_group_router[0].rearrange("(k p) g -> p k g", p=P)).then_inc(s_wr, 16)
            for g in range(EG):
                sp.dma_start(wr[:, :, 4 + 8 * g:12 + 8 * g], w_expert_router[0, g].rearrange("(k p) e -> p k e", p=P)).then_inc(s_wr, 16)
            sp.dma_start(brow[:, 0:4], b_group_router.broadcast_to([P, EG])).then_inc(s_wr, 16)
            sp.dma_start(brow[:, 4:36], b_expert_router.rearrange("u g e -> u (g e)").broadcast_to([P, E])).then_inc(s_wr, 16)
            for cc in range(LCH):
                sp.wait_ge(s_h2, cc + 1)
                sp.dma_start(h2_dram[cc * P:(cc + 1) * P, :], h2[:, cc, :]).then_inc(s_h2st, 16)

        def merge_tensor(pe):
            def pair(t, warm):
                for r in range(2):
                    j = t * 2 + r
                    pe.wait_ge(s_wm[r], t * 64 + 64)
                    if warm:
                        pe.wait_ge(s_mx, j - 1)
                        pe.wait_ge(s_ar, j - 1)
                    if warm or r:
                        merge_gate(pe, 0, r)
                        merge_gate(pe, 1, r)
                    else:
                        pe.wait_ge(s_lp, START + (NL + 1) * HH)
                    for k in range(16):
                        pe.matmul(bank[4 * r + 2][:, :], wm[r][:, 16 + k, :], ysT[:, k, :], start=(k == 0), stop=(k == 15))
                    if not warm and not r:
                        pe.wait_ge(s_ohd, START + HH)
                    for k in range(KT):
                        mm = pe.matmul(bank[4 * r + 3][:, :], wm[r][:, 32 + k, :], ohT[:, k, :], start=(k == 0), stop=(k == KT - 1))
                    mm.then_inc(s_brp, 1)
                    pe.wait_ge(s_gms, j + 1)
                    pe.wait_ge(s_ac, j + 1)
                    pe.matmul(bank[4 * r][0:1, :], ones[:, 0:1], adac, start=True, stop=True).then_inc(s_as, 1)

            pair(0, False)
            with pe.Fori(1, KT // 2) as t:
                pair(t, True)
            pe.wait_ge(s_wout, 16)
            pe.wait_ge(s_mx, KT)
            pe.wait_ge(s_ar, KT)
            for cc in range(LCH):
                for hf in range(2):
                    for k in range(KT):
                        mm = pe.matmul(bank[2 * cc + hf][:, :], mixT[:, k, cc * P:(cc + 1) * P], wout[:, k, hf * 512:(hf + 1) * 512],
                                       start=(k == 0), stop=(k == KT - 1))
                mm.then_inc(s_mo, 1)
            pe.wait_ge(s_h2, LCH)
            for k in range(KT):
                if k >= 2:
                    pe.wait_ge(s_h2T, k - 1)
                for cc in range(LCH):
                    mm = pe.transpose(bank[k % 2][:, cc * P:(cc + 1) * P], h2[:, cc, k * P:(k + 1) * P], ident[:, :])
                mm.then_inc(s_h2t, 1)
            pe.wait_ge(s_h2T, KT)
            pe.wait_ge(s_wr, 16 * 7)
            for cc in range(LCH):
                for k in range(KT):
                    mm = pe.matmul(bank[2][:, cc * 36:(cc + 1) * 36], h2T[:, k, cc * P:(cc + 1) * P], wr[:, k, :],
                                   start=(k == 0), stop=(k == KT - 1))
            mm.then_inc(s_rp, 1)

        def merge_scalar(act, own):
            act.wait_ge(s_ohd, START + HH)

            def pair(t, warm):
                for r in range(2):
                    j = t * 2 + r
                    act.wait_ge(s_gmp, j + 1)
                    if warm:
                        act.wait_ge(s_mx, j - 1)
                    act.activation(sgm[r], bank[4 * r][:, :], ACT.Sigmoid)
                    act.activation(sgh[r], bank[4 * r + 1][:, :], ACT.Sigmoid).then_inc(s_gms, 1)
                    act.wait_ge(s_ar, j + 1)
                    act.dma_start(modrows[bass.ds(j, 1), :], adaw[0:1, :]).then_inc(s_modst, 16)

            pair(0, False)
            with act.Fori(1, KT // 2) as t:
                pair(t, True)
            act.wait_ge(s_mx, KT)
            act.wait_ge(s_brp, KT)
            for cc in range(LCH):
                act.wait_ge(s_mo, cc + 1)
                own.mark(act.activation(hflat[:, 5120:5632], bank[2 * cc][:, :], ACT.Square, accum_out=ssq[:, 0:1]))
                own.link(act.activation(hflat[:, 5632:6144], bank[2 * cc + 1][:, :], ACT.Square, accum_out=ssq[:, 1:2]))
                own.link(act.activation(ssq[:, 2:3], ssq[:, 0:1], ACT.Identity, bias=ssq[:, 1:2]))
                if cc:
                    act.wait_ge(s_xl, cc)
                own.link(act.activation(rst[:, 0:1], ssq[:, 2:3], ACT.Ln, scale=1.0 / D, bias=epsb[:, 0:1]))
                act.activation(rst[:, 0:1], rst[:, 0:1], ACT.Exp, scale=-0.5).then_inc(s_mr, 1)
                act.wait_ge(s_xl, cc + 1)
                if cc:
                    act.wait_ge(s_h2, cc)
                own.link(act.activation(hflat[:, 5120:6144], xl[:, cc, :], ACT.Square, accum_out=ssq[:, 3:4]))
                own.link(act.activation(rst[:, 1:2], ssq[:, 3:4], ACT.Ln, scale=1.0 / D, bias=epsb[:, 0:1]))
                act.activation(rst[:, 1:2], rst[:, 1:2], ACT.Exp, scale=-0.5).then_inc(s_xl2, 1)
            for k in range(KT):
                act.wait_ge(s_h2t, k + 1)
                act.copy(h2T[:, k, :], bank[k % 2][:, :]).then_inc(s_h2T, 1)

        def merge_vector(dve, own):
            def pair(t, warm):
                for r in range(2):
                    j = t * 2 + r
                    dve.wait_ge(s_aw, 16 * j + 16)
                    if warm or r:
                        dve.wait_ge(s_as, j)
                    own.link(dve.tensor_scalar(adac, wada2[:, 0, :], sc_in[:, 0:1], None, ALU.mult))
                    for k in range(1, KT):
                        ins = dve.scalar_tensor_tensor(adac, wada2[:, k, :], sc_in[:, k:k + 1], adac, ALU.mult, ALU.add)
                        if k < KT - 1:
                            own.link(ins)
                    ins.then_inc(s_ac, 1)
                    dve.wait_ge(s_gms, j + 1)
                    dve.wait_ge(s_brp, j + 1)
                    own.mark(dve.tensor_tensor(sgm[r], sgm[r], bank[4 * r + 2][:, :], ALU.mult))
                    own.link(dve.tensor_tensor(sgh[r], sgh[r], bank[4 * r + 3][:, :], ALU.mult))
                    dve.tensor_tensor(mixT[:, bass.ds(j, 1), :].rearrange("p a b -> p (a b)"), sgm[r], sgh[r], ALU.add).then_inc(s_mx, 1)
                    dve.wait_ge(s_as, j + 1)
                    dve.wait_ge(s_ab, 16 * j + 16)
                    dve.tensor_tensor(adaw[0:1, :], adaw[0:1, :], bank[4 * r][0:1, :], ALU.add).then_inc(s_ar, 1)

            pair(0, False)
            with dve.Fori(1, KT // 2) as t:
                own.enter(t - 1, 18)
                pair(t, True)
                own.leave(KT // 2 - 1)
            dve.wait_ge(s_rowv, 16 * 7)
            dve.wait_ge(s_xres, 16)
            own.mark(dve.tensor_tensor(rowv[:, 0, :], rowv[:, 0, :], rowg[:, 0, :], ALU.mult))
            own.mark(dve.scalar_tensor_tensor(rowv[:, 2, :], rowv[:, 2, :], 1.0, rowg[:, 1, :], ALU.add, ALU.mult))
            own.link(dve.tensor_tensor(rowv[:, 3, :], rowv[:, 3, :], rowg[:, 2, :], ALU.mult))
            for cc in range(LCH):
                tm = tmpd[cc % 2]
                dve.wait_ge(s_mr, cc + 1)
                for hf in range(2):
                    s = slice(hf * 512, (hf + 1) * 512)
                    own.mark(dve.scalar_tensor_tensor(tm[:, s], bank[2 * cc + hf][:, :], rst[:, 0:1], rowv[:, 0, s], ALU.mult, ALU.mult))
                own.wait()
                dve.tensor_tensor(xl[:, cc, :], tm, xres[:, cc, :], ALU.add).then_inc(s_xl, 1)
                dve.wait_ge(s_xl2, cc + 1)
                own.link(dve.scalar_tensor_tensor(tm, xl[:, cc, :], rst[:, 1:2], rowv[:, 2, :], ALU.mult, ALU.mult))
                dve.tensor_tensor(h2[:, cc, :], tm, rowv[:, 1, :], ALU.add).then_inc(s_h2, 1)

        NT = 2 * LCH
        NB = BLOCKS + 2
        at[0] = 2 * 3 * 4096
        xg = [take(D) for _ in range(2)]
        xgT = [take(KT, P) for _ in range(2)]
        gu = [take(FF) for _ in range(2)]
        guT = take(FT, P)
        yb = [take(D) for _ in range(2)]
        gidx = take(NB).bitcast(U32)
        sidx = take(NB).bitcast(U32)
        bexp = take(NB).bitcast(I32)
        npair = take(1).bitcast(I32)
        idg = [take(1).bitcast(U32) for _ in range(2)]
        ids = [take(1).bitcast(U32) for _ in range(2)]
        wsel = take(2, LCH)
        pad = take(2)
        row_keep = take(D)
        assert at[0] <= 34100
        at[0] = 0
        it_i = take(P).bitcast(I32)
        pid_i = take(NT).bitcast(I32)
        iof = take(P)
        pidf = take(NT)
        revg = take(EG)
        lg = take(LCH, 36)
        gmx, gsm, pg = take(LCH), take(LCH), take(LCH)
        gex, goh = take(LCH, EG), take(LCH, EG)
        top = take(LCH, 8)
        topi = take(LCH, 8).bitcast(U32)
        ef = take(2, LCH)
        oh = take(NT, E)
        strict = take(P)
        rank = take(NT, E)
        tsum = take(NT, E)
        cnt, nblk, binc, bst = take(E), take(E), take(E), take(E)
        tE = take(NT, E)
        rk, fl, blk, c1 = take(NT), take(NT), take(NT), take(NT)
        soh = take(NT, P)
        boh = take(NT, NB)
        cmpb = take(NB, E)
        bef = take(NB)
        tbl, inv, hi_ = take(NB), take(NB), take(NB)
        assert at[0] <= after_long
        s_iota = sem("index_rows_ready")
        s_wg = [sem(f"gate_up_loaded{r}") for r in range(2)]
        s_wd = [sem(f"down_loaded{r}") for r in range(2)]
        s_xg = [sem(f"rows_gathered{r}") for r in range(2)]
        s_xgt = sem("rows_transposed_for_experts")
        s_xgc = sem("row_columns_ready")
        s_g = sem("gate_projected")
        s_u = sem("up_projected")
        s_sig = sem("gate_activated")
        s_gu = sem("gated_ready")
        s_gut = sem("gated_transposed")
        s_guc = sem("gated_columns_ready")
        s_d = sem("down_projected")
        s_yb = sem("expert_rows_ready")
        s_sc = [sem(f"rows_scattered{r}") for r in range(2)]
        s_idx = sem("index_columns_copied")
        s_z = sem("gather_rows_cleared")
        s_yl = [sem(f"expert_outputs_loaded{cc}") for cc in range(2)]
        s_fa = sem("choices_added")
        s_fs = sem("ffn_squares_ready")
        s_fo = sem("output_chunk_ready")
        s_done = sem("output_stored")

        def route_gpsimd(pool, own):
            pool.wait_ge(s_ac, KT)
            own.mark(pool.iota(it_i, [[1, P]], base=0, channel_multiplier=0))
            own.link(pool.iota(pid_i, [[P, NT]], base=1, channel_multiplier=1))
            own.link(pool.tensor_copy(iof, it_i))
            own.link(pool.tensor_copy(pidf, pid_i))
            pool.tensor_scalar(revg, iof[:, 0:EG], -1.0, float(EG), ALU.mult, ALU.add).then_inc(s_iota, 1)

        def route_scalar(act):
            act.wait_ge(s_rv, GROUP_MAX)
            act.activation(gex.rearrange("p a b -> p (a b)"), gex.rearrange("p a b -> p (a b)"), ACT.Exp).then_inc(s_ra, 1)
            act.wait_ge(s_rv, EXPERT_DIFFS)
            act.activation(ef[:, 1, :], ef[:, 1, :], ACT.Exp).then_inc(s_ra, 1)

        def route_tensor(pe):
            pe.wait_ge(s_rv, CHOICES)
            ohf = oh.rearrange("p a b -> p (a b)")
            pe.matmul(bank[3][:, 0:NT * E], strict, ohf, start=True, stop=True)
            pe.matmul(bank[4][:, 0:NT * E], ones[:, :], ohf, start=True, stop=True).then_inc(s_rp, 1)
            pe.wait_ge(s_rv, SLOT_CHOICES)
            for j in range(NT):
                mm = pe.matmul(bank[5][:, 0:NB], soh[:, j, :], boh[:, j, :], start=(j == 0), stop=(j == NT - 1))
            mm.then_inc(s_rp, 1)

        def route_vector(dve, own):
            L = own.link

            def over(v, n):
                return v.unsqueeze(len(v.shape)).broadcast_to(list(v.shape) + [n])

            dve.wait_ge(s_rp, LOGITS)
            dve.wait_ge(s_iota, 1)
            L(dve.tensor_copy(row_keep, rowv[:, 3, :]))
            L(dve.tensor_tensor(lg, bank[2][:, 0:144].rearrange("p (c e) -> p c e", e=36),
                                brow.unsqueeze(1).broadcast_to([P, LCH, 36]), ALU.add))
            L(dve.tensor_reduce(gmx, lg[:, :, 0:EG], AX.X, ALU.max))
            L(dve.tensor_tensor(goh, lg[:, :, 0:EG], over(gmx, EG), ALU.is_equal))
            L(dve.tensor_tensor(goh, goh, revg.unsqueeze(1).broadcast_to([P, LCH, EG]), ALU.mult))
            L(dve.tensor_reduce(gsm, goh, AX.X, ALU.max))
            L(dve.tensor_tensor(goh, goh, over(gsm, EG), ALU.is_equal))
            dve.tensor_tensor(gex, lg[:, :, 0:EG], over(gmx, EG), ALU.subtract).then_inc(s_rv, 1)
            dve.wait_ge(s_ra, GROUP_EXPS)
            L(dve.tensor_reduce(gsm, gex, AX.X, ALU.add))
            L(dve.reciprocal(pg, gsm))
            L(dve.tensor_scalar(goh, goh, -1.0, 1e30, ALU.add, ALU.mult))
            for g in range(EG):
                own.mark(dve.tensor_tensor(lg[:, :, 4 + 8 * g:12 + 8 * g], lg[:, :, 4 + 8 * g:12 + 8 * g],
                                           goh[:, :, g:g + 1].broadcast_to([P, LCH, EPG]), ALU.add))
            own.wait()
            for cc in range(LCH):
                own.mark(dve.max(top[:, cc, :], lg[:, cc, 4:36]))
            own.wait()
            for cc in range(LCH):
                own.mark(dve.max_index(topi[:, cc, :], top[:, cc, :], lg[:, cc, 4:36]))
            own.wait()
            dve.tensor_tensor(ef[:, 1, :], top[:, :, 1], top[:, :, 0], ALU.subtract).then_inc(s_rv, 1)
            dve.wait_ge(s_ra, EXPERT_EXPS)
            L(dve.tensor_scalar(wsel[:, 0, :], ef[:, 1, :], 1.0, None, ALU.add))
            L(dve.reciprocal(wsel[:, 0, :], wsel[:, 0, :]))
            L(dve.tensor_tensor(wsel[:, 0, :], wsel[:, 0, :], pg, ALU.mult))
            L(dve.tensor_tensor(wsel[:, 1, :], wsel[:, 0, :], ef[:, 1, :], ALU.mult))
            for k in range(2):
                own.mark(dve.tensor_copy(ef[:, k, :], topi[:, :, k]))
            own.wait()
            own.mark(dve.tensor_tensor(strict, upper[:, :], ident[:, :], ALU.subtract))
            dve.tensor_tensor(oh, iof[:, 0:E].unsqueeze(1).broadcast_to([P, NT, E]),
                              over(ef.rearrange("p a b -> p (a b)"), E), ALU.is_equal).then_inc(s_rv, 1)
            own.wait()
            dve.wait_ge(s_rp, RANKS)
            own.mark(dve.tensor_copy(rank.rearrange("p a b -> p (a b)"), bank[3][:, 0:NT * E]))
            own.mark(dve.tensor_copy(tsum.rearrange("p a b -> p (a b)"), bank[4][:, 0:NT * E]))
            own.wait()
            L(dve.tensor_copy(cnt, tsum[:, 0, :]))
            for j in range(1, NT):
                L(dve.tensor_tensor(rank[:, j, :], rank[:, j, :], cnt, ALU.add))
                L(dve.tensor_tensor(cnt, cnt, tsum[:, j, :], ALU.add))
            L(dve.tensor_scalar(nblk, cnt, 0.0, None, ALU.is_gt))
            for m in range(1, LAT // P):
                L(dve.scalar_tensor_tensor(nblk, cnt, float(m * P), nblk, ALU.is_gt, ALU.add))
            L(dve.tensor_tensor_scan(binc, ones[:, 0:E], nblk, 0.0, ALU.mult, ALU.add))
            L(dve.tensor_tensor(cmpb, over(iof[:, 0:NB], E), binc.unsqueeze(1).broadcast_to([P, NB, E]), ALU.is_ge))
            L(dve.tensor_reduce(bef, cmpb, AX.X, ALU.add))
            L(dve.tensor_scalar(bef, bef, float(E - 1), None, ALU.min))
            L(dve.tensor_copy(bexp, bef))
            L(dve.tensor_scalar(bef, iof[:, 0:NB], binc[:, E - 1:E], None, ALU.is_lt))
            L(dve.tensor_reduce(c1[:, 0:1], bef.rearrange("p (a b) -> p a b", b=2)[:, :, 0], AX.X, ALU.add))
            dve.tensor_copy(npair, c1[:, 0:1]).then_inc(s_rv, 1)
            L(dve.tensor_tensor(bst, binc, nblk, ALU.subtract))
            L(dve.tensor_tensor(tE, oh, rank, ALU.mult))
            L(dve.tensor_reduce(rk, tE, AX.X, ALU.add))
            L(dve.tensor_tensor(tE, oh, bst.unsqueeze(1).broadcast_to([P, NT, E]), ALU.mult))
            L(dve.tensor_reduce(blk, tE, AX.X, ALU.add))
            L(dve.tensor_scalar(fl, rk, float(P), None, ALU.is_ge))
            for m in range(2, LAT // P):
                L(dve.scalar_tensor_tensor(fl, rk, float(m * P), fl, ALU.is_ge, ALU.add))
            L(dve.tensor_tensor(blk, blk, fl, ALU.add))
            L(dve.scalar_tensor_tensor(rk, fl, -float(P), rk, ALU.mult, ALU.add))
            L(dve.tensor_tensor(soh, iof.unsqueeze(1).broadcast_to([P, NT, P]), over(rk, P), ALU.is_equal))
            L(dve.tensor_tensor(boh, iof[:, 0:NB].unsqueeze(1).broadcast_to([P, NT, NB]), over(blk, NB), ALU.is_equal))
            dve.tensor_tensor(boh, boh, over(pidf, NB), ALU.mult).then_inc(s_rv, 1)
            dve.wait_ge(s_rp, SLOT_TABLE)
            L(dve.tensor_copy(tbl, bank[5][:, 0:NB]))
            L(dve.tensor_scalar(inv, tbl, 0.0, None, ALU.is_equal))
            L(dve.tensor_scalar(hi_, tbl, float(LAT), -float(LAT), ALU.is_gt, ALU.mult))
            L(dve.tensor_scalar(inv, inv, 4096.0, -1.0, ALU.mult, ALU.add))
            L(dve.tensor_tensor(tbl, tbl, inv, ALU.add))
            L(dve.tensor_copy(sidx, tbl))
            L(dve.tensor_tensor(tbl, tbl, hi_, ALU.add))
            dve.tensor_copy(gidx, tbl).then_inc(s_rv, 1)

        we = [arena[:, 12288 * (1 - r):12288 * (2 - r)] for r in range(2)]
        wgt = [w[:, 0:4096].rearrange("p (k f) -> p k f", f=FF) for w in we]
        wut = [w[:, 4096:8192].rearrange("p (k f) -> p k f", f=FF) for w in we]
        wdt_ = [w[:, 8192:12288].rearrange("p (k n) -> p k n", n=D) for w in we]

        def experts_sync(sp):
            sp.wait_ge(s_rv, EXPERTS)
            sp.wait_ge(s_h2st, 16 * LCH)
            n = sp.value_load(npair[0:1, 0:1], min_val=NT // 2, max_val=BLOCKS // 2)

            def load(t, warm):
                for r in range(2):
                    i = t * 2 + r
                    e = sp.value_load(bexp[0:1, bass.ds(i, 1)], min_val=0, max_val=E - 1)
                    if warm:
                        sp.wait_ge(s_u, START + i - 1)
                    elif r:
                        sp.wait_ge(s_rv, TABLES)
                    sp.dma_start(wgt[r], w_gate[0, bass.ds(e, 1)].rearrange("u (k p) f -> p (u k) f", p=P)).then_inc(s_wg[r], 16)
                    sp.dma_start(wut[r], w_up[0, bass.ds(e, 1)].rearrange("u (k p) f -> p (u k) f", p=P)).then_inc(s_wg[r], 16)
                    if warm:
                        sp.wait_ge(s_d, START + i - 1)
                    elif r == 0:
                        sp.wait_ge(s_xg[0], 16)
                    sp.dma_start(wdt_[r], w_down[0, bass.ds(e, 1)].rearrange("u (k p) n -> p (u k) n", p=P)).then_inc(s_wd[r], 16)

            load(0, False)
            with sp.Fori(1, n) as t:
                load(t, True)
            sp.wait_ge(s_sc[0], n * 16)
            sp.wait_ge(s_sc[1], n * 16)
            yl = arena[:, 0:8192].rearrange("p (j d) -> p j d", d=D)
            for half in range(2):
                js = slice(half * LCH // 2, (half + 1) * LCH // 2)
                for k in range(2):
                    sp.dma_start(yl[:, k * LCH:(k + 1) * LCH, :][:, js, :],
                                 y_dram[k * LAT:(k + 1) * LAT, :].rearrange("(j p) d -> p j d", p=P)[:, js, :]).then_inc(s_yl[half], 16)
            for cc in range(LCH):
                sp.wait_ge(s_fo, cc + 1)
                sp.dma_start(out[0, cc * P:(cc + 1) * P, :], yl[:, cc, :]).then_inc(s_done, 16)
            sp.wait_ge(s_done, 16 * LCH)

        def experts_gpsimd(pool, own):
            pool.wait_ge(s_rv, TABLES)
            pool.wait_ge(s_h2st, 16 * LCH)
            pool.memset(xg[0], 0.0).then_inc(s_z, 1)
            own.link(pool.memset(pad, 0.0))
            pool.memset(xg[1], 0.0).then_inc(s_z, 1)
            pool.wait_ge(s_z, 2)
            n = pool.value_load(npair[0:1, 0:1], min_val=NT // 2, max_val=BLOCKS // 2)

            def gather(i, r, copied):
                pool.tensor_copy(idg[r], gidx[:, bass.ds(i, 1)]).then_inc(s_idx, 1)
                pool.wait_ge(s_idx, copied)
                pool.tensor_tensor(pad[:, 0:1], pad[:, 0:1], pad[:, 0:1], ALU.mult)
                pool.indirect_dma_start(out=xg[r], out_offset=None, in_=h2_dram,
                                        in_offset=bass.IndirectOffsetOnAxis(ap=idg[r], axis=0),
                                        bounds_check=LAT - 1, oob_is_err=False).then_inc(s_xg[r], 16)

            gather(0, 0, 1)
            gather(1, 1, 2)

            def scatter(i, r, copied):
                pool.wait_ge(s_yb, START + i + 1)
                pool.tensor_tensor(pad[:, 1:2], pad[:, 1:2], pad[:, 1:2], ALU.mult)
                pool.tensor_copy(ids[r], sidx[:, bass.ds(i, 1)]).then_inc(s_idx, 1)
                pool.wait_ge(s_idx, copied)
                pool.tensor_tensor(pad[:, 0:1], pad[:, 0:1], pad[:, 0:1], ALU.mult)
                pool.indirect_dma_start(out=y_dram, out_offset=bass.IndirectOffsetOnAxis(ap=ids[r], axis=0),
                                        in_=yb[r], in_offset=None,
                                        bounds_check=2 * LAT - 1, oob_is_err=False).then_inc(s_sc[r], 16)

            def pair(t, warm):
                for r in range(2):
                    i = t * 2 + r
                    pool.wait_ge(s_xgt, START + i + 1)
                    if warm or r:
                        gather(i + 2, r, i * 2 + 2)
                        scatter(i - 1, 1 - r, i * 2 + 3)
                    else:
                        gather(2, 0, 3)

            pair(0, False)
            with pool.Fori(1, n) as t:
                pair(t, True)
            scatter(n * 2 - 1, 1, n * 4 + 2)
            pool.wait_ge(s_xg[0], n * 16 + 16)
            pool.wait_ge(s_xg[1], n * 16 + 16)

        def experts_scalar(act, own):
            act.wait_ge(s_rv, TABLES)
            n = act.value_load(npair[0:1, 0:1], min_val=NT // 2, max_val=BLOCKS // 2)

            def columns(i, r):
                act.wait_ge(s_xgt, START + i + 1)
                act.copy(xgT[r][:, 0:4, :].rearrange("p a b -> p (a b)"), bank[0][:, :])
                act.copy(xgT[r][:, 4:8, :].rearrange("p a b -> p (a b)"), bank[1][:, :]).then_inc(s_xgc, 1)

            def gated_columns(i, first=False):
                act.wait_ge(s_gut, START + i + 1)
                if not first:
                    act.wait_ge(s_d, START + i)
                act.copy(guT.rearrange("p a b -> p (a b)"), bank[4][:, :]).then_inc(s_guc, 1)

            def pair(t, warm):
                for r in range(2):
                    i = t * 2 + r
                    act.wait_ge(s_g, i + 1)
                    if warm:
                        act.wait_ge(s_gut, START + i - 1)
                    act.activation(gu[r], bank[2][:, :], ACT.Silu).then_inc(s_sig, 1)
                    if warm or r:
                        gated_columns(i - 1)
                        act.wait_ge(s_u, START + i)
                    columns(i + 1, 1 - r)

            columns(0, 0)
            pair(0, False)
            with act.Fori(1, n) as t:
                pair(t, True)
            gated_columns(n * 2 - 1)
            for cc in range(LCH):
                act.wait_ge(s_fa, cc + 1)
                own.link(act.activation(tmpf[cc % 2], ylc[:, cc, :], ACT.Square, accum_out=ssq[:, 4 + cc:5 + cc]))
                own.link(act.activation(rst[:, 4 + cc:5 + cc], ssq[:, 4 + cc:5 + cc], ACT.Ln, scale=1.0 / D, bias=epsb[:, 0:1]))
                act.activation(rst[:, 4 + cc:5 + cc], rst[:, 4 + cc:5 + cc], ACT.Exp, scale=-0.5).then_inc(s_fs, 1)

        def experts_tensor(pe):
            pe.wait_ge(s_rv, TABLES)
            n = pe.value_load(npair[0:1, 0:1], min_val=NT // 2, max_val=BLOCKS // 2)

            def rows(i, r, cnt):
                pe.wait_ge(s_xg[r], cnt)
                pe.wait_ge(s_xgc, START + i)
                for k in range(KT):
                    mm = pe.transpose(bank[k // 4][:, (k % 4) * P:(k % 4 + 1) * P], xg[r][:, k * P:(k + 1) * P], ident[:, :])
                mm.then_inc(s_xgt, 1)

            def down(i, r, loaded):
                pe.wait_ge(s_guc, i + 1)
                pe.wait_ge(s_wd[r], loaded)
                pe.wait_ge(s_yb, START + i)
                for hf in range(2):
                    for f in range(FT):
                        mm = pe.matmul(bank[5 + hf][:, :], guT[:, f, :], wdt_[r][:, f, hf * 512:(hf + 1) * 512],
                                       start=(f == 0), stop=(f == FT - 1))
                mm.then_inc(s_d, 1)

            def turn_gated(i, r):
                pe.wait_ge(s_gu, START + i + 1)
                for f in range(FT):
                    mm = pe.transpose(bank[4][:, f * P:(f + 1) * P], gu[r][:, f * P:(f + 1) * P], ident[:, :])
                mm.then_inc(s_gut, 1)

            def pair(t, warm):
                for r in range(2):
                    i = t * 2 + r
                    pe.wait_ge(s_xgc, START + i + 1)
                    pe.wait_ge(s_wg[r], t * 32 + 32)
                    pe.wait_ge(s_sig, START + i)
                    for k in range(KT):
                        mm = pe.matmul(bank[2][:, :], xgT[r][:, k, :], wgt[r][:, k, :], start=(k == 0), stop=(k == KT - 1))
                    mm.then_inc(s_g, 1)
                    if warm or r:
                        turn_gated(i - 1, 1 - r)
                    rows(i + 1, 1 - r, t * 16 + 16 + 16 * r)
                    pe.wait_ge(s_gu, START + i)
                    for k in range(KT):
                        mm = pe.matmul(bank[3][:, :], xgT[r][:, k, :], wut[r][:, k, :], start=(k == 0), stop=(k == KT - 1))
                    mm.then_inc(s_u, 1)
                    if warm or r:
                        down(i - 1, 1 - r, t * 16 + 16 * r)

            rows(0, 0, 16)
            pair(0, False)
            with pe.Fori(1, n) as t:
                pair(t, True)
            turn_gated(n * 2 - 1, 1)
            down(n * 2 - 1, 1, n * 16)

        ylc = arena[:, 0:4096].rearrange("p (j d) -> p j d", d=D)
        yl1 = arena[:, 4096:8192].rearrange("p (j d) -> p j d", d=D)
        tmpf = [arena[:, 8192 + D * i:8192 + D * (i + 1)] for i in range(2)]

        def experts_vector(dve, own):
            dve.wait_ge(s_rv, TABLES)
            n = dve.value_load(npair[0:1, 0:1], min_val=NT // 2, max_val=BLOCKS // 2)

            def rows(i, r, stored=None):
                dve.wait_ge(s_d, START + i + 1)
                if stored is not None:
                    dve.wait_ge(s_sc[0], stored)
                    dve.wait_ge(s_sc[1], stored)
                dve.tensor_copy(yb[r][:, 0:512], bank[5][:, :])
                dve.tensor_copy(yb[r][:, 512:1024], bank[6][:, :]).then_inc(s_yb, 1)

            def gated(i, r):
                dve.wait_ge(s_sig, START + i + 1)
                dve.wait_ge(s_u, START + i + 1)
                dve.tensor_tensor(gu[r], gu[r], bank[3][:, :], ALU.mult).then_inc(s_gu, 1)

            def pair(t, warm):
                gated(t * 2, 0)
                if warm:
                    rows(t * 2 - 1, 1)
                gated(t * 2 + 1, 1)
                rows(t * 2, 0, t * 16 if warm else None)

            pair(0, False)
            with dve.Fori(1, n) as t:
                pair(t, True)
            rows(n * 2 - 1, 1)
            for cc in range(LCH):
                dve.wait_ge(s_yl[cc // 2], 32)
                own.link(dve.tensor_scalar(ylc[:, cc, :], ylc[:, cc, :], wsel[:, 0, cc:cc + 1], None, ALU.mult))
                dve.scalar_tensor_tensor(ylc[:, cc, :], yl1[:, cc, :], wsel[:, 1, cc:cc + 1], ylc[:, cc, :],
                                         ALU.mult, ALU.add).then_inc(s_fa, 1)
            for cc in range(LCH):
                dve.wait_ge(s_fs, cc + 1)
                own.wait()
                dve.scalar_tensor_tensor(ylc[:, cc, :], ylc[:, cc, :], rst[:, 4 + cc:5 + cc], row_keep,
                                         ALU.mult, ALU.mult).then_inc(own.sem, 1)
                own.n += 1
                own.wait()
                dve.tensor_tensor(ylc[:, cc, :], ylc[:, cc, :], xl[:, cc, :], ALU.add).then_inc(s_fo, 1)

        block = es.enter_context(nc.Block())

        @block.sync
        def _(sp):
            modulate_sync(sp)
            ssd_sync(sp)
            hg_sync(sp)
            merge_sync(sp)
            experts_sync(sp)

        @block.gpsimd
        def _(pool):
            for s in (s_ld,):
                pool.sem_inc(s, START)
            own = Own(pool, s_pool)
            modulate_gpsimd(pool, own)
            ssd_gpsimd(pool)
            hg_gpsimd(pool, own)
            route_gpsimd(pool, own)
            experts_gpsimd(pool, own)

        @block.scalar
        def _(act):
            for s in (s_ys, s_pev, s_ln, s_qee, s_et, s_sig, s_xgc):
                act.sem_inc(s, START)
            own = Own(act, s_act)
            modulate_scalar(act, own)
            ssd_scalar(act, own)
            hg_scalar(act)
            merge_scalar(act, own)
            route_scalar(act)
            experts_scalar(act, own)

        @block.tensor
        def _(pe):
            for s in (s_xp, s_zp, s_kv, s_yd, s_yo, s_yt, s_kdT, s_la, s_kvH, s_out, s_xgt, s_u, s_d,
                      s_gut):
                pe.sem_inc(s, START)
            modulate_tensor(pe)
            ssd_tensor(pe)
            hg_tensor(pe)
            merge_tensor(pe)
            route_tensor(pe)
            experts_tensor(pe)

        @block.vector
        def _(dve):
            for s in (s_yz, s_you, s_b, s_chain, s_lp, s_lw, s_ohd, s_ohn, s_gu, s_yb):
                dve.sem_inc(s, START)
            own = Own(dve, s_dve)
            modulate_vector(dve, own)
            ssd_vector(dve, own)
            hg_vector(dve, own)
            merge_vector(dve, own)
            route_vector(dve, own)
            experts_vector(dve, own)


_INS = ['x', 'c', 'ctx', 'c_ctx', 'w_ada', 'b_ada', 'g_pre_mix', 'g_post_mix', 'g_pre_ffn', 'g_post_ffn', 'w_in',
        'conv_w', 'conv_b', 'dt_bias', 'a_log', 'd_skip', 'g_ssm_norm', 'hg_lb', 'g_hg_norm', 'w_branch_ssm',
        'w_branch_hg', 'w_out', 'w_group_router', 'b_group_router', 'w_expert_router', 'b_expert_router',
        'w_gate', 'w_up', 'w_down']
_OUTS = [((1, LAT, D), 'float32')]


def kernel(**inputs):
    import numpy as _np
    import concourse.bacc as _bacc
    from concourse import mybir as _mybir
    from concourse.bass_utils import run_bass_kernel_spmd as _run

    nc = _bacc.Bacc("TRN2", target_bir_lowering=False, num_devices=1)
    arrays, args = {}, []
    for name in _INS:
        a = _np.ascontiguousarray(inputs[name])
        arrays[f"in_{name}_dram"] = a
        args.append(nc.dram_tensor(f"in_{name}_dram", a.shape, _mybir.dt.from_np(a.dtype), kind="ExternalInput").ap())
    for i, (shape, dtype) in enumerate(_OUTS):
        dt = _mybir.dt.from_np(_np.dtype(dtype))
        args.append(nc.dram_tensor(f"out_{i}_dram", shape, dt, kind="ExternalOutput").ap())
    build(nc, *args)
    r = _run(nc, [arrays], core_ids=[0])
    got = tuple(r.results[0][f"out_{i}_dram"] for i in range(len(_OUTS)))
    return got[0]
```
